# Optimizing a Trainium2 kernel written in Bass

```python
import math
import jax
import jax.numpy as jnp
from jax import lax
import numpy as np

D_MODEL = 1024
BATCH = 1
SEQ = 1024
DEPTH = 2

N_MIXERS = 3
D_FF = 4 * D_MODEL
NORM_EPS = 1e-6
ROPE_THETA = 10000.0
OUT_SCALE = 0.5

RET_HEADS = 4
RET_DK = D_MODEL // RET_HEADS
RET_DV = 2 * RET_DK
RET_QK = RET_HEADS * RET_DK
RET_V = RET_HEADS * RET_DV
RET_CHUNK = 128

SWA_HEADS = 16
SWA_KV_HEADS = 4
SWA_HEAD_DIM = D_MODEL // SWA_HEADS
SWA_GROUP = SWA_HEADS // SWA_KV_HEADS
SWA_WINDOW = 128

GDN_QK_HEADS = 8
GDN_V_HEADS = 16
GDN_HEAD_DIM = 128
GDN_QK = GDN_QK_HEADS * GDN_HEAD_DIM
GDN_V = GDN_V_HEADS * GDN_HEAD_DIM
GDN_CONV_DIM = 2 * GDN_QK + GDN_V
GDN_CONV = 4
GDN_CHUNK = 64

N_RET = (DEPTH + N_MIXERS - 1) // N_MIXERS
N_SWA = (DEPTH + N_MIXERS - 2) // N_MIXERS
N_GDN = (DEPTH + N_MIXERS - 3) // N_MIXERS

kernel_name = "hybrid_retention_swa_gdn_trunk"

def rmsnorm(x, gain):
    xf = x.astype(jnp.float32)
    y = xf * lax.rsqrt(jnp.mean(xf * xf, axis=-1, keepdims=True) + NORM_EPS)
    return (y * gain.astype(jnp.float32)).astype(x.dtype)

def l2norm(x):
    xf = x.astype(jnp.float32)
    return xf * lax.rsqrt(jnp.sum(xf * xf, axis=-1, keepdims=True) + NORM_EPS)

def rope(x, positions):
    d = x.shape[-1]
    inv_freq = ROPE_THETA ** (-jnp.arange(0, d, 2, dtype=jnp.float32) / d)
    ang = positions.astype(jnp.float32)[:, :, None, None] * inv_freq
    cos, sin = jnp.cos(ang), jnp.sin(ang)
    xf = x.astype(jnp.float32)
    x1, x2 = xf[..., : d // 2], xf[..., d // 2:]
    return jnp.concatenate([x1 * cos - x2 * sin, x2 * cos + x1 * sin], axis=-1).astype(x.dtype)

def retention(h, positions, w_in, w_out):
    b, s, _ = h.shape
    c = RET_CHUNK
    n = s // c
    nh = RET_HEADS
    q, k, v, g = jnp.split(h @ w_in, [RET_QK, 2 * RET_QK, 2 * RET_QK + RET_V], axis=-1)
    q = rope(q.reshape(b, s, nh, RET_DK), positions)
    k = rope(k.reshape(b, s, nh, RET_DK), positions)

    def chunks(t):
        return t.astype(jnp.float32).reshape(b, n, c, nh, -1).transpose(0, 3, 1, 2, 4)

    qc = chunks(q)
    kc = chunks(k) * (RET_DK ** -0.5)
    vc = chunks(v.reshape(b, s, nh, RET_DV))
    log_gamma = jnp.log1p(-(2.0 ** (-5.0 - jnp.arange(nh, dtype=jnp.float32))))
    idx = jnp.arange(c, dtype=jnp.float32)
    diff = idx[:, None] - idx[None, :]
    causal = diff >= 0
    dmat = jnp.where(causal, jnp.exp(log_gamma[:, None, None] * jnp.where(causal, diff, 0.0)), 0.0)
    scores = jnp.einsum("bhncd,bhnsd->bhncs", qc, kc) * dmat[None, :, None]
    o_intra = jnp.einsum("bhncs,bhnse->bhnce", scores, vc)
    q_decay = jnp.exp(log_gamma[:, None] * (idx + 1.0))[None, :, :, None]
    k_decay = jnp.exp(log_gamma[:, None] * (c - 1.0 - idx))[None, :, :, None]
    chunk_decay = jnp.exp(log_gamma * c)[None, :, None, None]

    def step(state, inp):
        q_n, k_n, v_n = inp
        o = jnp.einsum("bhcd,bhde->bhce", q_n * q_decay, state)
        state = state * chunk_decay + jnp.einsum("bhcd,bhce->bhde", k_n * k_decay, v_n)
        return state, o

    state0 = jnp.zeros((b, nh, RET_DK, RET_DV), jnp.float32)
    lead = lambda t: jnp.moveaxis(t, 2, 0)
    _, o_cross = lax.scan(step, state0, (lead(qc), lead(kc), lead(vc)))
    o = o_intra + jnp.moveaxis(o_cross, 0, 2)
    o = o.transpose(0, 2, 3, 1, 4).reshape(b, s, nh, RET_DV)
    mu = jnp.mean(o, axis=-1, keepdims=True)
    var = jnp.mean(jnp.square(o - mu), axis=-1, keepdims=True)
    o = (o - mu) * lax.rsqrt(var + NORM_EPS)
    y = o.reshape(b, s, RET_V) * jax.nn.silu(g.astype(jnp.float32))
    return y.astype(h.dtype) @ w_out

def sliding_window_attention(h, positions, w_in, q_gain, k_gain, sinks, w_out):
    b, s, _ = h.shape
    w = SWA_WINDOW
    n = s // w
    dh = SWA_HEAD_DIM
    q, k, v = jnp.split(h @ w_in, [SWA_HEADS * dh, (SWA_HEADS + SWA_KV_HEADS) * dh], axis=-1)
    q = rope(rmsnorm(q.reshape(b, s, SWA_HEADS, dh), q_gain), positions)
    k = rope(rmsnorm(k.reshape(b, s, SWA_KV_HEADS, dh), k_gain), positions)
    qb = q.reshape(b, n, w, SWA_KV_HEADS, SWA_GROUP, dh)

    def with_prev(t):
        tb = t.reshape(b, n, w, SWA_KV_HEADS, dh)
        prev = jnp.pad(tb[:, :-1], ((0, 0), (1, 0), (0, 0), (0, 0), (0, 0)))
        return jnp.concatenate([prev, tb], axis=2)

    kb = with_prev(k)
    vb = with_prev(v.reshape(b, s, SWA_KV_HEADS, dh))
    scores = jnp.einsum("bnqkgd,bnskd->bnkgqs", qb, kb).astype(jnp.float32) * (dh ** -0.5)
    qpos = w + jnp.arange(w)
    kpos = jnp.arange(2 * w)
    rel = qpos[:, None] - kpos[None, :]
    band = (rel >= 0) & (rel < w)
    has_prev = (jnp.arange(n)[:, None, None] > 0) | (kpos[None, None, :] >= w)
    mask = (band[None] & has_prev)[None, :, None, None]
    scores = jnp.where(mask, scores, -jnp.inf)
    sink = jnp.broadcast_to(
        sinks.astype(jnp.float32).reshape(SWA_KV_HEADS, SWA_GROUP)[None, None, :, :, None, None],
        scores.shape[:-1] + (1,))
    probs = jax.nn.softmax(jnp.concatenate([scores, sink], axis=-1), axis=-1)[..., :-1]
    o = jnp.einsum("bnkgqs,bnskd->bnqkgd", probs.astype(vb.dtype), vb)
    return o.reshape(b, s, SWA_HEADS * dh) @ w_out

def causal_depthwise_conv(x, w):
    ch = x.shape[-1]
    return lax.conv_general_dilated(
        x, w[:, None, :].astype(x.dtype), window_strides=(1,), padding=[(GDN_CONV - 1, 0)],
        dimension_numbers=("NWC", "WIO", "NWC"), feature_group_count=ch)

def chunk_gated_delta_rule(q, k, v, g, beta):
    b, s, nh, dk = q.shape
    dv = v.shape[-1]
    c = GDN_CHUNK
    n = s // c

    def chunks(t):
        return t.astype(jnp.float32).reshape(b, n, c, nh, -1).transpose(0, 3, 1, 2, 4)

    q, k, v = chunks(q), chunks(k), chunks(v)
    g = chunks(g[..., None])[..., 0]
    beta = chunks(beta[..., None])[..., 0]
    g = jnp.cumsum(g, axis=-1)
    tril = jnp.tril(jnp.ones((c, c), dtype=bool))
    strict = jnp.tril(jnp.ones((c, c), dtype=bool), -1)
    decay = jnp.exp(jnp.where(tril, g[..., :, None] - g[..., None, :], -jnp.inf))
    k_beta = k * beta[..., None]
    lower = jnp.where(strict, jnp.einsum("bhncd,bhnsd->bhncs", k_beta, k) * decay, 0.0)
    eye = jnp.eye(c, dtype=jnp.float32)
    t_inv = lax.linalg.triangular_solve(lower + eye, jnp.broadcast_to(eye, lower.shape),
                                        left_side=True, lower=True, unit_diagonal=True)
    u = jnp.einsum("bhncs,bhnse->bhnce", t_inv, v * beta[..., None])
    wk = jnp.einsum("bhncs,bhnsd->bhncd", t_inv, k_beta * jnp.exp(g)[..., None])
    attn = jnp.einsum("bhncd,bhnsd->bhncs", q, k) * decay
    q_in = q * jnp.exp(g)[..., None]
    g_last = g[..., -1]
    k_out = k * jnp.exp(g_last[..., None] - g)[..., None]

    def step(state, inp):
        u_n, w_n, q_n, a_n, k_n, gl_n = inp
        v_new = u_n - jnp.einsum("bhcd,bhde->bhce", w_n, state)
        o = jnp.einsum("bhcd,bhde->bhce", q_n, state) + jnp.einsum("bhcs,bhse->bhce", a_n, v_new)
        state = state * jnp.exp(gl_n)[..., None, None] + jnp.einsum("bhcd,bhce->bhde", k_n, v_new)
        return state, o

    lead = lambda t: jnp.moveaxis(t, 2, 0)
    state0 = jnp.zeros((b, nh, dk, dv), jnp.float32)
    _, o = lax.scan(step, state0, (lead(u), lead(wk), lead(q_in), lead(attn), lead(k_out), lead(g_last)))
    return o.transpose(1, 0, 3, 2, 4).reshape(b, s, nh, dv)

def gated_deltanet(h, w_in, conv_w, a_log, dt_bias, out_gain, w_out):
    b, s, _ = h.shape
    dh = GDN_HEAD_DIM
    qkv, z, beta_logit, a = jnp.split(
        h @ w_in, [GDN_CONV_DIM, GDN_CONV_DIM + GDN_V, GDN_CONV_DIM + GDN_V + GDN_V_HEADS], axis=-1)
    qkv = jax.nn.silu(causal_depthwise_conv(qkv, conv_w))
    q, k, v = jnp.split(qkv, [GDN_QK, 2 * GDN_QK], axis=-1)
    rep = GDN_V_HEADS // GDN_QK_HEADS
    q = jnp.repeat(l2norm(q.reshape(b, s, GDN_QK_HEADS, dh)) * (dh ** -0.5), rep, axis=2)
    k = jnp.repeat(l2norm(k.reshape(b, s, GDN_QK_HEADS, dh)), rep, axis=2)
    v = v.reshape(b, s, GDN_V_HEADS, dh)
    beta = jax.nn.sigmoid(beta_logit.astype(jnp.float32))
    g = -jnp.exp(a_log.astype(jnp.float32)) * jax.nn.softplus(a.astype(jnp.float32) + dt_bias.astype(jnp.float32))
    o = chunk_gated_delta_rule(q, k, v, g, beta)
    o = rmsnorm(o, out_gain) * jax.nn.silu(z.reshape(b, s, GDN_V_HEADS, dh).astype(jnp.float32))
    return o.reshape(b, s, GDN_V).astype(h.dtype) @ w_out

def squared_relu_mlp(h, w_up, w_down):
    return jnp.square(jax.nn.relu(h @ w_up)) @ w_down

def setup_inputs(seed: int = 0) -> dict:
    key = jax.random.key(seed)
    ks = jax.random.split(key, 20)

    def normal(k, shape, scale):
        return jax.random.normal(k, shape, jnp.float32) * scale

    def gain(k, shape):
        return 1.0 + 0.1 * jax.random.normal(k, shape, jnp.float32)

    x = normal(ks[0], (BATCH, SEQ, D_MODEL), 1.0)
    offsets = jax.random.randint(ks[1], (BATCH, 1), 0, SEQ, dtype=jnp.int32)
    positions = (offsets + jnp.arange(SEQ, dtype=jnp.int32)[None, :]).astype(jnp.int32)
    norm_mix = gain(ks[2], (DEPTH, D_MODEL))
    norm_mlp = gain(ks[3], (DEPTH, D_MODEL))
    w_up = normal(ks[4], (DEPTH, D_MODEL, D_FF), D_MODEL ** -0.5)
    w_down = normal(ks[5], (DEPTH, D_FF, D_MODEL), OUT_SCALE * D_FF ** -0.5)
    ret_w_in = normal(ks[6], (N_RET, D_MODEL, 2 * RET_QK + 2 * RET_V), D_MODEL ** -0.5)
    ret_w_out = normal(ks[7], (N_RET, RET_V, D_MODEL), OUT_SCALE * RET_V ** -0.5)
    swa_w_in = normal(ks[8], (N_SWA, D_MODEL, (SWA_HEADS + 2 * SWA_KV_HEADS) * SWA_HEAD_DIM), D_MODEL ** -0.5)
    swa_q_gain = gain(ks[9], (N_SWA, SWA_HEAD_DIM))
    swa_k_gain = gain(ks[10], (N_SWA, SWA_HEAD_DIM))
    swa_sinks = normal(ks[11], (N_SWA, SWA_HEADS), 0.5)
    swa_w_out = normal(ks[12], (N_SWA, SWA_HEADS * SWA_HEAD_DIM, D_MODEL), OUT_SCALE * (SWA_HEADS * SWA_HEAD_DIM) ** -0.5)
    gdn_w_in = normal(ks[13], (N_GDN, D_MODEL, GDN_CONV_DIM + GDN_V + 2 * GDN_V_HEADS), D_MODEL ** -0.5)
    gdn_conv_w = normal(ks[14], (N_GDN, GDN_CONV, GDN_CONV_DIM), GDN_CONV ** -0.5)
    gdn_a_log = jnp.log(jax.random.uniform(ks[15], (N_GDN, GDN_V_HEADS), jnp.float32, minval=1.0, maxval=16.0))
    dt = jnp.exp(jax.random.uniform(ks[16], (N_GDN, GDN_V_HEADS), jnp.float32,
                                    minval=math.log(1e-3), maxval=math.log(1e-1)))
    gdn_dt_bias = dt + jnp.log(-jnp.expm1(-dt))
    gdn_out_gain = gain(ks[17], (N_GDN, GDN_HEAD_DIM))
    gdn_w_out = normal(ks[18], (N_GDN, GDN_V, D_MODEL), OUT_SCALE * GDN_V ** -0.5)
    return {
        "x": x, "positions": positions,
        "norm_mix": norm_mix, "norm_mlp": norm_mlp, "w_up": w_up, "w_down": w_down,
        "ret_w_in": ret_w_in, "ret_w_out": ret_w_out,
        "swa_w_in": swa_w_in, "swa_q_gain": swa_q_gain, "swa_k_gain": swa_k_gain,
        "swa_sinks": swa_sinks, "swa_w_out": swa_w_out,
        "gdn_w_in": gdn_w_in, "gdn_conv_w": gdn_conv_w, "gdn_a_log": gdn_a_log,
        "gdn_dt_bias": gdn_dt_bias, "gdn_out_gain": gdn_out_gain, "gdn_w_out": gdn_w_out,
    }

def reference(x, positions, norm_mix, norm_mlp, w_up, w_down, ret_w_in, ret_w_out,
              swa_w_in, swa_q_gain, swa_k_gain, swa_sinks, swa_w_out,
              gdn_w_in, gdn_conv_w, gdn_a_log, gdn_dt_bias, gdn_out_gain, gdn_w_out):
    for i in range(DEPTH):
        m, j = i % N_MIXERS, i // N_MIXERS
        h = rmsnorm(x, norm_mix[i])
        if m == 0:
            y = retention(h, positions, ret_w_in[j], ret_w_out[j])
        elif m == 1:
            y = sliding_window_attention(h, positions, swa_w_in[j], swa_q_gain[j], swa_k_gain[j],
                                         swa_sinks[j], swa_w_out[j])
        else:
            y = gated_deltanet(h, gdn_w_in[j], gdn_conv_w[j], gdn_a_log[j], gdn_dt_bias[j],
                               gdn_out_gain[j], gdn_w_out[j])
        x = x + y.astype(x.dtype)
        h = rmsnorm(x, norm_mlp[i])
        x = x + squared_relu_mlp(h, w_up[i], w_down[i]).astype(x.dtype)
    return x


_drawn_inputs = setup_inputs


def setup_inputs(seed=0):
    import zlib

    import numpy as np

    out = dict(_drawn_inputs(seed))
    spreads = {}
    factors = {'swa_q_gain': 8.0, 'swa_k_gain': 8.0, 'swa_sinks': 200.0}
    for name, (base, spread) in spreads.items():
        noise = np.random.default_rng([zlib.crc32(name.encode()), seed]).standard_normal(out[name].shape)
        drawn = base * np.exp(spread * noise) if base else spread * noise
        out[name] = jnp.asarray(drawn.astype(out[name].dtype))
    for name, factor in factors.items():
        out[name] = (out[name] * factor).astype(out[name].dtype)
    return out
```

```python
import math
from contextlib import ExitStack

import concourse.bass as bass
from concourse import mybir

F32 = mybir.dt.float32
F32R = mybir.dt.float32r
I32 = mybir.dt.int32
ALU = mybir.AluOpType
ACT = mybir.ActivationFunctionType
AX = mybir.AxisListType

P = 128
D = 1024
S = 1024
KT = D // P
TT = S // P
HALF = 512
EPS = 1e-6
D_FF = 4 * D
PIECE = 1024
RING = 4

HEADS = 4
DK = D // HEADS
DV = 2 * DK
CH = P
NCH = S // CH

SW_HEADS = 16
SW_KV = 4
SW_DH = 64
SW_GQ = (SW_HEADS // SW_KV) * SW_DH
SW_COLS = SW_GQ + 2 * SW_DH
SW_NH = SW_GQ // SW_DH + 1
THETA = 10000.0

RET_GROUPS = HEADS * DV // 256
MLP_GROUPS = D_FF // 256
RET_PIECES = 12
SW_PIECES = 8
PC_OUT = RET_PIECES * HEADS
PC_M0 = PC_OUT + 4 * RET_GROUPS
PC_SW = PC_M0 + 4 * MLP_GROUPS
PC_M1 = PC_SW + SW_PIECES * SW_KV
DG_M0 = RET_GROUPS
DG_SW = DG_M0 + MLP_GROUPS
DG_M1 = DG_SW + SW_KV
RSQ = 11

TWO_PI = 2.0 * math.pi
C1 = 6.28125
C2 = 1.93500518798828125e-3
C3 = TWO_PI - C1 - C2
PI_IN = 3.1415925
NEG = -1e30
ROUND = 12582912.0


def wait(eng, sem, value):
    if isinstance(value, int) and value <= 0:
        return
    eng.wait_ge(sem, value)


def trunk(nc, x_in, positions, norm_mix, norm_mlp, w_up, w_down, ret_in, ret_out, sw_in, q_gain,
          k_gain, sinks, sw_out, c_ident, c_causal, c_mask, c_head, c_freq, c_freq_row, out, y_dram):
    ctx = ExitStack()
    with ctx:
        def sb(name, shape, dt=F32, stack=ctx):
            return stack.enter_context(nc.sbuf_tensor(name, shape, dt))

        def sem(name):
            return ctx.enter_context(nc.semaphore(name))

        ident = sb("ident", [P, P])
        causal = sb("causal", [P, P])
        headc = sb("headc", [P, HEADS, 4])
        hc = sb("hc", [P, 4])
        freq = sb("freq", [P, 1])
        gain_b = sb("gain_b", [P, D])
        raw = sb("raw", [P, RING, PIECE])
        xn = sb("xn", [P, 2, D])
        ss = sb("ss", [P, TT])
        var = sb("var", [P, TT])
        rstd = sb("rstd", [P, TT])
        rtmp = sb("rtmp", [P, TT])
        hT_hi = sb("hT_hi", [P, KT, S], F32R)
        hT_lo = sb("hT_lo", [P, KT, S], F32R)

        with ExitStack() as place:
            x = sb("x", [P, TT, D], F32, place)
        with ExitStack() as ret:
            wv_hi = sb("wv_hi", [P, 4, PIECE], F32R, ret)
            wv_lo = sb("wv_lo", [P, 4, PIECE], F32R, ret)
            wqg_hi = sb("wqg_hi", [P, 4, PIECE], F32R, ret)
            wqg_lo = sb("wqg_lo", [P, 4, PIECE], F32R, ret)
            kq = sb("kq", [P, 4, S], F32, ret)
            cosr = sb("cosr", [P, S], F32, ret)
            sinr = sb("sinr", [P, S], F32, ret)
            rope_t = sb("rope_t", [P, HALF], F32, ret)
            q_hi = sb("q_hi", [P, 2, CH], F32R, ret)
            q_lo = sb("q_lo", [P, 2, CH], F32R, ret)
            k_hi = sb("k_hi", [P, DK], F32R, ret)
            k_lo = sb("k_lo", [P, DK], F32R, ret)
            v_hi = sb("v_hi", [P, DV], F32R, ret)
            v_lo = sb("v_lo", [P, DV], F32R, ret)
            sc = sb("sc", [P, CH], F32, ret)
            sc_hi = sb("sc_hi", [P, CH], F32R, ret)
            sc_lo = sb("sc_lo", [P, CH], F32R, ret)
            state = sb("state", [P, 2, DV], F32, ret)
            st_hi = sb("st_hi", [P, 2, DV], F32R, ret)
            st_lo = sb("st_lo", [P, 2, DV], F32R, ret)
            sgate = sb("sgate", [P, DV], F32, ret)
            bn = sb("bn", [P, 6], F32, ret)
            mv = sb("mv", [P, 2], F32, ret)
            gvar = sb("gvar", [P, 1], F32, ret)
            grs = sb("grs", [P, 1], F32, ret)
            gtmp = sb("gtmp", [P, 1], F32, ret)
            gscale = sb("gscale", [P, 1], F32, ret)
            gbias = sb("gbias", [P, 1], F32, ret)
        yn, y, yT, rope_u = xn[:, 0, 0:DV], xn[:, 0, DV:D], xn[:, 1, 0:DV], xn[:, 1, DV:D]
        posf = kq[:, 0, :]
        turns = kq[:, 1, :]
        pos_i = kq[:, 2, :].bitcast(I32)
        ang = kq[:, 3, :]

        with ExitStack() as later:
            sb("x_place", [P, TT, D], F32, later)
            aT_hi = [sb("aT_hi0", [P, 2, S], F32R, later)]
            aT_lo = [sb("aT_lo0", [P, 2, S], F32R, later)]
            wd_hi = [sb("wd_hi0", [P, 2, D], F32R, later)]
            wd_lo = [sb("wd_lo0", [P, 2, D], F32R, later)]
            with ExitStack() as o:
                aT_hi.append(sb("aT_hi1", [P, 2, S], F32R, o))
                aT_lo.append(sb("aT_lo1", [P, 2, S], F32R, o))
                wd_hi.append(sb("wd_hi1", [P, 2, D], F32R, o))
                wd_lo.append(sb("wd_lo1", [P, 2, D], F32R, o))
                wu_hi = sb("wu_hi", [P, KT, 256], F32R, o)
                wu_lo = sb("wu_lo", [P, KT, 256], F32R, o)
            with ExitStack() as m:
                relu_t = sb("relu_t", [P, 2, HALF], F32, m)
                sqr_t = sb("sqr_t", [P, 2, HALF], F32, m)
            with ExitStack() as s:
                ws_hi = sb("ws_hi", [P, KT, SW_COLS], F32R, s)
                ws_lo = sb("ws_lo", [P, KT, SW_COLS], F32R, s)
                kr = sb("kr", [P, 3, SW_DH], F32, s)
                qT_hi = sb("qT_hi", [P, 2, P], F32R, s)
                qT_lo = sb("qT_lo", [P, 2, P], F32R, s)
                kT_hi = sb("kT_hi", [P, 2, 2, P], F32R, s)
                kT_lo = sb("kT_lo", [P, 2, 2, P], F32R, s)
                vp_hi = sb("vp_hi", [P, 4, 3 * SW_DH], F32R, s)
                vp_lo = sb("vp_lo", [P, 4, 3 * SW_DH], F32R, s)
                pT_hi = sb("pT_hi", [P, 2, 4, P], F32R, s)
                pT_lo = sb("pT_lo", [P, 2, 4, P], F32R, s)
                coss = sb("coss", [P, TT, 32], F32, s)
                sins = sb("sins", [P, TT, 32], F32, s)
                qkgain = sb("qkgain", [P, SW_NH, SW_DH], F32, s)
                sink_b = sb("sink_b", [P, SW_HEADS], F32, s)
                swmask = sb("swmask", [P, 4, P], F32, s)
                pos_si = sb("pos_si", [P, TT], I32, s)
                pos_sf = sb("pos_sf", [P, TT], F32, s)
                freq_row = sb("freq_row", [P, 32], F32, s)
                hss = sb("hss", [P, SW_NH], F32, s)
                hvar = sb("hvar", [P, SW_NH], F32, s)
                hrs = sb("hrs", [P, SW_NH], F32, s)
                htmp = sb("htmp", [P, SW_NH], F32, s)
                smax = sb("smax", [P, 4], F32, s)
                nmax = sb("nmax", [P, 4], F32, s)
                sdif = sb("sdif", [P, 4], F32, s)
                ssum = sb("ssum", [P, 4], F32, s)
                esink = sb("esink", [P, 4], F32, s)
                den = sb("den", [P, 4], F32, s)
                rden = sb("rden", [P, 4], F32, s)
        prob = xn[:, 0, :].rearrange("p (h s n) -> p h s n", s=2, n=P)
        nqk = SW_NH * SW_DH
        qkn = xn[:, 1, 0:nqk].rearrange("p (a d) -> p a d", d=SW_DH)
        rope_s = xn[:, 1, nqk:2 * nqk].rearrange("p (a d) -> p a d", d=SW_DH)
        qr = xn[:, 1, 2 * nqk:2 * nqk + SW_GQ]
        ang_s = rope_s[:, 0:4, :].rearrange("p a d -> p (a d)").rearrange("p (t f) -> p t f", f=32)
        turn_s = qkn[:, 0:4, :].rearrange("p a d -> p (a d)").rearrange("p (t f) -> p t f", f=32)

        ps = ctx.enter_context(nc.psum_tensor("ps", [P, 8, HALF], F32))
        BT = (6, 7)
        BU = (4, 5)
        BD = (0, 1, 2, 3)
        BV, BG, BK, BSC, BO, BST, BY = 0, 1, 2, 3, 4, 5, 7
        SA, SB, SS, SP_, SO = 0, 1, 2, 4, 6
        BDS = (7, 1)

        raw_in = [sem(f"raw_in{i}") for i in range(RING)]
        const_in = sem("const_in")
        passed = {"SP": sem("sp_passed"), "DVE": sem("dve_passed")}
        gain_in = sem("gain_in")
        pos_in = sem("pos_in")
        x_in_s = sem("x_in_s")
        w_hi = sem("w_hi")
        w_lo = sem("w_lo")
        n_sq = sem("n_sq")
        n_var = sem("n_var")
        n_rsq = sem("n_rsq")
        n_scaled = sem("n_scaled")
        n_gained = sem("n_gained")
        n_tr = sem("n_tr")
        n_hi = sem("n_hi")
        n_lo = sem("n_lo")
        tab = sem("tab")
        tab_act = sem("tab_act")
        hc_set = sem("hc_set")
        qk_mm = sem("qk_mm")
        rope_mul = sem("rope_mul")
        rope_add = sem("rope_add")
        v_mm = sem("v_mm")
        g_mm = sem("g_mm")
        kt_mm = sem("kt_mm")
        sc_mm = sem("sc_mm")
        chunk_mm = sem("chunk_mm")
        yt_mm = sem("yt_mm")
        v_hi_s = sem("v_hi_s")
        v_lo_s = sem("v_lo_s")
        silu_s = sem("silu_s")
        q_hi_s = sem("q_hi_s")
        q_lo_s = sem("q_lo_s")
        k_hi_s = sem("k_hi_s")
        k_lo_s = sem("k_lo_s")
        sc_masked = sem("sc_masked")
        sc_hi_s = sem("sc_hi_s")
        sc_lo_s = sem("sc_lo_s")
        stats = sem("stats")
        g_rsq = sem("g_rsq")
        g_scale = sem("g_scale")
        st_upd = sem("st_upd")
        st_hi_s = sem("st_hi_s")
        st_lo_s = sem("st_lo_s")
        yn_s = sem("yn_s")
        y_s = sem("y_s")
        yT_s = sem("yT_s")
        yT_out = sem("yT_out")
        down_mm = sem("down_mm")
        x_add = sem("x_add")
        up_mm = sem("up_mm")
        relu_s = sem("relu_s")
        sqr_s = sem("sqr_s")
        a_hi_s = sem("a_hi_s")
        a_lo_s = sem("a_lo_s")
        sw_const = sem("sw_const")
        sw_zero = sem("sw_zero")
        a_mm = sem("a_mm")
        sw_sq = sem("sw_sq")
        sw_vhi = sem("sw_vhi")
        sw_vlo = sem("sw_vlo")
        sw_var = sem("sw_var")
        sw_rsq = sem("sw_rsq")
        sw_norm = sem("sw_norm")
        sw_rmul = sem("sw_rmul")
        sw_radd = sem("sw_radd")
        b_mm = sem("b_mm")
        sw_qhi = sem("sw_qhi")
        sw_qlo = sem("sw_qlo")
        c_mm = sem("c_mm")
        sw_masked = sem("sw_masked")
        sw_max = sem("sw_max")
        sw_exp = sem("sw_exp")
        sw_den = sem("sw_den")
        sw_prob = sem("sw_prob")
        d_mm = sem("d_mm")
        sw_phi = sem("sw_phi")
        sw_plo = sem("sw_plo")
        e_mm = sem("e_mm")
        sw_ohi = sem("sw_ohi")
        sw_olo = sem("sw_olo")
        stored = sem("stored")

        block = ctx.enter_context(nc.Block())

        def apart(eng):
            eng.sem_inc(passed[eng.engine.name], 1)

        def arrived(eng, m0, i, per, j, dmas=1):
            eng.wait_ge(raw_in[j % RING], 16 * (m0 // RING + j // RING + 1) + 16 * (per // RING) * i)

        def load_piece(sp, m0, i, per, j, src, fold):
            wait(sp, w_lo, m0 + per * i + j - RING + 1)
            apart(sp)
            dst = raw[:, j % RING, :]
            sp.dma_start(dst.rearrange("p (k n) -> p k n", n=fold), src).then_inc(raw_in[j % RING], 16)

        def split_hi(act, m0, i, per, j, dst, shape=None):
            arrived(act, m0, i, per, j)
            src = raw[:, j % RING, :]
            if shape:
                src = src.rearrange("p (k n) -> p k n", n=shape)
            act.activation(dst, src, ACT.Copy).then_inc(w_hi, 1)

        def split_lo(dve, m0, i, per, j, dst, hi, shape=None):
            dve.wait_ge(w_hi, m0 + per * i + j + 1)
            src = raw[:, j % RING, :]
            if shape:
                src = src.rearrange("p (k n) -> p k n", n=shape)
            dve.tensor_tensor(dst, src, hi.bitcast(F32), ALU.subtract).then_inc(w_lo, 1)

        def rsqrt(dve, count, base, a, r, t):
            dve.tensor_scalar(r.bitcast(I32), a.bitcast(I32), 1, None, ALU.logical_shift_right).then_inc(count, 1)
            dve.wait_ge(count, base + 1)
            dve.tensor_scalar(r.bitcast(I32), r.bitcast(I32), -1.0, float(0x5F3759DF), ALU.mult, ALU.add).then_inc(count, 1)
            for i in range(3):
                dve.wait_ge(count, base + 2 + 3 * i)
                dve.scalar_tensor_tensor(t, r, -0.5, r, ALU.mult, ALU.mult).then_inc(count, 1)
                dve.wait_ge(count, base + 3 + 3 * i)
                dve.tensor_tensor(t, t, a, ALU.mult).then_inc(count, 1)
                dve.wait_ge(count, base + 4 + 3 * i)
                dve.scalar_tensor_tensor(r, t, 1.5, r, ALU.add, ALU.mult).then_inc(count, 1)
            dve.wait_ge(count, base + RSQ)

        def product(pe, bank, pairs):
            last = None
            for i, (ah, al, bh, bl) in enumerate(pairs):
                pe.matmul(bank, ah, bh, start=(i == 0), stop=False)
                pe.matmul(bank, ah, bl, start=False, stop=False)
                last = pe.matmul(bank, al, bh, start=False, stop=(i == len(pairs) - 1))
            return last

        def norm_act_x(act, n, t):
            k = TT * n + t
            wait(act, n_tr, 2 * (k - 1))
            act.activation(xn[:, t % 2, :], x[:, t, :], ACT.Square, accum_out=ss[:, t:t + 1]).then_inc(n_sq, 1)
            act.wait_ge(n_rsq, RSQ * (k + 1))
            act.wait_ge(n_sq, k + 1)
            act.activation(xn[:, t % 2, :], x[:, t, :], ACT.Copy, scale=rstd[:, t:t + 1]).then_inc(n_scaled, 1)

        def norm_dve_var(dve, n, t):
            k = TT * n + t
            dve.wait_ge(n_sq, k + 1)
            dve.tensor_scalar(var[:, t:t + 1], ss[:, t:t + 1], 1.0 / D, EPS, ALU.mult, ALU.add).then_inc(n_var, 1)
            dve.wait_ge(n_var, k + 1)
            rsqrt(dve, n_rsq, RSQ * k, var[:, t:t + 1], rstd[:, t:t + 1], rtmp[:, t:t + 1])

        def norm_pool(pool, n, t):
            k = TT * n + t
            if t == 0:
                pool.wait_ge(gain_in, 16 * (n + 1))
            pool.wait_ge(n_scaled, k + 1)
            pool.tensor_tensor(xn[:, t % 2, :], xn[:, t % 2, :], gain_b[:], ALU.mult).then_inc(n_gained, 1)

        def norm_pe(pe, n, t):
            k = TT * n + t
            pe.wait_ge(n_gained, k + 1)
            for q in range(2):
                wait(pe, n_hi, 2 * (k - 1) + q + 1)
                wait(pe, n_lo, 2 * (k - 1) + q + 1)
                for j in range(4):
                    c = (4 * q + j) * P
                    last = pe.transpose(ps[:, BT[q], j * P:(j + 1) * P], xn[:, t % 2, c:c + P], ident[:])
                last.then_inc(n_tr, 1)

        def norm_act_hi(act, n, t):
            for q in range(2):
                act.wait_ge(n_tr, 2 * (TT * n + t) + q + 1)
                act.activation(hT_hi[:, 4 * q:4 * q + 4, t * P:(t + 1) * P],
                               ps[:, BT[q], :].rearrange("p (k n) -> p k n", n=P), ACT.Copy).then_inc(n_hi, 1)

        def norm_dve_lo(dve, n, t):
            for q in range(2):
                dve.wait_ge(n_hi, 2 * (TT * n + t) + q + 1)
                dve.tensor_tensor(hT_lo[:, 4 * q:4 * q + 4, t * P:(t + 1) * P],
                                  ps[:, BT[q], :].rearrange("p (k n) -> p k n", n=P),
                                  hT_hi[:, 4 * q:4 * q + 4, t * P:(t + 1) * P].bitcast(F32),
                                  ALU.subtract).then_inc(n_lo, 1)

        def hT_ready(eng, n, t):
            eng.wait_ge(n_lo, 2 * (TT * n + t + 1))

        def load_gain(sp, n, row):
            wait(sp, n_gained, TT * n)
            sp.dma_start(gain_b[:], row.partition_broadcast(P)).then_inc(gain_in, 16)

        def down_tile(pe, g, t, b=0, banks=BD):
            for c in range(2):
                nb = len(banks)
                bank = ps[:, banks[(2 * t + c) % nb], :]
                wait(pe, x_add, 16 * g + 2 * t + c + 1 - nb)
                product(pe, bank, [(aT_hi[b][:, k, t * P:(t + 1) * P], aT_lo[b][:, k, t * P:(t + 1) * P],
                                    wd_hi[b][:, k, c * HALF:(c + 1) * HALF], wd_lo[b][:, k, c * HALF:(c + 1) * HALF])
                                   for k in range(2)]).then_inc(down_mm, 1)

        def add_tile(dve, g, t, banks=BD):
            for c in range(2):
                dve.wait_ge(down_mm, 16 * g + 2 * t + c + 1)
                xs = x[:, t, c * HALF:(c + 1) * HALF]
                dve.tensor_tensor(xs, ps[:, banks[(2 * t + c) % len(banks)], :], xs, ALU.add).then_inc(x_add, 1)

        def mlp_up(pe, u, i):
            half, f = i // 2, i % 2
            wait(pe, relu_s, 4 * u + i - 1)
            product(pe, ps[:, BU[i % 2], :],
                    [(wu_hi[:, k, f * P:(f + 1) * P], wu_lo[:, k, f * P:(f + 1) * P],
                      hT_hi[:, k, half * HALF:(half + 1) * HALF], hT_lo[:, k, half * HALF:(half + 1) * HALF])
                     for k in range(KT)]).then_inc(up_mm, 1)

        def mlp_pe(pe, g, u0, dg0, pc0, n, tile_done):
            pe.wait_ge(w_lo, pc0 + 4 * g + 2)
            for i in range(4):
                if isinstance(g, int) and g == 0:
                    hT_ready(pe, n, 4 * (i // 2) + 3)
                mlp_up(pe, u0 + g, i)
            pe.wait_ge(w_lo, pc0 + 4 * g + 4)
            for t in range(TT):
                if t % 4 == 0:
                    pe.wait_ge(a_lo_s, 4 * (u0 + g) + 2 * (t // 4) + 2)
                down_tile(pe, dg0 + g, t)
                if tile_done:
                    tile_done(t)

        def mlp_sp(sp, layer, g, pc0, up):
            wu = w_up[layer].rearrange("(k p) n -> p k n", p=P)
            wd = w_down[layer].rearrange("(k p) n -> p k n", p=P)
            for j in range(2):
                if up:
                    load_piece(sp, pc0, g, 4, j, wu[:, 4 * j:4 * j + 4, bass.ds(256 * g, 256)], 256)
            for j in range(2):
                if not up:
                    load_piece(sp, pc0, g, 4, 2 + j, wd[:, bass.ds(2 * g + j, 1), :], D)

        def mlp_up_hi(act, g, pc0):
            for j in range(2):
                split_hi(act, pc0, g, 4, j, wu_hi[:, 4 * j:4 * j + 4, :], 256)

        def mlp_up_lo(dve, g, pc0):
            for j in range(2):
                split_lo(dve, pc0, g, 4, j, wu_lo[:, 4 * j:4 * j + 4, :], wu_hi[:, 4 * j:4 * j + 4, :], 256)

        def mlp_act(act, g, u0, dg0, pc0):
            act.wait_ge(down_mm, 16 * (dg0 + g))
            for j in range(2):
                split_hi(act, pc0, g, 4, 2 + j, wd_hi[0][:, j, :])
            for i in range(4):
                half, f = i // 2, i % 2
                k = 4 * (u0 + g) + i
                act.wait_ge(up_mm, k + 1)
                wait(act, sqr_s, k - 1)
                wait(act, a_hi_s, k - 1)
                act.activation(relu_t[:, i % 2, :], ps[:, BU[i % 2], :], ACT.Relu).then_inc(relu_s, 1)
                act.wait_ge(relu_s, k + 1)
                act.activation(aT_hi[0][:, f, half * HALF:(half + 1) * HALF], relu_t[:, i % 2, :],
                               ACT.Square).then_inc(a_hi_s, 1)

        def mlp_pool(pool, g, u0):
            for i in range(4):
                k = 4 * (u0 + g) + i
                pool.wait_ge(relu_s, k + 1)
                wait(pool, a_lo_s, k - 1)
                pool.tensor_tensor(sqr_t[:, i % 2, :], relu_t[:, i % 2, :], relu_t[:, i % 2, :], ALU.mult).then_inc(sqr_s, 1)

        def mlp_dve(dve, g, u0, dg0, pc0, next_lo, tile_done):
            for i in range(4):
                half, f = i // 2, i % 2
                k = 4 * (u0 + g) + i
                if i < 2:
                    split_lo(dve, pc0, g, 4, 2 + i, wd_lo[0][:, i, :], wd_hi[0][:, i, :])
                dve.wait_ge(sqr_s, k + 1)
                dve.wait_ge(a_hi_s, k + 1)
                dve.tensor_tensor(aT_lo[0][:, f, half * HALF:(half + 1) * HALF], sqr_t[:, i % 2, :],
                                  aT_hi[0][:, f, half * HALF:(half + 1) * HALF].bitcast(F32),
                                  ALU.subtract).then_inc(a_lo_s, 1)
            for t in range(TT):
                add_tile(dve, dg0 + g, t)
                if t == 1:
                    next_lo()
                if tile_done:
                    tile_done(t)

        MLP_LAST = MLP_GROUPS - 1

        def mlp_pe_all(pe, u0, dg0, pc0, n, n_next):
            mlp_pe(pe, 0, u0, dg0, pc0, n, None)
            with pe.Fori(1, MLP_LAST) as g:
                mlp_pe(pe, g, u0, dg0, pc0, n, None)

            def tile(t):
                if n_next is not None and t >= 2:
                    norm_pe(pe, n_next, t - 2)
            mlp_pe(pe, MLP_LAST, u0, dg0, pc0, n, tile)
            if n_next is not None:
                norm_pe(pe, n_next, TT - 2)
                norm_pe(pe, n_next, TT - 1)

        def mlp_act_all(act, u0, dg0, pc0):
            def body(g):
                mlp_act(act, g, u0, dg0, pc0)
                act.wait_ge(up_mm, 4 * (u0 + g + 1))
                mlp_up_hi(act, g + 1, pc0)
            body(0)
            with act.Fori(1, MLP_LAST) as g:
                body(g)
            mlp_act(act, MLP_LAST, u0, dg0, pc0)

        def mlp_dve_all(dve, u0, dg0, pc0, n_next, last_lo):
            mlp_dve(dve, 0, u0, dg0, pc0, lambda: mlp_up_lo(dve, 1, pc0), None)
            with dve.Fori(1, MLP_LAST) as g:
                mlp_dve(dve, g, u0, dg0, pc0, lambda: mlp_up_lo(dve, g + 1, pc0), None)
            mlp_dve(dve, MLP_LAST, u0, dg0, pc0, last_lo,
                    None if n_next is None else lambda t: norm_dve_step(dve, n_next, t))
            if n_next is not None:
                norm_dve_step(dve, n_next, TT)
                norm_dve_step(dve, n_next, TT + 1)

        def mlp_pool_all(pool, u0):
            mlp_pool(pool, 0, u0)
            with pool.Fori(1, MLP_GROUPS) as g:
                mlp_pool(pool, g, u0)

        def mlp_sp_all(sp, layer, pc0):
            mlp_sp(sp, layer, 0, pc0, True)
            with sp.Fori(0, MLP_LAST) as g:
                mlp_sp(sp, layer, g, pc0, False)
                mlp_sp(sp, layer, g + 1, pc0, True)
            mlp_sp(sp, layer, MLP_LAST, pc0, False)

        def norm_after(act, n, dg):
            for t in range(TT):
                act.wait_ge(x_add, 16 * dg + 2 * t + 2)
                norm_act_x(act, n, t)
                if t >= 1:
                    norm_act_hi(act, n, t - 1)
            norm_act_hi(act, n, TT - 1)

        def norm_dve_step(dve, n, t):
            if t >= 2:
                norm_dve_lo(dve, n, t - 2)
            if t < TT:
                norm_dve_var(dve, n, t)

        def qk_pair(pe, h, i):
            pe.wait_ge(w_lo, RET_PIECES * h + 2 * (i // 2) + 2)
            if i == 0:
                wait(pe, v_lo_s, NCH * h)
                wait(pe, silu_s, NCH * h)
            if i == 1:
                wait(pe, k_lo_s, NCH * h)
                wait(pe, sc_masked, NCH * h)
            if i >= 2:
                pe.wait_ge(rope_mul, 16 * h + 4 * (i - 1))
            half = i % 2
            for a in range(2):
                j = 2 * (i // 2) + a
                wh = wqg_hi[:, j, :].rearrange("p (k n) -> p k n", n=P)
                wl = wqg_lo[:, j, :].rearrange("p (k n) -> p k n", n=P)
                last = product(pe, ps[:, 2 * (i % 2) + a, :],
                               [(wh[:, k, :], wl[:, k, :], hT_hi[:, k, half * HALF:(half + 1) * HALF],
                                 hT_lo[:, k, half * HALF:(half + 1) * HALF]) for k in range(KT)])
            last.then_inc(qk_mm, 1)

        def vg_product(pe, n, bank, w_h, w_l):
            return product(pe, ps[:, bank, :],
                           [(hT_hi[:, k, n * P:(n + 1) * P], hT_lo[:, k, n * P:(n + 1) * P],
                             w_h[:, k // 2, (k % 2) * HALF:(k % 2 + 1) * HALF],
                             w_l[:, k // 2, (k % 2) * HALF:(k % 2 + 1) * HALF]) for k in range(KT)])

        def v_proj(pe, h, n):
            if n == 0:
                pe.wait_ge(w_lo, RET_PIECES * h + 8)
                pe.wait_ge(rope_mul, 16 * h + 12)
            else:
                pe.wait_ge(v_lo_s, NCH * h + n)
            vg_product(pe, n, BV, wv_hi, wv_lo).then_inc(v_mm, 1)

        def g_proj(pe, h, n):
            if n == 0:
                pe.wait_ge(w_lo, RET_PIECES * h + 12)
            else:
                pe.wait_ge(silu_s, NCH * h + n)
            vg_product(pe, n, BG, wqg_hi, wqg_lo).then_inc(g_mm, 1)

        def y_transpose(pe, h, n):
            pe.wait_ge(y_s, NCH * h + n + 1)
            wait(pe, yT_s, NCH * h + n)
            for j in range(4):
                last = pe.transpose(ps[:, BY, j * P:(j + 1) * P], y[:, j * P:(j + 1) * P], ident[:])
            last.then_inc(yt_mm, 1)

        def chunk_pe(pe, h, n):
            k = NCH * h + n
            cols = slice(n * CH, (n + 1) * CH)
            if n == 0:
                pe.wait_ge(rope_add, 8 * h + 8)
                pe.wait_ge(rope_mul, 16 * h + 16)
            else:
                pe.wait_ge(k_lo_s, k)
                pe.wait_ge(sc_masked, k)
            for j in range(2):
                last = pe.transpose(ps[:, BK, j * P:(j + 1) * P], kq[:, j, cols], ident[:])
            last.then_inc(kt_mm, 1)
            for j in range(2):
                last = pe.matmul(ps[:, BSC, 0:CH], kq[:, j, cols], kq[:, 2 + j, cols], start=(j == 0), stop=(j == 1))
            last.then_inc(sc_mm, 1)
            if n < NCH - 1:
                v_proj(pe, h, n + 1)
            wait(pe, yn_s, k)
            pe.wait_ge(q_lo_s, k + 1)
            pairs = []
            if n:
                pe.wait_ge(st_lo_s, (NCH - 1) * h + n)
                pairs = [(q_hi[:, j, :], q_lo[:, j, :], st_hi[:, j, :], st_lo[:, j, :]) for j in range(2)]
            pe.wait_ge(sc_lo_s, k + 1)
            pe.wait_ge(v_lo_s, k + 1)
            last = product(pe, ps[:, BO, :], pairs + [(sc_hi[:], sc_lo[:], v_hi[:], v_lo[:])])
            if n < NCH - 1:
                pe.wait_ge(k_lo_s, k + 1)
                wait(pe, st_upd, (NCH - 1) * h + n)
                for j in range(2):
                    last = product(pe, ps[:, BST + j, :],
                                   [(k_hi[:, j * P:(j + 1) * P], k_lo[:, j * P:(j + 1) * P], v_hi[:], v_lo[:])])
            last.then_inc(chunk_mm, 1)
            if n < NCH - 1:
                g_proj(pe, h, n + 1)
                y_transpose(pe, h, n)

        def head_pe(pe, h, first):
            qk_pair(pe, h, 0)
            if not first:
                y_transpose(pe, h - 1, NCH - 1)
            for i in range(1, 4):
                qk_pair(pe, h, i)
            v_proj(pe, h, 0)
            g_proj(pe, h, 0)
            for n in range(NCH):
                chunk_pe(pe, h, n)

        def v_hi_act(act, h, n):
            k = NCH * h + n
            if n == 0:
                act.wait_ge(hc_set, h + 1)
            act.wait_ge(v_mm, k + 1)
            wait(act, chunk_mm, k)
            act.activation(v_hi[:], ps[:, BV, :], ACT.Copy, scale=hc[:, 0:1]).then_inc(v_hi_s, 1)

        def silu_act(act, h, n):
            k = NCH * h + n
            act.wait_ge(g_mm, k + 1)
            wait(act, y_s, k)
            act.activation(sgate[:], ps[:, BG, :], ACT.Silu).then_inc(silu_s, 1)

        def yT_act(act, h, n):
            k = NCH * h + n
            act.wait_ge(yt_mm, k + 1)
            wait(act, yT_out, 16 * k)
            act.activation(yT, ps[:, BY, :], ACT.Copy).then_inc(yT_s, 1)

        def qk_hi_act(act, h):
            wait(act, g_mm, NCH * h)
            for j in range(4):
                split_hi(act, 0, h, RET_PIECES, j, wqg_hi[:, j, :])

        def chunk_act(act, h, n, before_end=None):
            k = NCH * h + n
            cols = slice(n * CH, (n + 1) * CH)
            if n == 0:
                act.wait_ge(rope_add, 8 * h + 8)
            wait(act, chunk_mm, k)
            act.activation(q_hi[:], kq[:, 2:4, cols], ACT.Copy).then_inc(q_hi_s, 1)
            act.wait_ge(kt_mm, k + 1)
            act.activation(k_hi[:], ps[:, BK, 0:DK], ACT.Copy).then_inc(k_hi_s, 1)
            act.wait_ge(sc_masked, k + 1)
            act.activation(sc_hi[:], sc[:], ACT.Copy).then_inc(sc_hi_s, 1)
            if n < NCH - 1:
                v_hi_act(act, h, n + 1)
            elif before_end:
                before_end()
            act.wait_ge(g_scale, 2 * k + 2)
            wait(act, y_s, k)
            act.activation(yn, ps[:, BO, :], ACT.Identity, bias=gbias[:], scale=gscale[:]).then_inc(yn_s, 1)
            if n < NCH - 1:
                act.wait_ge(st_upd, (NCH - 1) * h + n + 1)
                act.activation(st_hi[:], state[:], ACT.Copy, scale=hc[:, 3:4]).then_inc(st_hi_s, 1)
                silu_act(act, h, n + 1)
                yT_act(act, h, n)

        def head_act(act, h, first, last):
            if not first:
                yT_act(act, h - 1, NCH - 1)
            for j in range(4):
                if j == 0:
                    if first:
                        act.wait_ge(n_scaled, TT)
                    else:
                        act.wait_ge(v_mm, NCH * h)
                split_hi(act, 0, h, RET_PIECES, 4 + j, wv_hi[:, j, :])
            for j in range(4):
                act.wait_ge(qk_mm, 4 * h + 2 * (j // 2) + 2)
                split_hi(act, 0, h, RET_PIECES, 8 + j, wqg_hi[:, j, :])
            v_hi_act(act, h, 0)
            silu_act(act, h, 0)
            for n in range(NCH):
                chunk_act(act, h, n, None if last else lambda: qk_hi_act(act, h + 1))

        def rope_dve(dve, h, i):
            half = i % 2
            cols = slice(half * HALF, (half + 1) * HALF)
            a, b = ps[:, 2 * (i % 2), :], ps[:, 2 * (i % 2) + 1, :]
            j = 2 * (i // 2)
            dve.wait_ge(qk_mm, 4 * h + i + 1)
            dve.tensor_tensor(kq[:, j, cols], a, cosr[:, cols], ALU.mult).then_inc(rope_mul, 1)
            dve.tensor_tensor(kq[:, j + 1, cols], b, cosr[:, cols], ALU.mult).then_inc(rope_mul, 1)
            wait(dve, rope_add, 8 * h + 2 * i - 1)
            dve.tensor_tensor(rope_t[:], b, sinr[:, cols], ALU.mult).then_inc(rope_mul, 1)
            wait(dve, rope_add, 8 * h + 2 * i)
            dve.tensor_tensor(rope_u, a, sinr[:, cols], ALU.mult).then_inc(rope_mul, 1)

        def rope_pool(pool, h, i):
            cols = slice((i % 2) * HALF, (i % 2 + 1) * HALF)
            j = 2 * (i // 2)
            pool.wait_ge(rope_mul, 16 * h + 4 * i + 3)
            pool.tensor_tensor(kq[:, j, cols], kq[:, j, cols], rope_t[:], ALU.subtract).then_inc(rope_add, 1)
            pool.wait_ge(rope_mul, 16 * h + 4 * i + 4)
            pool.tensor_tensor(kq[:, j + 1, cols], kq[:, j + 1, cols], rope_u, ALU.add).then_inc(rope_add, 1)

        def y_pool(pool, h, n):
            k = NCH * h + n
            pool.wait_ge(yn_s, k + 1)
            pool.wait_ge(silu_s, k + 1)
            wait(pool, yt_mm, k)
            pool.tensor_tensor(y, yn, sgate[:], ALU.mult).then_inc(y_s, 1)

        def v_lo_dve(dve, h, n):
            dve.wait_ge(v_hi_s, NCH * h + n + 1)
            dve.scalar_tensor_tensor(v_lo[:], ps[:, BV, :], hc[:, 0:1], v_hi[:].bitcast(F32),
                                     ALU.mult, ALU.subtract).then_inc(v_lo_s, 1)

        def qk_lo_dve(dve, h):
            for j in range(4):
                split_lo(dve, 0, h, RET_PIECES, j, wqg_lo[:, j, :], wqg_hi[:, j, :])

        def chunk_dve(dve, h, n, before_end=None):
            k = NCH * h + n
            cols = slice(n * CH, (n + 1) * CH)
            dve.wait_ge(q_hi_s, k + 1)
            dve.tensor_tensor(q_lo[:], kq[:, 2:4, cols], q_hi[:].bitcast(F32), ALU.subtract).then_inc(q_lo_s, 1)
            dve.wait_ge(sc_mm, k + 1)
            wait(dve, sc_lo_s, k)
            wait(dve, sc_hi_s, k)
            dve.tensor_tensor(sc[:], ps[:, BSC, 0:CH], causal[:], ALU.mult).then_inc(sc_masked, 1)
            dve.wait_ge(k_hi_s, k + 1)
            dve.tensor_tensor(k_lo[:], ps[:, BK, 0:DK], k_hi[:].bitcast(F32), ALU.subtract).then_inc(k_lo_s, 1)
            dve.wait_ge(sc_hi_s, k + 1)
            dve.wait_ge(sc_masked, k + 1)
            dve.tensor_tensor(sc_lo[:], sc[:], sc_hi[:].bitcast(F32), ALU.subtract).then_inc(sc_lo_s, 1)
            if n == NCH - 1 and before_end:
                before_end()
            dve.wait_ge(chunk_mm, k + 1)
            dve.bn_stats(bn[:], ps[:, BO, :]).then_inc(stats, 1)
            dve.wait_ge(stats, 3 * k + 1)
            apart(dve)
            dve.bn_aggr(mv[:], bn[:]).then_inc(stats, 1)
            dve.wait_ge(stats, 3 * k + 2)
            dve.tensor_scalar(gvar[:], mv[:, 1:2], hc[:, 2:3], EPS, ALU.mult, ALU.add).then_inc(stats, 1)
            dve.wait_ge(stats, 3 * k + 3)
            rsqrt(dve, g_rsq, RSQ * k, gvar[:], grs[:], gtmp[:])
            wait(dve, yn_s, k)
            dve.tensor_tensor(gscale[:], grs[:], hc[:, 1:2], ALU.mult).then_inc(g_scale, 1)
            dve.wait_ge(g_scale, 2 * k + 1)
            dve.scalar_tensor_tensor(gbias[:], mv[:, 0:1], -1.0, gscale[:], ALU.mult, ALU.mult).then_inc(g_scale, 1)
            if n < NCH - 1:
                v_lo_dve(dve, h, n + 1)
                s = (NCH - 1) * h + n
                upd = ps[:, BST:BST + 2, :]
                if n == 0:
                    dve.tensor_copy(state[:], upd).then_inc(st_upd, 1)
                else:
                    dve.scalar_tensor_tensor(state[:], state[:], hc[:, 3:4], upd, ALU.mult, ALU.add).then_inc(st_upd, 1)
                dve.wait_ge(st_hi_s, s + 1)
                dve.wait_ge(st_upd, s + 1)
                dve.scalar_tensor_tensor(st_lo[:], state[:], hc[:, 3:4], st_hi[:].bitcast(F32),
                                         ALU.mult, ALU.subtract).then_inc(st_lo_s, 1)

        def head_dve(dve, h, last):
            wait(dve, yn_s, NCH * h)
            dve.tensor_copy(hc[:], headc[:, bass.ds(h, 1), :]).then_inc(hc_set, 1)
            dve.wait_ge(hc_set, h + 1)
            for i in range(4):
                rope_dve(dve, h, i)
                for j in range(2):
                    m = 4 + 2 * i + j
                    hi, lo, jj = (wv_hi, wv_lo, m - 4) if m < 8 else (wqg_hi, wqg_lo, m - 8)
                    split_lo(dve, 0, h, RET_PIECES, m, lo[:, jj, :], hi[:, jj, :])
            v_lo_dve(dve, h, 0)
            for n in range(NCH):
                chunk_dve(dve, h, n, None if last else lambda: qk_lo_dve(dve, h + 1))

        def head_pool(pool, h):
            for i in range(4):
                rope_pool(pool, h, i)
            for n in range(NCH):
                y_pool(pool, h, n)

        ret_w = ret_in[0].rearrange("(k p) n -> p k n", p=P)

        def qk_sp(sp, h):
            for j in range(4):
                c = (D if j < 2 else 0) + (j % 2) * P
                load_piece(sp, 0, h, RET_PIECES, j, ret_w[:, :, bass.ds(c + DK * h, P)], P)

        def yT_sp(sp, h, n):
            k = NCH * h + n
            sp.wait_ge(yT_s, k + 1)
            apart(sp)
            dst = y_dram[bass.ds(DV * h, DV), n * P:(n + 1) * P].rearrange("(j p) n -> p j n", p=P)
            sp.dma_start(dst, yT.rearrange("p (j n) -> p j n", n=P)).then_inc(yT_out, 16)

        def head_sp(sp, h, last):
            for j in range(8):
                c = 2 * D + (j // 4) * HEADS * DV
                load_piece(sp, 0, h, RET_PIECES, 4 + j,
                           ret_w[:, 2 * (j % 4):2 * (j % 4) + 2, bass.ds(c + DV * h, DV)], DV)
            for n in range(NCH):
                if n == 4 and not last:
                    qk_sp(sp, h + 1)
                if n < NCH - 1:
                    yT_sp(sp, h, n)

        ret_o = ret_out[0].rearrange("(k p) n -> p k n", p=P)
        y_k = y_dram.rearrange("(k p) n -> p k n", p=P)

        def out_sp(sp, g):
            for j in range(2):
                load_piece(sp, PC_OUT, g, 4, j, y_k[:, bass.ds(2 * g + j, 1), :], D)
            for j in range(2):
                load_piece(sp, PC_OUT, g, 4, 2 + j, ret_o[:, bass.ds(2 * g + j, 1), :], D)

        def out_act(act, g, b):
            if isinstance(g, int) and g < 2:
                act.wait_ge(yt_mm, NCH * HEADS)
            else:
                act.wait_ge(down_mm, 16 * (g - 1))
            for j in range(2):
                split_hi(act, PC_OUT, g, 4, j, aT_hi[b][:, j, :])
            for j in range(2):
                split_hi(act, PC_OUT, g, 4, 2 + j, wd_hi[b][:, j, :])

        def out_lo(dve, g, b, j):
            if j < 2:
                split_lo(dve, PC_OUT, g, 4, j, aT_lo[b][:, j, :], aT_hi[b][:, j, :])
            else:
                split_lo(dve, PC_OUT, g, 4, j, wd_lo[b][:, j - 2, :], wd_hi[b][:, j - 2, :])

        def out_dve(dve, g, b, next_lo, tile_done=None):
            for t in range(TT):
                add_tile(dve, g, t)
                next_lo(t)
                if tile_done:
                    tile_done(t)

        def out_pe(pe, g, b, tile_done=None):
            pe.wait_ge(w_lo, PC_OUT + 4 * g + 4)
            for t in range(TT):
                down_tile(pe, g, t, b)
                if tile_done:
                    tile_done(t)

        sw_w = sw_in[0].rearrange("(k p) n -> p k n", p=P)
        sw_o = sw_out[0].rearrange("(k p) n -> p k n", p=P)
        KC = SW_HEADS * SW_DH
        VC = KC + SW_KV * SW_DH

        def sw_sp_in(sp, g):
            for j in range(2):
                load_piece(sp, PC_SW, g, SW_PIECES, j, sw_w[:, :, bass.ds(SW_GQ * g + j * P, P)], P)
            for j in range(2):
                m = PC_SW + SW_PIECES * g + 2 + j
                wait(sp, w_lo, m - RING + 1)
                apart(sp)
                c = KC if j == 0 else VC
                dst = raw[:, 2 + j, 0:KT * SW_DH].rearrange("p (k n) -> p k n", n=SW_DH)
                sp.dma_start(dst, sw_w[:, :, bass.ds(c + SW_DH * g, SW_DH)]).then_inc(raw_in[2 + j], 16)

        def sw_sp_out(sp, g):
            for j in range(4):
                m = PC_SW + SW_PIECES * g + 4 + j
                wait(sp, w_lo, m - RING + 1)
                apart(sp)
                src = sw_o[:, bass.ds(2 * g + j // 2, 1), (j % 2) * HALF:(j % 2 + 1) * HALF]
                dst = raw[:, j, 0:HALF].rearrange("p (k n) -> p k n", n=HALF)
                sp.dma_start(dst, src).then_inc(raw_in[j], 16)

        def sw_piece(j):
            if j < 2:
                return (raw[:, j, :].rearrange("p (k n) -> p k n", n=P),
                        ws_hi[:, :, j * P:(j + 1) * P], ws_lo[:, :, j * P:(j + 1) * P])
            if j < 4:
                c = SW_GQ + (j - 2) * SW_DH
                return (raw[:, j, 0:KT * SW_DH].rearrange("p (k n) -> p k n", n=SW_DH),
                        ws_hi[:, :, c:c + SW_DH], ws_lo[:, :, c:c + SW_DH])
            k, c = (j - 4) // 2, (j % 2) * HALF
            return raw[:, j - 4, 0:HALF], wd_hi[0][:, k, c:c + HALF], wd_lo[0][:, k, c:c + HALF]

        def sw_split_hi(act, g, j):
            arrived(act, PC_SW, g, SW_PIECES, j)
            src, hi, _ = sw_piece(j)
            act.activation(hi, src, ACT.Copy).then_inc(w_hi, 1)

        def sw_split_lo(dve, g, j):
            dve.wait_ge(w_hi, PC_SW + SW_PIECES * g + j + 1)
            src, hi, lo = sw_piece(j)
            dve.tensor_tensor(lo, src, hi.bitcast(F32), ALU.subtract).then_inc(w_lo, 1)

        def a_pe(pe, g, t):
            i = TT * g + t
            if t == 0:
                pe.wait_ge(w_lo, PC_SW + SW_PIECES * g + 4)
                if isinstance(g, int) and g == 0:
                    pe.wait_ge(x_add, 16 * DG_SW)
            if isinstance(g, int) and g == 0:
                hT_ready(pe, 2, t)
            wait(pe, sw_vlo, i)
            wait(pe, sw_norm, 2 * i)
            product(pe, ps[:, SA, 0:SW_COLS],
                    [(hT_hi[:, k, t * P:(t + 1) * P], hT_lo[:, k, t * P:(t + 1) * P], ws_hi[:, k, :], ws_lo[:, k, :])
                     for k in range(KT)]).then_inc(a_mm, 1)

        def b_pe(pe, g, t):
            i = TT * g + t
            pe.wait_ge(sw_radd, 4 * (i + 1))
            wait(pe, sw_qlo, 2 * i)
            wait(pe, x_add, 16 * DG_SW + 2 * (i - 2))
            krf = kr[:, :, :].rearrange("p a d -> p (a d)")
            for j in range(2):
                pe.transpose(ps[:, SB, j * P:(j + 1) * P], qr[:, j * P:(j + 1) * P], ident[:])
            pe.transpose(ps[:, SB, 2 * P:3 * P], krf[:, SW_DH:3 * SW_DH], ident[:])
            pe.transpose(ps[:, SB, 3 * P:4 * P], krf[:, 0:2 * SW_DH], ident[:]).then_inc(b_mm, 1)

        def c_pe(pe, g, t):
            i = TT * g + t
            pe.wait_ge(sw_qlo, 2 * (i + 1))
            for j in range(2):
                wait(pe, sw_masked, 2 * (i - 1) + j + 1)
                product(pe, ps[:, SS + j, :],
                        [(qT_hi[:, j, :], qT_lo[:, j, :], kT_hi[:].rearrange("p e s n -> p (e s n)"),
                          kT_lo[:].rearrange("p e s n -> p (e s n)"))]).then_inc(c_mm, 1)

        def d_pe(pe, g, t):
            i = TT * g + t
            pe.wait_ge(sw_prob, i + 1)
            for s in range(2):
                wait(pe, sw_plo, 2 * (i - 1) + s + 1)
                for hh in range(4):
                    last = pe.transpose(ps[:, SP_ + s, hh * P:(hh + 1) * P], prob[:, hh, s, :], ident[:])
                last.then_inc(d_mm, 1)

        def e_pe(pe, g, t):
            i = TT * g + t
            pe.wait_ge(sw_plo, 2 * (i + 1))
            wait(pe, sw_olo, i)
            if isinstance(g, int) and i == 0:
                hT_ready(pe, 2, TT - 1)
            pairs = []
            for s in range(2):
                vs = t % 4 if t % 2 == s else (t - 1) % 4
                for odd in range(2):
                    c = slice(SW_DH, 3 * SW_DH) if odd == 0 else slice(0, 2 * SW_DH)
                    pairs.append((vp_hi[:, vs, c], vp_lo[:, vs, c], pT_hi[:, s, odd::2, :], pT_lo[:, s, odd::2, :]))
            product(pe, ps[:, SO, 0:2 * P].rearrange("p (j n) -> p j n", n=P), pairs).then_inc(e_mm, 1)

        def f_pe(pe, g, t):
            i = TT * g + t
            pe.wait_ge(sw_olo, i + 1)
            if t == 0:
                pe.wait_ge(w_lo, PC_SW + SW_PIECES * g + 8)
            down_tile(pe, DG_SW + g, t, 0, BDS)

        def sq_act(act, g, t):
            i = TT * g + t
            act.wait_ge(a_mm, i + 1)
            wait(act, sw_rmul, 4 * i)
            act.activation(qkn, ps[:, SA, 0:SW_NH * SW_DH].rearrange("p (a d) -> p a d", d=SW_DH),
                           ACT.Square).then_inc(sw_sq, 1)
            wait(act, e_mm, i - 2)
            act.activation(vp_hi[:, t % 4, SW_DH:2 * SW_DH], ps[:, SA, SW_GQ + SW_DH:SW_COLS],
                           ACT.Copy).then_inc(sw_vhi, 1)

        def qkT_act(act, g, t):
            i = TT * g + t
            act.wait_ge(b_mm, i + 1)
            wait(act, c_mm, 2 * i)
            tr = ps[:, SB, :].rearrange("p (j n) -> p j n", n=P)
            act.activation(qT_hi[:], tr[:, 0:2, :], ACT.Copy).then_inc(sw_qhi, 1)
            act.activation(kT_hi[:, :, t % 2, :], tr[:, 2:4, :], ACT.Copy).then_inc(sw_qhi, 1)

        def pT_act(act, g, t):
            i = TT * g + t
            for s in range(2):
                act.wait_ge(d_mm, 2 * i + s + 1)
                wait(act, e_mm, i)
                act.activation(pT_hi[:, s, :, :], ps[:, SP_ + s, :].rearrange("p (j n) -> p j n", n=P),
                               ACT.Copy).then_inc(sw_phi, 1)

        def exp_act(act, g, t):
            i = TT * g + t
            act.wait_ge(sw_max, 4 * (i + 1))
            wait(act, sw_den, 2 * i)
            for hh in range(4):
                act.activation(prob[:, hh, :, :], prob[:, hh, :, :], ACT.Exp, bias=nmax[:, hh:hh + 1],
                               accum_out=ssum[:, hh:hh + 1]).then_inc(sw_exp, 1)
            act.activation(esink[:], sdif[:], ACT.Exp).then_inc(sw_exp, 1)

        def oT_act(act, g, t):
            i = TT * g + t
            act.wait_ge(e_mm, i + 1)
            wait(act, down_mm, 16 * (DG_SW + g - 1) + 2 * t + 2)
            act.activation(aT_hi[0][:, :, t * P:(t + 1) * P], ps[:, SO, 0:2 * P].rearrange("p (j n) -> p j n", n=P),
                           ACT.Copy).then_inc(sw_ohi, 1)

        def qkT_dve(dve, g, t):
            i = TT * g + t
            tr = ps[:, SB, :].rearrange("p (j n) -> p j n", n=P)
            dve.wait_ge(sw_qhi, 2 * i + 2)
            dve.tensor_tensor(qT_lo[:], tr[:, 0:2, :], qT_hi[:].bitcast(F32), ALU.subtract).then_inc(sw_qlo, 1)
            dve.tensor_tensor(kT_lo[:, :, t % 2, :], tr[:, 2:4, :], kT_hi[:, :, t % 2, :].bitcast(F32),
                              ALU.subtract).then_inc(sw_qlo, 1)

        def pT_dve(dve, g, t):
            i = TT * g + t
            for s in range(2):
                dve.wait_ge(sw_phi, 2 * i + s + 1)
                dve.tensor_tensor(pT_lo[:, s, :, :], ps[:, SP_ + s, :].rearrange("p (j n) -> p j n", n=P),
                                  pT_hi[:, s, :, :].bitcast(F32), ALU.subtract).then_inc(sw_plo, 1)

        def mask_dve(dve, g, t):
            i = TT * g + t
            b = 2 if t == 0 else (1 if t % 2 else 0)
            for j in range(2):
                dve.wait_ge(c_mm, 2 * i + j + 1)
                wait(dve, d_mm, 2 * i)
                for e in range(2):
                    ins = dve.scalar_tensor_tensor(
                        prob[:, 2 * j + e, :, :], ps[:, SS + j, e * 2 * P:(e + 1) * 2 * P].rearrange("p (s n) -> p s n", n=P),
                        SW_DH ** -0.5, swmask[:, b:b + 2, :], ALU.mult, ALU.add)
                ins.then_inc(sw_masked, 1)
            dve.wait_ge(sw_masked, 2 * (i + 1))
            wait(dve, sw_exp, 5 * i)
            dve.tensor_reduce(smax[:], prob.rearrange("p h s n -> p h (s n)"), axis=AX.X, op=ALU.max).then_inc(sw_max, 1)
            dve.wait_ge(sw_max, 4 * i + 1)
            dve.tensor_tensor(smax[:], smax[:], sink_b[:, bass.ds(4 * g, 4)], ALU.max).then_inc(sw_max, 1)
            dve.wait_ge(sw_max, 4 * i + 2)
            dve.tensor_scalar(nmax[:], smax[:], -1.0, None, ALU.mult).then_inc(sw_max, 1)
            dve.tensor_tensor(sdif[:], sink_b[:, bass.ds(4 * g, 4)], smax[:], ALU.subtract).then_inc(sw_max, 1)

        def den_dve(dve, g, t):
            i = TT * g + t
            dve.wait_ge(sw_exp, 5 * (i + 1))
            wait(dve, sw_prob, i)
            dve.tensor_tensor(den[:], ssum[:], esink[:], ALU.add).then_inc(sw_den, 1)
            dve.wait_ge(sw_den, 2 * i + 1)
            dve.reciprocal(rden[:], den[:]).then_inc(sw_den, 1)

        def norm_dve(dve, g, t):
            i = TT * g + t
            dve.wait_ge(sw_vhi, i + 1)
            dve.tensor_tensor(vp_lo[:, t % 4, SW_DH:2 * SW_DH], ps[:, SA, SW_GQ + SW_DH:SW_COLS],
                              vp_hi[:, t % 4, SW_DH:2 * SW_DH].bitcast(F32), ALU.subtract).then_inc(sw_vlo, 1)
            dve.wait_ge(sw_sq, i + 1)
            dve.tensor_reduce(hss[:], qkn, axis=AX.X, op=ALU.add).then_inc(sw_var, 1)
            dve.wait_ge(sw_var, 2 * i + 1)
            dve.tensor_scalar(hvar[:], hss[:], 1.0 / SW_DH, EPS, ALU.mult, ALU.add).then_inc(sw_var, 1)
            dve.wait_ge(sw_var, 2 * i + 2)
            rsqrt(dve, sw_rsq, RSQ * i, hvar[:], hrs[:], htmp[:])
            dve.tensor_tensor(qkn, ps[:, SA, 0:SW_NH * SW_DH].rearrange("p (a d) -> p a d", d=SW_DH),
                              hrs[:].unsqueeze(2).to_broadcast([P, SW_NH, SW_DH]), ALU.mult).then_inc(sw_norm, 1)
            dve.wait_ge(sw_norm, 2 * i + 1)
            dve.tensor_tensor(qkn, qkn, qkgain[:], ALU.mult).then_inc(sw_norm, 1)
            dve.wait_ge(sw_norm, 2 * i + 2)
            h = SW_DH // 2
            x1, x2 = qkn[:, :, 0:h], qkn[:, :, h:SW_DH]
            cos = coss[:, t:t + 1, :].to_broadcast([P, SW_NH, h])
            sin = sins[:, t:t + 1, :].to_broadcast([P, SW_NH, h])
            wait(dve, b_mm, i)
            wait(dve, sw_radd, 4 * i)
            q4 = qr.rearrange("p (a d) -> p a d", d=SW_DH)
            nq = SW_NH - 1
            dve.tensor_tensor(rope_s[:, :, 0:h], x2, sin, ALU.mult).then_inc(sw_rmul, 1)
            dve.tensor_tensor(rope_s[:, :, h:SW_DH], x1, sin, ALU.mult).then_inc(sw_rmul, 1)
            cos2 = coss[:, t:t + 1, :]
            dve.tensor_tensor(q4[:, :, 0:h], x1[:, 0:nq, :], cos[:, 0:nq, :], ALU.mult)
            dve.tensor_tensor(q4[:, :, h:SW_DH], x2[:, 0:nq, :], cos[:, 0:nq, :], ALU.mult).then_inc(sw_rmul, 1)
            dve.tensor_tensor(kr[:, 1:2, 0:h], x1[:, nq:SW_NH, :], cos2, ALU.mult)
            dve.tensor_tensor(kr[:, 1:2, h:SW_DH], x2[:, nq:SW_NH, :], cos2, ALU.mult).then_inc(sw_rmul, 1)

        def rope_sw_pool(pool, g, t):
            i = TT * g + t
            h = SW_DH // 2
            nq = SW_NH - 1
            q4 = qr.rearrange("p (a d) -> p a d", d=SW_DH)
            pool.wait_ge(sw_rmul, 4 * i + 3)
            pool.tensor_tensor(q4[:, :, 0:h], q4[:, :, 0:h], rope_s[:, 0:nq, 0:h], ALU.subtract).then_inc(sw_radd, 1)
            pool.tensor_tensor(q4[:, :, h:SW_DH], q4[:, :, h:SW_DH], rope_s[:, 0:nq, h:SW_DH], ALU.add).then_inc(sw_radd, 1)
            pool.wait_ge(sw_rmul, 4 * i + 4)
            pool.tensor_tensor(kr[:, 1:2, 0:h], kr[:, 1:2, 0:h], rope_s[:, nq:SW_NH, 0:h], ALU.subtract).then_inc(sw_radd, 1)
            pool.tensor_tensor(kr[:, 1:2, h:SW_DH], kr[:, 1:2, h:SW_DH], rope_s[:, nq:SW_NH, h:SW_DH], ALU.add).then_inc(sw_radd, 1)

        def prob_pool(pool, g, t):
            i = TT * g + t
            pool.wait_ge(sw_den, 2 * (i + 1))
            pool.tensor_tensor(prob.rearrange("p h s n -> p h (s n)"), prob.rearrange("p h s n -> p h (s n)"),
                               rden[:].unsqueeze(2).to_broadcast([P, 4, 2 * P]), ALU.mult).then_inc(sw_prob, 1)

        def oT_dve(dve, g, t):
            i = TT * g + t
            dve.wait_ge(sw_ohi, i + 1)
            dve.tensor_tensor(aT_lo[0][:, :, t * P:(t + 1) * P], ps[:, SO, 0:2 * P].rearrange("p (j n) -> p j n", n=P),
                              aT_hi[0][:, :, t * P:(t + 1) * P].bitcast(F32), ALU.subtract).then_inc(sw_olo, 1)

        def sw_steps(which, eng):
            def item(g, s, lag):
                if s - lag >= 0:
                    return (g, s - lag)
                if isinstance(g, int) and g == 0:
                    return None
                return (g - 1, s - lag + TT)

            def run(f, g, s, lag):
                it = item(g, s, lag)
                if it and (s - lag < TT):
                    f(eng, *it)

            def step(g, s, last_group):
                if which == "pe":
                    run(a_pe, g, s, 0)
                    run(b_pe, g, s, 1)
                    run(d_pe, g, s, 2)
                    run(c_pe, g, s, 1)
                    run(e_pe, g, s, 2)
                    run(f_pe, g, s, 3)
                if which == "act":
                    run(sq_act, g, s, 0)
                    run(qkT_act, g, s, 1)
                    run(pT_act, g, s, 2)
                    run(exp_act, g, s, 1)
                    run(oT_act, g, s, 2)
                    if s == 2:
                        eng.wait_ge(down_mm, 16 * (DG_SW + g))
                        for j in range(4, 8):
                            sw_split_hi(eng, g, j)
                    if s == TT - 1 and not last_group:
                        eng.wait_ge(a_mm, TT * (g + 1))
                        for j in range(4):
                            sw_split_hi(eng, g + 1, j)
                if which == "dve":
                    run(qkT_dve, g, s, 1)
                    run(pT_dve, g, s, 2)
                    run(mask_dve, g, s, 1)
                    run(norm_dve, g, s, 0)
                    run(oT_dve, g, s, 2)
                    run(den_dve, g, s, 1)
                    it = item(g, s, 3)
                    if it and s - 3 < TT:
                        add_tile(eng, DG_SW + it[0], it[1], BDS)
                    if s == 2:
                        for j in range(4, 8):
                            sw_split_lo(eng, g, j)
                    if s == TT - 1 and not last_group:
                        for j in range(4):
                            sw_split_lo(eng, g + 1, j)
                if which == "pool":
                    run(rope_sw_pool, g, s, 0)
                    run(prob_pool, g, s, 1)
            def group(g, last_group):
                for s in range(TT):
                    step(g, s, last_group)
            group(0, False)
            with eng.Fori(1, SW_KV - 1) as g:
                group(g, False)
            group(SW_KV - 1, True)
            for s in range(TT, TT + 3):
                step(SW_KV - 1, s, True)

        def table(dve, base, angle, turn, work, quarter):
            steps = (
                lambda: dve.tensor_scalar(work, angle, 1.0 / TWO_PI, quarter, ALU.mult, ALU.add),
                lambda: dve.tensor_scalar(work, work, ROUND, ROUND, ALU.add, ALU.subtract),
                lambda: dve.scalar_tensor_tensor(turn, work, -C1, angle, ALU.mult, ALU.add),
                lambda: dve.scalar_tensor_tensor(turn, work, -C2, turn, ALU.mult, ALU.add),
                lambda: dve.scalar_tensor_tensor(turn, work, -C3, turn, ALU.mult, ALU.add),
                lambda: dve.tensor_scalar(turn, turn, quarter * TWO_PI, PI_IN, ALU.add, ALU.min),
                lambda: dve.tensor_scalar(turn, turn, -PI_IN, None, ALU.max),
            )
            for n, step in enumerate(steps):
                dve.wait_ge(tab, base + n)
                step().then_inc(tab, 1)

        @block.sync
        def _(sp):
            sp.dma_start(x[:, 0, :], x_in[0, 0:P, :]).then_inc(x_in_s, 16)
            load_gain(sp, 0, norm_mix[0])
            sp.dma_start(pos_i, positions[0].partition_broadcast(P)).then_inc(pos_in, 16)
            for dst, src in ((ident[:], c_ident), (causal[:], c_causal), (headc[:], c_head), (freq[:], c_freq)):
                sp.dma_start(dst, src).then_inc(const_in, 16)
            for t in range(1, TT):
                sp.dma_start(x[:, t, :], x_in[0, t * P:(t + 1) * P, :]).then_inc(x_in_s, 16)
            qk_sp(sp, 0)
            load_gain(sp, 1, norm_mlp[0])
            head_sp(sp, 0, False)
            with sp.Fori(1, HEADS - 1) as h:
                yT_sp(sp, h - 1, NCH - 1)
                head_sp(sp, h, False)
            yT_sp(sp, HEADS - 2, NCH - 1)
            head_sp(sp, HEADS - 1, True)
            sp.wait_ge(v_mm, NCH * HEADS)
            for t in range(TT):
                sp.dma_start(x[:, t, :], x_in[0, t * P:(t + 1) * P, :]).then_inc(x_in_s, 16)
            yT_sp(sp, HEADS - 1, NCH - 1)
            sp.wait_ge(yT_out, 16 * NCH * HEADS)
            with sp.Fori(0, RET_GROUPS) as g:
                out_sp(sp, g)
            mlp_sp_all(sp, 0, PC_M0)
            load_gain(sp, 2, norm_mix[1])
            sp.wait_ge(a_lo_s, 4 * MLP_GROUPS)
            for a in range(SW_NH - 1):
                sp.dma_start(qkgain[:, a, :], q_gain[0].partition_broadcast(P)).then_inc(sw_const, 16)
            sp.dma_start(qkgain[:, SW_NH - 1, :], k_gain[0].partition_broadcast(P)).then_inc(sw_const, 16)
            sp.dma_start(sink_b[:], sinks[0].partition_broadcast(P)).then_inc(sw_const, 16)
            sp.dma_start(pos_si[:], positions[0].rearrange("(t p) -> p t", p=P),
                         allow_slow_non_contiguous=True).then_inc(sw_const, 16)
            sp.dma_start(freq_row[:], c_freq_row).then_inc(sw_const, 16)
            sp.dma_start(swmask[:], c_mask).then_inc(sw_const, 16)
            sw_sp_in(sp, 0)
            with sp.Fori(0, SW_KV - 1) as g:
                sw_sp_out(sp, g)
                sw_sp_in(sp, g + 1)
            sw_sp_out(sp, SW_KV - 1)
            load_gain(sp, 3, norm_mlp[1])
            mlp_sp_all(sp, 1, PC_M1)
            for t in range(TT):
                sp.wait_ge(x_add, 16 * (DG_M1 + MLP_LAST) + 2 * t + 2)
                sp.dma_start(out[0, t * P:(t + 1) * P, :], x[:, t, :]).then_inc(stored, 16)
            sp.wait_ge(stored, 16 * TT)

        @block.scalar
        def _(act):
            act.wait_ge(tab, 9)
            act.activation(sinr[:], turns, ACT.Sin).then_inc(tab_act, 1)
            act.wait_ge(tab, 16)
            act.activation(cosr[:], turns, ACT.Sin).then_inc(tab_act, 1)
            act.wait_ge(x_in_s, 16 * TT)
            for t in range(TT):
                norm_act_x(act, 0, t)
                if t >= 1:
                    norm_act_hi(act, 0, t - 1)
            norm_act_hi(act, 0, TT - 1)
            qk_hi_act(act, 0)
            head_act(act, 0, True, False)
            with act.Fori(1, HEADS - 1) as h:
                head_act(act, h, False, False)
            head_act(act, HEADS - 1, False, True)
            yT_act(act, HEADS - 1, NCH - 1)
            for g in range(2):
                out_act(act, g, g)
            with act.Fori(1, RET_GROUPS // 2) as gg:
                for b in range(2):
                    out_act(act, 2 * gg + b, b)
            mlp_up_hi(act, 0, PC_M0)
            norm_after(act, 1, RET_GROUPS - 1)
            mlp_act_all(act, 0, DG_M0, PC_M0)
            act.wait_ge(a_lo_s, 4 * MLP_GROUPS)
            for j in range(4):
                sw_split_hi(act, 0, j)
            norm_after(act, 2, DG_SW - 1)
            act.wait_ge(tab, 25)
            act.activation(sins[:], turn_s, ACT.Sin).then_inc(tab_act, 1)
            act.wait_ge(tab, 32)
            act.activation(coss[:], turn_s, ACT.Sin).then_inc(tab_act, 1)
            act.wait_ge(tab_act, 4)
            act.wait_ge(sw_zero, 5)
            sw_steps("act", act)
            act.wait_ge(down_mm, 16 * DG_M1)
            act.wait_ge(x_add, 16 * DG_M1)
            mlp_up_hi(act, 0, PC_M1)
            norm_after(act, 3, DG_M1 - 1)
            mlp_act_all(act, MLP_GROUPS, DG_M1, PC_M1)

        @block.vector
        def _(dve):
            dve.wait_ge(pos_in, 16)
            dve.wait_ge(const_in, 64)
            dve.tensor_copy(posf, pos_i).then_inc(tab, 1)
            dve.wait_ge(tab, 1)
            dve.tensor_scalar(ang, posf, freq[:], None, ALU.mult).then_inc(tab, 1)
            table(dve, 2, ang, turns, posf, 0.0)
            dve.wait_ge(tab_act, 1)
            table(dve, 9, ang, turns, posf, 0.25)
            for t in range(TT + 2):
                norm_dve_step(dve, 0, t)
            qk_lo_dve(dve, 0)
            dve.wait_ge(tab_act, 2)
            head_dve(dve, 0, False)
            with dve.Fori(1, HEADS - 1) as h:
                head_dve(dve, h, False)
            head_dve(dve, HEADS - 1, True)
            for j in range(4):
                out_lo(dve, 0, 0, j)
            dve.wait_ge(x_in_s, 32 * TT)

            def lo_of(g, b):
                def lo(t):
                    if t % 2 == 0:
                        out_lo(dve, g, b, t // 2)
                return lo

            out_dve(dve, 0, 0, lo_of(1, 1))
            with dve.Fori(0, RET_GROUPS // 2 - 1) as gg:
                out_dve(dve, 2 * gg + 1, 1, lo_of(2 * gg + 2, 0))
                out_dve(dve, 2 * gg + 2, 0, lo_of(2 * gg + 3, 1))
            out_dve(dve, RET_GROUPS - 1, 1, lambda t: mlp_up_lo(dve, 0, PC_M0) if t == 1 else None,
                    lambda t: norm_dve_step(dve, 1, t))
            norm_dve_step(dve, 1, TT)
            norm_dve_step(dve, 1, TT + 1)

            def sw_first_lo():
                for j in range(4):
                    sw_split_lo(dve, 0, j)

            mlp_dve_all(dve, 0, DG_M0, PC_M0, 2, sw_first_lo)
            dve.wait_ge(sw_const, 16 * (SW_NH + 4))
            dve.tensor_copy(pos_sf[:], pos_si[:]).then_inc(tab, 1)
            dve.wait_ge(tab, 17)
            dve.tensor_tensor(ang_s, pos_sf[:].unsqueeze(2).to_broadcast([P, TT, 32]),
                              freq_row[:].unsqueeze(1).to_broadcast([P, TT, 32]), ALU.mult).then_inc(tab, 1)
            work_s = qr.rearrange("p (t f) -> p t f", f=32)
            table(dve, 18, ang_s, turn_s, work_s, 0.0)
            dve.wait_ge(tab_act, 3)
            table(dve, 25, ang_s, turn_s, work_s, 0.25)
            dve.wait_ge(tab_act, 4)
            dve.wait_ge(sw_zero, 5)
            sw_steps("dve", dve)
            mlp_up_lo(dve, 0, PC_M1)
            for t in range(TT + 2):
                norm_dve_step(dve, 3, t)
            mlp_dve_all(dve, MLP_GROUPS, DG_M1, PC_M1, None, lambda: None)

        @block.gpsimd
        def _(pool):
            for t in range(TT):
                norm_pool(pool, 0, t)
            head_pool(pool, 0)
            with pool.Fori(1, HEADS) as h:
                head_pool(pool, h)
            for t in range(TT):
                norm_pool(pool, 1, t)
            mlp_pool_all(pool, 0)
            pool.wait_ge(a_lo_s, 4 * MLP_GROUPS)
            for z in (kr, kT_hi, kT_lo, vp_hi, vp_lo):
                flat = z[:].rearrange("p a b c -> p (a b c)") if len(z.shape) == 4 else z[:].rearrange("p a b -> p (a b)")
                pool.memset(flat if z is kr else flat.bitcast(F32), 0.0).then_inc(sw_zero, 1)
            for t in range(TT):
                norm_pool(pool, 2, t)
            sw_steps("pool", pool)
            for t in range(TT):
                norm_pool(pool, 3, t)
            mlp_pool_all(pool, MLP_GROUPS)

        @block.tensor
        def _(pe):
            pe.wait_ge(const_in, 64)
            for t in range(TT):
                norm_pe(pe, 0, t)
            hT_ready(pe, 0, TT - 1)
            head_pe(pe, 0, True)
            with pe.Fori(1, HEADS) as h:
                head_pe(pe, h, False)
            y_transpose(pe, HEADS - 1, NCH - 1)
            out_pe(pe, 0, 0)
            with pe.Fori(0, RET_GROUPS // 2 - 1) as gg:
                out_pe(pe, 2 * gg + 1, 1)
                out_pe(pe, 2 * gg + 2, 0)

            def tile(t):
                if t >= 2:
                    norm_pe(pe, 1, t - 2)
            out_pe(pe, RET_GROUPS - 1, 1, tile)
            norm_pe(pe, 1, TT - 2)
            norm_pe(pe, 1, TT - 1)
            mlp_pe_all(pe, 0, DG_M0, PC_M0, 1, 2)
            sw_steps("pe", pe)
            pe.wait_ge(x_add, 16 * DG_M1)
            for t in range(TT):
                norm_pe(pe, 3, t)
            mlp_pe_all(pe, MLP_GROUPS, DG_M1, PC_M1, 3, None)


_INS = ["x", "positions", "norm_mix", "norm_mlp", "w_up", "w_down", "ret_w_in", "ret_w_out", "swa_w_in",
        "swa_q_gain", "swa_k_gain", "swa_sinks", "swa_w_out"]


def _constants():
    import numpy as np
    i = np.arange(P)
    causal = (i[:, None] <= i[None, :]).astype(np.float32)
    cur = np.where(i[None, :] <= i[:, None], 0.0, NEG)
    prev = np.where(i[None, :] > i[:, None], 0.0, NEG)
    mask = np.stack([cur, prev, cur, np.full((P, P), NEG)], axis=1).astype(np.float32)
    head = np.zeros((P, HEADS, 4), np.float32)
    for h in range(HEADS):
        log_gamma = math.log1p(-(2.0 ** (-5.0 - h)))
        head[:, h, 0] = np.exp(-log_gamma * (i + 1)) * DK ** -0.5
        head[:, h, 1] = np.exp(log_gamma * (i + 1))
        head[:, h, 2] = np.exp(2 * log_gamma * (i + 1))
        head[:, h, 3] = np.exp(log_gamma * CH)
    freq = lambda d: np.float32(THETA) ** (-np.arange(0, d, 2, dtype=np.float32) / np.float32(d))
    return {"c_ident": np.eye(P, dtype=np.float32), "c_causal": causal, "c_mask": mask, "c_head": head,
            "c_freq": freq(DK).astype(np.float32).reshape(P, 1),
            "c_freq_row": np.ascontiguousarray(np.broadcast_to(freq(SW_DH).astype(np.float32), (P, 32)))}


def kernel(**inputs):
    import numpy as np
    from concourse import bacc
    from concourse.bass_utils import run_bass_kernel_spmd

    nc = bacc.Bacc("TRN2", target_bir_lowering=False, num_devices=1)
    arrays, args = {}, []
    for name in _INS:
        arrays[f"in_{name}"] = np.ascontiguousarray(inputs[name])
    arrays.update(_constants())
    for name, a in arrays.items():
        args.append(nc.dram_tensor(name, a.shape, mybir.dt.from_np(a.dtype), kind="ExternalInput").ap())
    out = nc.dram_tensor("out", (1, S, D), F32, kind="ExternalOutput").ap()
    y_dram = nc.dram_tensor("y_dram", (HEADS * DV, S), F32, kind="Internal").ap()
    trunk(nc, *args, out, y_dram)
    r = run_bass_kernel_spmd(nc, [arrays], core_ids=[0])
    return r.results[0]["out"]
```

```python
import math
from contextlib import ExitStack

import concourse.bass as bass
from concourse import mybir

F32 = mybir.dt.float32
F32R = mybir.dt.float32r
I32 = mybir.dt.int32
ALU = mybir.AluOpType
ACT = mybir.ActivationFunctionType
AX = mybir.AxisListType

P = 128
D = 1024
S = 1024
KT = D // P
TT = S // P
HALF = 512
EPS = 1e-6
D_FF = 4 * D
PIECE = 1024
RING = 4

HEADS = 4
DK = D // HEADS
DV = 2 * DK
CH = P
NCH = S // CH

SW_HEADS = 16
SW_KV = 4
SW_DH = 64
SW_GQ = (SW_HEADS // SW_KV) * SW_DH
SW_COLS = SW_GQ + 2 * SW_DH
SW_NH = SW_GQ // SW_DH + 1
THETA = 10000.0

RET_GROUPS = HEADS * DV // 256
MLP_GROUPS = D_FF // 256
RET_PIECES = 12
SW_PIECES = 8
PC_OUT = RET_PIECES * HEADS
PC_M0 = PC_OUT + 4 * RET_GROUPS
PC_SW = PC_M0 + 4 * MLP_GROUPS
PC_M1 = PC_SW + SW_PIECES * SW_KV
DG_M0 = RET_GROUPS
DG_SW = DG_M0 + MLP_GROUPS
DG_M1 = DG_SW + SW_KV
RSQ = 9

TWO_PI = 2.0 * math.pi
C1 = 6.28125
C2 = 1.93500518798828125e-3
C3 = TWO_PI - C1 - C2
PI_IN = 3.1415925
NEG = -1e30
NU = TT + 3
ROUND = 12582912.0


def wait(eng, sem, value):
    if isinstance(value, int) and value <= 0:
        return
    eng.wait_ge(sem, value)


def trunk(nc, x_in, positions, norm_mix, norm_mlp, w_up, w_down, ret_in, ret_out, sw_in, q_gain,
          k_gain, sinks, sw_out, c_ident, c_causal, c_mask, c_head, c_freq, c_freq_row, out, y_dram):
    ctx = ExitStack()
    with ctx:
        def sb(name, shape, dt=F32, stack=ctx):
            return stack.enter_context(nc.sbuf_tensor(name, shape, dt))

        def sem(name):
            return ctx.enter_context(nc.semaphore(name))

        ident = sb("ident", [P, P])
        causal = sb("causal", [P, P])
        headc = sb("headc", [P, HEADS, 4])
        hc = sb("hc", [P, 4])
        freq = sb("freq", [P, 1])
        gain_b = sb("gain_b", [P, D])
        raw = sb("raw", [P, RING, PIECE])
        xn = sb("xn", [P, 2, D])
        ss = sb("ss", [P, TT])
        var = sb("var", [P, TT])
        rstd = sb("rstd", [P, TT])
        rtmp = sb("rtmp", [P, TT])
        hT_hi = sb("hT_hi", [P, KT, S], F32R)
        hT_lo = sb("hT_lo", [P, KT, S], F32R)

        with ExitStack() as place:
            x = sb("x", [P, TT, D], F32, place)
        with ExitStack() as ret:
            wv_hi = sb("wv_hi", [P, 4, PIECE], F32R, ret)
            wv_lo = sb("wv_lo", [P, 4, PIECE], F32R, ret)
            wqg_hi = sb("wqg_hi", [P, 4, PIECE], F32R, ret)
            wqg_lo = sb("wqg_lo", [P, 4, PIECE], F32R, ret)
            kq = sb("kq", [P, 4, S], F32, ret)
            cosr = sb("cosr", [P, S], F32, ret)
            sinr = sb("sinr", [P, S], F32, ret)
            rope_t = sb("rope_t", [P, HALF], F32, ret)
            q_hi = sb("q_hi", [P, 2, CH], F32R, ret)
            q_lo = sb("q_lo", [P, 2, CH], F32R, ret)
            k_hi = sb("k_hi", [P, DK], F32R, ret)
            k_lo = sb("k_lo", [P, DK], F32R, ret)
            v_hi = sb("v_hi", [P, DV], F32R, ret)
            v_lo = sb("v_lo", [P, DV], F32R, ret)
            sc = sb("sc", [P, CH], F32, ret)
            sc_hi = sb("sc_hi", [P, CH], F32R, ret)
            sc_lo = sb("sc_lo", [P, CH], F32R, ret)
            state = sb("state", [P, 2, DV], F32, ret)
            st_hi = sb("st_hi", [P, 2, DV], F32R, ret)
            st_lo = sb("st_lo", [P, 2, DV], F32R, ret)
            sgate = sb("sgate", [P, DV], F32, ret)
            bn = sb("bn", [P, 6], F32, ret)
            mv = sb("mv", [P, 2], F32, ret)
            gvar = sb("gvar", [P, 1], F32, ret)
            grs = sb("grs", [P, 1], F32, ret)
            gtmp = sb("gtmp", [P, 1], F32, ret)
            gscale = sb("gscale", [P, 1], F32, ret)
            gbias = sb("gbias", [P, 1], F32, ret)
        yn, y, yT, rope_u = xn[:, 0, 0:DV], xn[:, 0, DV:D], xn[:, 1, 0:DV], xn[:, 1, DV:D]
        posf = kq[:, 0, :]
        turns = kq[:, 1, :]
        pos_i = kq[:, 2, :].bitcast(I32)
        ang = kq[:, 3, :]

        with ExitStack() as later:
            sb("x_place", [P, TT, D], F32, later)
            aT_hi = [sb("aT_hi0", [P, 2, S], F32R, later)]
            aT_lo = [sb("aT_lo0", [P, 2, S], F32R, later)]
            wd_hi = [sb("wd_hi0", [P, 2, D], F32R, later)]
            wd_lo = [sb("wd_lo0", [P, 2, D], F32R, later)]
            with ExitStack() as o:
                aT_hi.append(sb("aT_hi1", [P, 2, S], F32R, o))
                aT_lo.append(sb("aT_lo1", [P, 2, S], F32R, o))
                wd_hi.append(sb("wd_hi1", [P, 2, D], F32R, o))
                wd_lo.append(sb("wd_lo1", [P, 2, D], F32R, o))
                wu_hi = sb("wu_hi", [P, KT, 256], F32R, o)
                wu_lo = sb("wu_lo", [P, KT, 256], F32R, o)
            with ExitStack() as m:
                relu_t = sb("relu_t", [P, 2, HALF], F32, m)
                sqr_t = sb("sqr_t", [P, 2, HALF], F32, m)
                squares = sb("squares", [P, D], F32, m)
            with ExitStack() as s:
                ws_hi = sb("ws_hi", [P, KT, SW_COLS], F32R, s)
                ws_lo = sb("ws_lo", [P, KT, SW_COLS], F32R, s)
                kr = sb("kr", [P, 3, SW_DH], F32, s)
                qT_hi = sb("qT_hi", [P, 2, P], F32R, s)
                qT_lo = sb("qT_lo", [P, 2, P], F32R, s)
                kT_hi = sb("kT_hi", [P, 2, 2, P], F32R, s)
                kT_lo = sb("kT_lo", [P, 2, 2, P], F32R, s)
                vp_hi = sb("vp_hi", [P, 9 * SW_DH], F32R, s)
                vp_lo = sb("vp_lo", [P, 9 * SW_DH], F32R, s)
                pT_hi = sb("pT_hi", [P, 2, 4, P], F32R, s)
                pT_lo = sb("pT_lo", [P, 2, 4, P], F32R, s)
                coss = sb("coss", [P, TT, 32], F32, s)
                sins = sb("sins", [P, TT, 32], F32, s)
                qkgain = sb("qkgain", [P, SW_NH, SW_DH], F32, s)
                sink_b = sb("sink_b", [P, SW_HEADS], F32, s)
                swmask = sb("swmask", [P, 4, P], F32, s)
                pos_si = sb("pos_si", [P, TT], I32, s)
                pos_sf = sb("pos_sf", [P, TT], F32, s)
                freq_row = sb("freq_row", [P, 32], F32, s)
                hss = sb("hss", [P, SW_NH], F32, s)
                hvar = sb("hvar", [P, SW_NH], F32, s)
                hrs = sb("hrs", [P, SW_NH], F32, s)
                htmp = sb("htmp", [P, SW_NH], F32, s)
                smax = sb("smax", [P, 4], F32, s)
                nmax = sb("nmax", [P, 4], F32, s)
                sdif = sb("sdif", [P, 4], F32, s)
                ssum = sb("ssum", [P, 4], F32, s)
                esink = sb("esink", [P, 4], F32, s)
                den = sb("den", [P, 4], F32, s)
                rden = sb("rden", [P, 4], F32, s)
                qk_raw = sb("qk_raw", [P, SW_NH, SW_DH], F32, s)
        prob = xn[:, 0, :].rearrange("p (h s n) -> p h s n", s=2, n=P)
        nqk = SW_NH * SW_DH
        qkn = xn[:, 1, 0:nqk].rearrange("p (a d) -> p a d", d=SW_DH)
        rope_s = xn[:, 1, nqk:2 * nqk].rearrange("p (a d) -> p a d", d=SW_DH)
        qr = xn[:, 1, 2 * nqk:2 * nqk + SW_GQ]
        work_s = qk_raw[:, 0:4, :].rearrange("p a d -> p (a d)").rearrange("p (t f) -> p t f", f=32)

        ps = ctx.enter_context(nc.psum_tensor("ps", [P, 8, HALF], F32))
        BT = ((6, 7), (6, 7), (6, 7), (2, 3))
        BU = (4, 5)
        BD = (0, 1, 2, 3)
        BV, BG, BK, BSC, BO, BST, BY = 0, 1, 2, 3, 4, 5, 7
        SA, SB, SS, SP_, SO = 0, 1, 2, 4, 6
        BDS = (7, 1)

        raw_in = [sem(f"raw_in{i}") for i in range(RING)]
        const_in = sem("const_in")
        passed = {"SP": sem("sp_passed"), "DVE": sem("dve_passed")}
        gain_in = sem("gain_in")
        pos_in = sem("pos_in")
        x_in_s = [sem(f"x_in{t}") for t in range(TT)]
        w_hi = sem("w_hi")
        w_lo = sem("w_lo")
        n_sq = sem("n_sq")
        n_var = sem("n_var")
        n_rsq = sem("n_rsq")
        n_gained = sem("n_gained")
        n_scaled = sem("n_scaled")
        n_tr = sem("n_tr")
        n_hi = sem("n_hi")
        n_lo = sem("n_lo")
        tab = sem("tab")
        tab_act = sem("tab_act")
        hc_set = sem("hc_set")
        qk_mm = sem("qk_mm")
        rope_mul = sem("rope_mul")
        rope_add = sem("rope_add")
        v_mm = sem("v_mm")
        g_mm = sem("g_mm")
        kt_mm = sem("kt_mm")
        sc_mm = sem("sc_mm")
        o_mm = sem("o_mm")
        upd_mm = sem("upd_mm")
        yt_mm = sem("yt_mm")
        v_hi_s = sem("v_hi_s")
        v_lo_s = sem("v_lo_s")
        silu_s = sem("silu_s")
        q_hi_s = sem("q_hi_s")
        q_lo_s = sem("q_lo_s")
        k_hi_s = sem("k_hi_s")
        k_lo_s = sem("k_lo_s")
        sc_masked = sem("sc_masked")
        sc_hi_s = sem("sc_hi_s")
        sc_lo_s = sem("sc_lo_s")
        stats = sem("stats")
        g_rsq = sem("g_rsq")
        g_scale = sem("g_scale")
        st_upd = sem("st_upd")
        st_hi_s = sem("st_hi_s")
        st_lo_s = sem("st_lo_s")
        yn_s = sem("yn_s")
        y_s = sem("y_s")
        yT_s = sem("yT_s")
        yT_out = sem("yT_out")
        down_mm = sem("down_mm")
        x_add = sem("x_add")
        up_mm = sem("up_mm")
        relu_s = sem("relu_s")
        sqr_s = sem("sqr_s")
        a_hi_s = sem("a_hi_s")
        a_lo_s = sem("a_lo_s")
        sw_const = sem("sw_const")
        sw_zero = sem("sw_zero")
        a_mm = sem("a_mm")
        sw_sq = sem("sw_sq")
        sw_raw = sem("sw_raw")
        sw_vhi = sem("sw_vhi")
        sw_vlo = sem("sw_vlo")
        sw_var = sem("sw_var")
        sw_rsq = sem("sw_rsq")
        sw_norm = sem("sw_norm")
        sw_gain = sem("sw_gain")
        sw_rcos = sem("sw_rcos")
        sw_rsin = sem("sw_rsin")
        sw_radd = sem("sw_radd")
        b_mm = sem("b_mm")
        sw_qhi = sem("sw_qhi")
        sw_qlo = sem("sw_qlo")
        c_mm = sem("c_mm")
        sw_masked = sem("sw_masked")
        sw_max = sem("sw_max")
        sw_exp = sem("sw_exp")
        sw_den = sem("sw_den")
        sw_prob = sem("sw_prob")
        d_mm = sem("d_mm")
        sw_phi = sem("sw_phi")
        sw_plo = sem("sw_plo")
        e_mm = sem("e_mm")
        sw_ohi = sem("sw_ohi")
        sw_olo = sem("sw_olo")
        stored = sem("stored")

        block = ctx.enter_context(nc.Block())

        def apart(eng):
            eng.sem_inc(passed[eng.engine.name], 1)

        def arrived(eng, m0, i, per, j, dmas=1):
            eng.wait_ge(raw_in[j % RING], 16 * (m0 // RING + j // RING + 1) + 16 * (per // RING) * i)

        def load_piece(sp, m0, i, per, j, src, fold):
            wait(sp, w_lo, m0 + per * i + j - RING + 1)
            apart(sp)
            dst = raw[:, j % RING, :]
            sp.dma_start(dst.rearrange("p (k n) -> p k n", n=fold), src).then_inc(raw_in[j % RING], 16)

        def split_hi(act, m0, i, per, j, dst, shape=None):
            arrived(act, m0, i, per, j)
            src = raw[:, j % RING, :]
            if shape:
                src = src.rearrange("p (k n) -> p k n", n=shape)
            act.activation(dst, src, ACT.Copy).then_inc(w_hi, 1)

        def split_lo(dve, m0, i, per, j, dst, hi, shape=None):
            dve.wait_ge(w_hi, m0 + per * i + j + 1)
            src = raw[:, j % RING, :]
            if shape:
                src = src.rearrange("p (k n) -> p k n", n=shape)
            dve.tensor_tensor(dst, src, hi.bitcast(F32), ALU.subtract).then_inc(w_lo, 1)

        def rsqrt(dve, count, base, a, r, t, meanwhile=()):
            todo = list(meanwhile)
            each = -(-len(todo) // (RSQ - 1)) if todo else 0

            def step(k, ins):
                ins.then_inc(count, 1)
                for work in todo[each * k:each * (k + 1)]:
                    work()
                dve.wait_ge(count, base + k + 1)

            step(0, dve.tensor_scalar(r.bitcast(I32), a.bitcast(I32), 1, None, ALU.logical_shift_right))
            step(1, dve.tensor_scalar(r.bitcast(I32), r.bitcast(I32), -1.0, float(0x5F3759DF), ALU.mult, ALU.add))
            step(2, dve.scalar_tensor_tensor(t, r, -0.5, r, ALU.mult, ALU.mult))
            step(3, dve.tensor_tensor(t, t, a, ALU.mult))
            step(4, dve.scalar_tensor_tensor(r, t, 1.5, r, ALU.add, ALU.mult))
            c = math.sqrt(3 / 8)
            step(5, dve.scalar_tensor_tensor(t, r, c, r, ALU.mult, ALU.mult))
            step(6, dve.tensor_tensor(t, t, a, ALU.mult))
            step(7, dve.scalar_tensor_tensor(t, t, -10 / 8 / c, t, ALU.add, ALU.mult))
            step(8, dve.scalar_tensor_tensor(r, t, 15 / 8, r, ALU.add, ALU.mult))

        def product(pe, bank, pairs):
            last = None
            for i, (ah, al, bh, bl) in enumerate(pairs):
                pe.matmul(bank, ah, bh, start=(i == 0), stop=False)
                pe.matmul(bank, ah, bl, start=False, stop=False)
                last = pe.matmul(bank, al, bh, start=False, stop=(i == len(pairs) - 1))
            return last

        def xslot(n, t):
            if n < 3:
                return xn[:, t % 2, :]
            return (relu_t, sqr_t)[t % 2][:].rearrange("p a b -> p (a b)")

        def norm_act(act, n, u, x_ready):
            if u < TT:
                k = TT * n + u
                x_ready(u)
                wait(act, n_sq, k)
                to = ps[:, 4:6, :] if n < 3 else squares[:].rearrange("p (a b) -> p a b", b=HALF)
                act.activation(to, x[:, u, :].rearrange("p (a b) -> p a b", b=HALF), ACT.Square,
                               accum_out=ss[:, u:u + 1]).then_inc(n_sq, 1)
            if 3 <= u:
                t = u - 3
                for q in range(2):
                    act.wait_ge(n_tr, 2 * (TT * n + t) + q + 1)
                    act.activation(hT_hi[:, 4 * q:4 * q + 4, t * P:(t + 1) * P],
                                   ps[:, BT[n][q], :].rearrange("p (k n) -> p k n", n=P), ACT.Copy).then_inc(n_hi, 1)
            if 1 <= u <= TT:
                k = TT * n + u - 1
                act.wait_ge(n_rsq, RSQ * (k // 2 + 1))
                act.wait_ge(n_gained, k + 1)
                act.activation(xslot(n, u - 1), xslot(n, u - 1), ACT.Copy, scale=rstd[:, u - 1:u]).then_inc(n_scaled, 1)

        def norm_dve_lo(dve, n, t, q):
            dve.wait_ge(n_hi, 2 * (TT * n + t) + q + 1)
            dve.tensor_tensor(hT_lo[:, 4 * q:4 * q + 4, t * P:(t + 1) * P],
                              ps[:, BT[n][q], :].rearrange("p (k n) -> p k n", n=P),
                              hT_hi[:, 4 * q:4 * q + 4, t * P:(t + 1) * P].bitcast(F32),
                              ALU.subtract).then_inc(n_lo, 1)

        def norm_dve(dve, n, u, behind=()):
            lows = [lambda q=q: norm_dve_lo(dve, n, u - 3, q) for q in range(2)] if u >= 3 else []
            if u < TT and u % 2:
                k = TT * n + u
                pair = slice(u - 1, u + 1)
                dve.wait_ge(n_sq, k + 1)
                dve.tensor_scalar(var[:, pair], ss[:, pair], 1.0 / D, EPS, ALU.mult, ALU.add).then_inc(n_var, 1)
                dve.wait_ge(n_var, k // 2 + 1)
                work = [lambda: None] * (RSQ - 1)
                work[2:2 + 2 * len(lows):2] = lows
                rsqrt(dve, n_rsq, RSQ * (k // 2), var[:, pair], rstd[:, pair], rtmp[:, pair], work)
                lows = []
            for work in lows + list(behind):
                work()

        def norm_pool(pool, n, t, x_ready):
            if t == 0:
                pool.wait_ge(gain_in, 16 * (n + 1))
            x_ready(t)
            wait(pool, n_tr, 2 * (TT * n + t - 1))
            pool.tensor_tensor(xslot(n, t), x[:, t, :], gain_b[:], ALU.mult).then_inc(n_gained, 1)

        def norm_pe(pe, n, t):
            k = TT * n + t
            pe.wait_ge(n_scaled, k + 1)
            if n == 3 and t == 0:
                pe.wait_ge(sw_masked, 2 * TT * SW_KV)
            for q in range(2):
                wait(pe, n_lo, 2 * (k - 1) + q + 1)
                for j in range(4):
                    c = (4 * q + j) * P
                    last = pe.transpose(ps[:, BT[n][q], j * P:(j + 1) * P], xslot(n, t)[:, c:c + P], ident[:])
                last.then_inc(n_tr, 1)

        def norm_behind(pe, n):
            def done(t):
                if t >= 3:
                    norm_pe(pe, n, t - 3)
                if t == TT - 1:
                    norm_pe(pe, n, TT - 3)
            return done

        def hT_ready(eng, n, t):
            eng.wait_ge(n_lo, 2 * (TT * n + t + 1))

        def load_x(sp, t):
            sp.dma_start(x[:, t, :], x_in[0, t * P:(t + 1) * P, :]).then_inc(x_in_s[t], 16)

        def load_gain(sp, n, row):
            wait(sp, n_gained, TT * n)
            sp.dma_start(gain_b[:], row.partition_broadcast(P)).then_inc(gain_in, 16)

        def down_half(pe, g, t, c, b=0, banks=BD):
            nb = len(banks)
            wait(pe, x_add, 16 * g + 2 * t + c + 1 - nb)
            product(pe, ps[:, banks[(2 * t + c) % nb], :],
                    [(aT_hi[b][:, k, t * P:(t + 1) * P], aT_lo[b][:, k, t * P:(t + 1) * P],
                      wd_hi[b][:, k, c * HALF:(c + 1) * HALF], wd_lo[b][:, k, c * HALF:(c + 1) * HALF])
                     for k in range(2)]).then_inc(down_mm, 1)

        def down_tile(pe, g, t, b=0, banks=BD):
            for c in range(2):
                down_half(pe, g, t, c, b, banks)

        def add_half(dve, g, t, c, banks=BD):
            dve.wait_ge(down_mm, 16 * g + 2 * t + c + 1)
            xs = x[:, t, c * HALF:(c + 1) * HALF]
            dve.tensor_tensor(xs, ps[:, banks[(2 * t + c) % len(banks)], :], xs, ALU.add).then_inc(x_add, 1)

        def add_tile(dve, g, t, banks=BD):
            for c in range(2):
                add_half(dve, g, t, c, banks)

        def last_group_dve(dve, g, n, lo):
            add_tile(dve, g, 0)
            for u in range(NU):
                more = [lambda c=c: add_half(dve, g, u + 1, c) for c in range(2)] if u + 1 < TT else []
                norm_dve(dve, n, u, more)
                lo(u)

        def x_final(eng, g):
            return lambda t: eng.wait_ge(x_add, 16 * g + 2 * t + 2)

        def mlp_up(pe, u, i):
            half, f = i // 2, i % 2
            wait(pe, relu_s, 4 * u + i - 1)
            product(pe, ps[:, BU[i % 2], :],
                    [(wu_hi[:, k, f * P:(f + 1) * P], wu_lo[:, k, f * P:(f + 1) * P],
                      hT_hi[:, k, half * HALF:(half + 1) * HALF], hT_lo[:, k, half * HALF:(half + 1) * HALF])
                     for k in range(KT)]).then_inc(up_mm, 1)

        def mlp_pe(pe, g, u0, dg0, pc0, n, tile_done):
            pe.wait_ge(w_lo, pc0 + 4 * g + 2)
            for i in range(4):
                if isinstance(g, int) and g == 0:
                    if i == 0:
                        pe.wait_ge(n_sq, TT * (n + 1))
                    if i in (1, 2):
                        norm_pe(pe, n, TT - 3 + i)
                    hT_ready(pe, n, 3 if i < 2 else TT - 1)
                mlp_up(pe, u0 + g, i)
            pe.wait_ge(w_lo, pc0 + 4 * g + 4)
            for t in range(TT):
                if t % 4 == 0:
                    pe.wait_ge(a_lo_s, 4 * (u0 + g) + 2 * (t // 4) + 2)
                down_tile(pe, dg0 + g, t)
                if tile_done:
                    tile_done(t)

        def mlp_sp(sp, layer, g, pc0, up):
            wu = w_up[layer].rearrange("(k p) n -> p k n", p=P)
            wd = w_down[layer].rearrange("(k p) n -> p k n", p=P)
            for j in range(2):
                if up:
                    load_piece(sp, pc0, g, 4, j, wu[:, 4 * j:4 * j + 4, bass.ds(256 * g, 256)], 256)
            for j in range(2):
                if not up:
                    load_piece(sp, pc0, g, 4, 2 + j, wd[:, bass.ds(2 * g + j, 1), :], D)

        def mlp_up_hi(act, g, pc0):
            for j in range(2):
                split_hi(act, pc0, g, 4, j, wu_hi[:, 4 * j:4 * j + 4, :], 256)

        def mlp_up_lo(dve, g, pc0):
            for j in range(2):
                split_lo(dve, pc0, g, 4, j, wu_lo[:, 4 * j:4 * j + 4, :], wu_hi[:, 4 * j:4 * j + 4, :], 256)

        def mlp_act(act, g, u0, dg0, pc0):
            act.wait_ge(down_mm, 16 * (dg0 + g))
            for j in range(2):
                split_hi(act, pc0, g, 4, 2 + j, wd_hi[0][:, j, :])
            for i in range(4):
                half, f = i // 2, i % 2
                k = 4 * (u0 + g) + i
                act.wait_ge(up_mm, k + 1)
                wait(act, sqr_s, k - 1)
                wait(act, a_hi_s, k - 1)
                act.activation(relu_t[:, i % 2, :], ps[:, BU[i % 2], :], ACT.Relu).then_inc(relu_s, 1)
                act.wait_ge(relu_s, k + 1)
                act.activation(aT_hi[0][:, f, half * HALF:(half + 1) * HALF], relu_t[:, i % 2, :],
                               ACT.Square).then_inc(a_hi_s, 1)

        def mlp_pool(pool, g, u0):
            for i in range(4):
                k = 4 * (u0 + g) + i
                pool.wait_ge(relu_s, k + 1)
                wait(pool, a_lo_s, k - 1)
                pool.tensor_tensor(sqr_t[:, i % 2, :], relu_t[:, i % 2, :], relu_t[:, i % 2, :], ALU.mult).then_inc(sqr_s, 1)

        def mlp_dve(dve, g, u0, dg0, pc0, adds):
            for i in range(4):
                half, f = i // 2, i % 2
                k = 4 * (u0 + g) + i
                if i < 2:
                    split_lo(dve, pc0, g, 4, 2 + i, wd_lo[0][:, i, :], wd_hi[0][:, i, :])
                dve.wait_ge(sqr_s, k + 1)
                dve.wait_ge(a_hi_s, k + 1)
                dve.tensor_tensor(aT_lo[0][:, f, half * HALF:(half + 1) * HALF], sqr_t[:, i % 2, :],
                                  aT_hi[0][:, f, half * HALF:(half + 1) * HALF].bitcast(F32),
                                  ALU.subtract).then_inc(a_lo_s, 1)
            adds()

        MLP_LAST = MLP_GROUPS - 1

        def mlp_pe_all(pe, u0, dg0, pc0, n, n_next):
            mlp_pe(pe, 0, u0, dg0, pc0, n, None)
            with pe.Fori(1, MLP_LAST) as g:
                mlp_pe(pe, g, u0, dg0, pc0, n, None)
            mlp_pe(pe, MLP_LAST, u0, dg0, pc0, n, None if n_next is None else norm_behind(pe, n_next))

        def mlp_act_all(act, u0, dg0, pc0):
            def body(g):
                mlp_act(act, g, u0, dg0, pc0)
                act.wait_ge(up_mm, 4 * (u0 + g + 1))
                mlp_up_hi(act, g + 1, pc0)
            body(0)
            with act.Fori(1, MLP_LAST) as g:
                body(g)
            mlp_act(act, MLP_LAST, u0, dg0, pc0)

        def mlp_dve_all(dve, u0, dg0, pc0, last_adds):
            def adds(g):
                for t in range(TT):
                    add_tile(dve, dg0 + g, t)
                    if t == 1:
                        mlp_up_lo(dve, g + 1, pc0)
            mlp_dve(dve, 0, u0, dg0, pc0, lambda: adds(0))
            with dve.Fori(1, MLP_LAST) as g:
                mlp_dve(dve, g, u0, dg0, pc0, lambda: adds(g))
            mlp_dve(dve, MLP_LAST, u0, dg0, pc0, last_adds)

        def mlp_pool_all(pool, u0):
            mlp_pool(pool, 0, u0)
            with pool.Fori(1, MLP_GROUPS) as g:
                mlp_pool(pool, g, u0)

        def mlp_sp_all(sp, layer, pc0):
            mlp_sp(sp, layer, 0, pc0, True)
            with sp.Fori(0, MLP_LAST) as g:
                mlp_sp(sp, layer, g, pc0, False)
                mlp_sp(sp, layer, g + 1, pc0, True)
            mlp_sp(sp, layer, MLP_LAST, pc0, False)

        def qk_pair(pe, h, i):
            pe.wait_ge(w_lo, RET_PIECES * h + 2 * (i // 2) + 2)
            if i == 0:
                wait(pe, v_lo_s, NCH * h)
                wait(pe, silu_s, NCH * h)
            if i == 1:
                wait(pe, k_lo_s, NCH * h)
                wait(pe, sc_masked, NCH * h)
            if i >= 2:
                pe.wait_ge(rope_mul, 16 * h + 4 * (i - 1))
            half = i % 2
            for a in range(2):
                j = 2 * (i // 2) + a
                wh = wqg_hi[:, j, :].rearrange("p (k n) -> p k n", n=P)
                wl = wqg_lo[:, j, :].rearrange("p (k n) -> p k n", n=P)
                last = product(pe, ps[:, 2 * (i % 2) + a, :],
                               [(wh[:, k, :], wl[:, k, :], hT_hi[:, k, half * HALF:(half + 1) * HALF],
                                 hT_lo[:, k, half * HALF:(half + 1) * HALF]) for k in range(KT)])
            last.then_inc(qk_mm, 1)

        def vg_product(pe, n, bank, w_h, w_l):
            return product(pe, ps[:, bank, :],
                           [(hT_hi[:, k, n * P:(n + 1) * P], hT_lo[:, k, n * P:(n + 1) * P],
                             w_h[:, k // 2, (k % 2) * HALF:(k % 2 + 1) * HALF],
                             w_l[:, k // 2, (k % 2) * HALF:(k % 2 + 1) * HALF]) for k in range(KT)])

        def v_proj(pe, h, n):
            if n == 0:
                pe.wait_ge(w_lo, RET_PIECES * h + 8)
                pe.wait_ge(rope_mul, 16 * h + 12)
            else:
                pe.wait_ge(v_lo_s, NCH * h + n)
            vg_product(pe, n, BV, wv_hi, wv_lo).then_inc(v_mm, 1)

        def g_proj(pe, h, n):
            if n == 0:
                pe.wait_ge(w_lo, RET_PIECES * h + 12)
            else:
                pe.wait_ge(silu_s, NCH * h + n)
            vg_product(pe, n, BG, wqg_hi, wqg_lo).then_inc(g_mm, 1)

        def y_transpose(pe, h, n):
            pe.wait_ge(y_s, NCH * h + n + 1)
            wait(pe, yT_s, NCH * h + n)
            for j in range(4):
                last = pe.transpose(ps[:, BY, j * P:(j + 1) * P], y[:, j * P:(j + 1) * P], ident[:])
            last.then_inc(yt_mm, 1)

        def chunk_pe(pe, h, n):
            k = NCH * h + n
            cols = slice(n * CH, (n + 1) * CH)
            if n == 0:
                pe.wait_ge(rope_add, 8 * h + 8)
                pe.wait_ge(rope_mul, 16 * h + 16)
            else:
                pe.wait_ge(k_lo_s, k)
                pe.wait_ge(sc_masked, k)
            for j in range(2):
                last = pe.transpose(ps[:, BK, j * P:(j + 1) * P], kq[:, j, cols], ident[:])
            last.then_inc(kt_mm, 1)
            for j in range(2):
                last = pe.matmul(ps[:, BSC, 0:CH], kq[:, j, cols], kq[:, 2 + j, cols], start=(j == 0), stop=(j == 1))
            last.then_inc(sc_mm, 1)
            if n < NCH - 1:
                v_proj(pe, h, n + 1)
            wait(pe, yn_s, k)
            pe.wait_ge(q_lo_s, k + 1)
            pairs = []
            if n:
                pe.wait_ge(st_lo_s, (NCH - 1) * h + n)
                pairs = [(q_hi[:, j, :], q_lo[:, j, :], st_hi[:, j, :], st_lo[:, j, :]) for j in range(2)]
            pe.wait_ge(sc_lo_s, k + 1)
            pe.wait_ge(v_lo_s, k + 1)
            last = product(pe, ps[:, BO, :], pairs + [(sc_hi[:], sc_lo[:], v_hi[:], v_lo[:])])
            last.then_inc(o_mm, 1)
            if n < NCH - 1:
                pe.wait_ge(k_lo_s, k + 1)
                wait(pe, st_upd, (NCH - 1) * h + n)
                for j in range(2):
                    last = product(pe, ps[:, BST + j, :],
                                   [(k_hi[:, j * P:(j + 1) * P], k_lo[:, j * P:(j + 1) * P], v_hi[:], v_lo[:])])
                last.then_inc(upd_mm, 1)
                g_proj(pe, h, n + 1)
                y_transpose(pe, h, n)

        def head_pe(pe, h, first):
            if first:
                for t in range(4):
                    norm_pe(pe, 0, t)
                hT_ready(pe, 0, 3)
            qk_pair(pe, h, 0)
            if first:
                for t in range(4, TT):
                    norm_pe(pe, 0, t)
                hT_ready(pe, 0, TT - 1)
            else:
                y_transpose(pe, h - 1, NCH - 1)
            for i in range(1, 4):
                qk_pair(pe, h, i)
            v_proj(pe, h, 0)
            g_proj(pe, h, 0)
            for n in range(NCH):
                chunk_pe(pe, h, n)

        def chunk_used(eng, h, n):
            if n:
                eng.wait_ge(upd_mm, (NCH - 1) * h + n)
            else:
                wait(eng, o_mm, NCH * h)

        def v_hi_act(act, h, n):
            k = NCH * h + n
            if n == 0:
                act.wait_ge(hc_set, h + 1)
            act.wait_ge(v_mm, k + 1)
            chunk_used(act, h, n)
            act.activation(v_hi[:], ps[:, BV, :], ACT.Copy, scale=hc[:, 0:1]).then_inc(v_hi_s, 1)

        def silu_act(act, h, n):
            k = NCH * h + n
            act.wait_ge(g_mm, k + 1)
            wait(act, y_s, k)
            act.activation(sgate[:], ps[:, BG, :], ACT.Silu).then_inc(silu_s, 1)

        def yT_act(act, h, n):
            k = NCH * h + n
            act.wait_ge(yt_mm, k + 1)
            wait(act, yT_out, 16 * k)
            act.activation(yT, ps[:, BY, :], ACT.Copy).then_inc(yT_s, 1)

        def qk_hi_act(act, h):
            wait(act, g_mm, NCH * h)
            for j in range(4):
                split_hi(act, 0, h, RET_PIECES, j, wqg_hi[:, j, :])

        def chunk_act(act, h, n, before_end):
            k = NCH * h + n
            cols = slice(n * CH, (n + 1) * CH)
            if n == 0:
                act.wait_ge(rope_add, 8 * h + 8)
            chunk_used(act, h, n)
            act.activation(q_hi[:], kq[:, 2:4, cols], ACT.Copy).then_inc(q_hi_s, 1)
            act.wait_ge(kt_mm, k + 1)
            act.activation(k_hi[:], ps[:, BK, 0:DK], ACT.Copy).then_inc(k_hi_s, 1)
            act.wait_ge(sc_masked, k + 1)
            act.activation(sc_hi[:], sc[:], ACT.Copy).then_inc(sc_hi_s, 1)
            if n < NCH - 1:
                v_hi_act(act, h, n + 1)
            else:
                before_end()
            act.wait_ge(g_scale, 2 * k + 2)
            wait(act, y_s, k)
            act.activation(yn, ps[:, BO, :], ACT.Identity, bias=gbias[:], scale=gscale[:]).then_inc(yn_s, 1)
            if n < NCH - 1:
                act.wait_ge(st_upd, (NCH - 1) * h + n + 1)
                act.activation(st_hi[:], state[:], ACT.Copy, scale=hc[:, 3:4]).then_inc(st_hi_s, 1)
                silu_act(act, h, n + 1)
                yT_act(act, h, n)

        def head_act(act, h, first, last):
            if not first:
                yT_act(act, h - 1, NCH - 1)
            for j in range(4):
                if j == 0:
                    if first:
                        act.wait_ge(n_scaled, TT)
                    else:
                        act.wait_ge(v_mm, NCH * h)
                split_hi(act, 0, h, RET_PIECES, 4 + j, wv_hi[:, j, :])
            for j in range(4):
                act.wait_ge(qk_mm, 4 * h + 2 * (j // 2) + 2)
                split_hi(act, 0, h, RET_PIECES, 8 + j, wqg_hi[:, j, :])
            v_hi_act(act, h, 0)
            silu_act(act, h, 0)
            for n in range(NCH):
                chunk_act(act, h, n, (lambda: out_act(act, 0, 0)) if last else (lambda: qk_hi_act(act, h + 1)))

        def rope_dve(dve, h, i):
            half = i % 2
            cols = slice(half * HALF, (half + 1) * HALF)
            a, b = ps[:, 2 * (i % 2), :], ps[:, 2 * (i % 2) + 1, :]
            j = 2 * (i // 2)
            dve.wait_ge(qk_mm, 4 * h + i + 1)
            dve.tensor_tensor(kq[:, j, cols], a, cosr[:, cols], ALU.mult).then_inc(rope_mul, 1)
            dve.tensor_tensor(kq[:, j + 1, cols], b, cosr[:, cols], ALU.mult).then_inc(rope_mul, 1)
            wait(dve, rope_add, 8 * h + 2 * i - 1)
            dve.tensor_tensor(rope_t[:], b, sinr[:, cols], ALU.mult).then_inc(rope_mul, 1)
            wait(dve, rope_add, 8 * h + 2 * i)
            dve.tensor_tensor(rope_u, a, sinr[:, cols], ALU.mult).then_inc(rope_mul, 1)

        def rope_pool(pool, h, i):
            cols = slice((i % 2) * HALF, (i % 2 + 1) * HALF)
            j = 2 * (i // 2)
            pool.wait_ge(rope_mul, 16 * h + 4 * i + 3)
            pool.tensor_tensor(kq[:, j, cols], kq[:, j, cols], rope_t[:], ALU.subtract).then_inc(rope_add, 1)
            pool.wait_ge(rope_mul, 16 * h + 4 * i + 4)
            pool.tensor_tensor(kq[:, j + 1, cols], kq[:, j + 1, cols], rope_u, ALU.add).then_inc(rope_add, 1)

        def y_pool(pool, h, n):
            k = NCH * h + n
            pool.wait_ge(yn_s, k + 1)
            pool.wait_ge(silu_s, k + 1)
            wait(pool, yt_mm, k)
            pool.tensor_tensor(y, yn, sgate[:], ALU.mult).then_inc(y_s, 1)

        def v_lo_dve(dve, h, n):
            dve.wait_ge(v_hi_s, NCH * h + n + 1)
            dve.scalar_tensor_tensor(v_lo[:], ps[:, BV, :], hc[:, 0:1], v_hi[:].bitcast(F32),
                                     ALU.mult, ALU.subtract).then_inc(v_lo_s, 1)

        def qk_lo_dve(dve, h):
            for j in range(4):
                split_lo(dve, 0, h, RET_PIECES, j, wqg_lo[:, j, :], wqg_hi[:, j, :])

        def chunk_dve(dve, h, n, before_end):
            k = NCH * h + n
            cols = slice(n * CH, (n + 1) * CH)
            dve.wait_ge(q_hi_s, k + 1)
            dve.tensor_tensor(q_lo[:], kq[:, 2:4, cols], q_hi[:].bitcast(F32), ALU.subtract).then_inc(q_lo_s, 1)
            dve.wait_ge(sc_mm, k + 1)
            wait(dve, sc_lo_s, k)
            wait(dve, sc_hi_s, k)
            dve.tensor_tensor(sc[:], ps[:, BSC, 0:CH], causal[:], ALU.mult).then_inc(sc_masked, 1)
            dve.wait_ge(k_hi_s, k + 1)
            dve.tensor_tensor(k_lo[:], ps[:, BK, 0:DK], k_hi[:].bitcast(F32), ALU.subtract).then_inc(k_lo_s, 1)
            dve.wait_ge(sc_hi_s, k + 1)
            dve.wait_ge(sc_masked, k + 1)
            dve.tensor_tensor(sc_lo[:], sc[:], sc_hi[:].bitcast(F32), ALU.subtract).then_inc(sc_lo_s, 1)
            if n == NCH - 1:
                before_end()
            dve.wait_ge(o_mm, k + 1)
            dve.bn_stats(bn[:], ps[:, BO, :]).then_inc(stats, 1)
            dve.wait_ge(stats, 3 * k + 1)
            apart(dve)
            dve.bn_aggr(mv[:], bn[:]).then_inc(stats, 1)
            dve.wait_ge(stats, 3 * k + 2)
            dve.tensor_scalar(gvar[:], mv[:, 1:2], hc[:, 2:3], EPS, ALU.mult, ALU.add).then_inc(stats, 1)
            dve.wait_ge(stats, 3 * k + 3)
            more = n < NCH - 1

            def update():
                upd = ps[:, BST:BST + 2, :]
                dve.wait_ge(upd_mm, (NCH - 1) * h + n + 1)
                if n == 0:
                    dve.tensor_copy(state[:], upd).then_inc(st_upd, 1)
                else:
                    dve.scalar_tensor_tensor(state[:], state[:], hc[:, 3:4], upd, ALU.mult, ALU.add).then_inc(st_upd, 1)

            rsqrt(dve, g_rsq, RSQ * k, gvar[:], grs[:], gtmp[:],
                  [lambda: None] * 4 + [lambda: v_lo_dve(dve, h, n + 1)] if more else ())
            wait(dve, yn_s, k)
            dve.tensor_tensor(gscale[:], grs[:], hc[:, 1:2], ALU.mult).then_inc(g_scale, 1)
            dve.wait_ge(g_scale, 2 * k + 1)
            dve.scalar_tensor_tensor(gbias[:], mv[:, 0:1], -1.0, gscale[:], ALU.mult, ALU.mult).then_inc(g_scale, 1)
            if more:
                update()
                s = (NCH - 1) * h + n
                dve.wait_ge(st_hi_s, s + 1)
                dve.wait_ge(st_upd, s + 1)
                dve.scalar_tensor_tensor(st_lo[:], state[:], hc[:, 3:4], st_hi[:].bitcast(F32),
                                         ALU.mult, ALU.subtract).then_inc(st_lo_s, 1)

        def head_dve(dve, h, last):
            wait(dve, yn_s, NCH * h)
            dve.tensor_copy(hc[:], headc[:, bass.ds(h, 1), :]).then_inc(hc_set, 1)
            dve.wait_ge(hc_set, h + 1)
            for i in range(4):
                rope_dve(dve, h, i)
                for j in range(2):
                    m = 4 + 2 * i + j
                    hi, lo, jj = (wv_hi, wv_lo, m - 4) if m < 8 else (wqg_hi, wqg_lo, m - 8)
                    split_lo(dve, 0, h, RET_PIECES, m, lo[:, jj, :], hi[:, jj, :])
            v_lo_dve(dve, h, 0)
            for n in range(NCH):
                chunk_dve(dve, h, n, (lambda: [out_lo(dve, 0, 0, j) for j in range(4)]) if last else (lambda: qk_lo_dve(dve, h + 1)))

        def head_pool(pool, h):
            for i in range(4):
                rope_pool(pool, h, i)
            for n in range(NCH):
                y_pool(pool, h, n)

        ret_w = ret_in[0].rearrange("(k p) n -> p k n", p=P)

        def qk_sp(sp, h):
            for j in range(4):
                c = (D if j < 2 else 0) + (j % 2) * P
                load_piece(sp, 0, h, RET_PIECES, j, ret_w[:, :, bass.ds(c + DK * h, P)], P)

        def yT_sp(sp, h, n):
            k = NCH * h + n
            sp.wait_ge(yT_s, k + 1)
            apart(sp)
            dst = y_dram[bass.ds(DV * h, DV), n * P:(n + 1) * P].rearrange("(j p) n -> p j n", p=P)
            sp.dma_start(dst, yT.rearrange("p (j n) -> p j n", n=P)).then_inc(yT_out, 16)

        def head_sp(sp, h, last):
            for j in range(8):
                c = 2 * D + (j // 4) * HEADS * DV
                load_piece(sp, 0, h, RET_PIECES, 4 + j,
                           ret_w[:, 2 * (j % 4):2 * (j % 4) + 2, bass.ds(c + DV * h, DV)], DV)
            for n in range(NCH):
                if n == 4 and not last:
                    qk_sp(sp, h + 1)
                if n == 4 and last:
                    sp.wait_ge(yT_out, 16 * NCH * (HEADS - 1))
                    out_sp(sp, 0)
                if n < NCH - 1:
                    yT_sp(sp, h, n)

        ret_o = ret_out[0].rearrange("(k p) n -> p k n", p=P)
        y_k = y_dram.rearrange("(k p) n -> p k n", p=P)

        def out_sp(sp, g):
            for j in range(2):
                load_piece(sp, PC_OUT, g, 4, j, y_k[:, bass.ds(2 * g + j, 1), :], D)
            for j in range(2):
                load_piece(sp, PC_OUT, g, 4, 2 + j, ret_o[:, bass.ds(2 * g + j, 1), :], D)

        def out_act(act, g, b):
            if isinstance(g, int) and g == 0:
                act.wait_ge(g_mm, NCH * HEADS)
            elif isinstance(g, int) and g == 1:
                act.wait_ge(yt_mm, NCH * HEADS)
            else:
                act.wait_ge(down_mm, 16 * (g - 1))
            for j in range(2):
                split_hi(act, PC_OUT, g, 4, j, aT_hi[b][:, j, :])
            for j in range(2):
                split_hi(act, PC_OUT, g, 4, 2 + j, wd_hi[b][:, j, :])

        def out_lo(dve, g, b, j):
            if j < 2:
                split_lo(dve, PC_OUT, g, 4, j, aT_lo[b][:, j, :], aT_hi[b][:, j, :])
            else:
                split_lo(dve, PC_OUT, g, 4, j, wd_lo[b][:, j - 2, :], wd_hi[b][:, j - 2, :])

        def out_dve(dve, g, b):
            for t in range(TT):
                add_tile(dve, g, t)
                if t % 2 == 0:
                    out_lo(dve, g + 1, 1 - b, t // 2)

        def out_pe(pe, g, b, tile_done=None):
            pe.wait_ge(w_lo, PC_OUT + 4 * g + 4)
            for t in range(TT):
                down_tile(pe, g, t, b)
                if tile_done:
                    tile_done(t)

        sw_w = sw_in[0].rearrange("(k p) n -> p k n", p=P)
        sw_o = sw_out[0].rearrange("(k p) n -> p k n", p=P)
        KC = SW_HEADS * SW_DH
        VC = KC + SW_KV * SW_DH

        def sw_sp_in(sp, g):
            for j in range(2):
                load_piece(sp, PC_SW, g, SW_PIECES, j, sw_w[:, :, bass.ds(SW_GQ * g + j * P, P)], P)
            for j in range(2):
                m = PC_SW + SW_PIECES * g + 2 + j
                wait(sp, w_lo, m - RING + 1)
                apart(sp)
                c = KC if j == 0 else VC
                dst = raw[:, 2 + j, 0:KT * SW_DH].rearrange("p (k n) -> p k n", n=SW_DH)
                sp.dma_start(dst, sw_w[:, :, bass.ds(c + SW_DH * g, SW_DH)]).then_inc(raw_in[2 + j], 16)

        def sw_sp_out(sp, g):
            for j in range(4):
                m = PC_SW + SW_PIECES * g + 4 + j
                wait(sp, w_lo, m - RING + 1)
                apart(sp)
                src = sw_o[:, bass.ds(2 * g + j // 2, 1), (j % 2) * HALF:(j % 2 + 1) * HALF]
                dst = raw[:, j, 0:HALF].rearrange("p (k n) -> p k n", n=HALF)
                sp.dma_start(dst, src).then_inc(raw_in[j], 16)

        def sw_piece(j):
            if j < 2:
                return (raw[:, j, :].rearrange("p (k n) -> p k n", n=P),
                        ws_hi[:, :, j * P:(j + 1) * P], ws_lo[:, :, j * P:(j + 1) * P])
            if j < 4:
                c = SW_GQ + (j - 2) * SW_DH
                return (raw[:, j, 0:KT * SW_DH].rearrange("p (k n) -> p k n", n=SW_DH),
                        ws_hi[:, :, c:c + SW_DH], ws_lo[:, :, c:c + SW_DH])
            k, c = (j - 4) // 2, (j % 2) * HALF
            return raw[:, j - 4, 0:HALF], wd_hi[0][:, k, c:c + HALF], wd_lo[0][:, k, c:c + HALF]

        def sw_split_hi(act, g, j):
            arrived(act, PC_SW, g, SW_PIECES, j)
            src, hi, _ = sw_piece(j)
            act.activation(hi, src, ACT.Copy).then_inc(w_hi, 1)

        def sw_split_lo(dve, g, j):
            dve.wait_ge(w_hi, PC_SW + SW_PIECES * g + j + 1)
            src, hi, lo = sw_piece(j)
            dve.tensor_tensor(lo, src, hi.bitcast(F32), ALU.subtract).then_inc(w_lo, 1)

        def a_pe(pe, g, t):
            i = TT * g + t
            if t == 0:
                pe.wait_ge(w_lo, PC_SW + SW_PIECES * g + 4)
                if isinstance(g, int) and g == 0:
                    pe.wait_ge(x_add, 16 * DG_SW)
            if isinstance(g, int) and g == 0:
                hT_ready(pe, 2, min(t, TT - 1))
            wait(pe, sw_vlo, i)
            product(pe, ps[:, SA, 0:SW_COLS],
                    [(hT_hi[:, k, t * P:(t + 1) * P], hT_lo[:, k, t * P:(t + 1) * P], ws_hi[:, k, :], ws_lo[:, k, :])
                     for k in range(KT)]).then_inc(a_mm, 1)

        def b_pe(pe, g, t):
            i = TT * g + t
            pe.wait_ge(sw_radd, i + 1)
            wait(pe, sw_qlo, 2 * i)
            wait(pe, x_add, 16 * DG_SW + 2 * (i - 2))
            krf = kr[:, :, :].rearrange("p a d -> p (a d)")
            for j in range(2):
                pe.transpose(ps[:, SB, j * P:(j + 1) * P], qr[:, j * P:(j + 1) * P], ident[:])
            pe.transpose(ps[:, SB, 2 * P:3 * P], krf[:, SW_DH:3 * SW_DH], ident[:])
            pe.transpose(ps[:, SB, 3 * P:4 * P], krf[:, 0:2 * SW_DH], ident[:]).then_inc(b_mm, 1)

        def c_pe(pe, g, t):
            i = TT * g + t
            pe.wait_ge(sw_qlo, 2 * (i + 1))
            for j in range(2):
                wait(pe, sw_masked, 2 * (i - 1) + j + 1)
                product(pe, ps[:, SS + j, :],
                        [(qT_hi[:, j, :], qT_lo[:, j, :], kT_hi[:].rearrange("p e s n -> p (e s n)"),
                          kT_lo[:].rearrange("p e s n -> p (e s n)"))]).then_inc(c_mm, 1)

        def d_pe(pe, g, t):
            i = TT * g + t
            pe.wait_ge(sw_prob, 2 * (i + 1))
            for s in range(2):
                wait(pe, sw_plo, 2 * (i - 1) + s + 1)
                for hh in range(4):
                    last = pe.transpose(ps[:, SP_ + s, hh * P:(hh + 1) * P], prob[:, hh, s, :], ident[:])
                last.then_inc(d_mm, 1)

        def e_pe(pe, g, t):
            i = TT * g + t
            pe.wait_ge(sw_plo, 2 * (i + 1))
            wait(pe, sw_olo, i)
            if isinstance(g, int) and i == 0:
                hT_ready(pe, 2, TT - 1)
            pairs = []
            for s in range(2):
                vs = t % 4 if t % 2 == s else (t - 1) % 4
                for odd in range(2):
                    c = slice(2 * SW_DH * vs + SW_DH * (1 - odd), 2 * SW_DH * vs + SW_DH * (3 - odd))
                    pairs.append((vp_hi[:, c], vp_lo[:, c], pT_hi[:, s, odd::2, :], pT_lo[:, s, odd::2, :]))
            product(pe, ps[:, SO, 0:2 * P].rearrange("p (j n) -> p j n", n=P), pairs).then_inc(e_mm, 1)

        def f_pe(pe, g, t, c):
            i = TT * g + t
            if c == 0:
                pe.wait_ge(sw_olo, i + 1)
                if t == 0:
                    pe.wait_ge(w_lo, PC_SW + SW_PIECES * g + 8)
            down_half(pe, DG_SW + g, t, c, 0, BDS)

        def v_cols(t):
            c = SW_DH * (2 * (t % 4) + 1)
            return slice(c, c + SW_DH)

        def sq_act(act, g, t):
            i = TT * g + t
            act.wait_ge(a_mm, i + 1)
            wait(act, sw_rcos, i)
            wait(act, sw_rsin, i)
            act.activation(qkn, ps[:, SA, 0:SW_NH * SW_DH].rearrange("p (a d) -> p a d", d=SW_DH),
                           ACT.Square).then_inc(sw_sq, 1)

        def copy_act(act, g, t):
            i = TT * g + t
            wait(act, sw_norm, i)
            act.activation(qk_raw[:], ps[:, SA, 0:SW_NH * SW_DH].rearrange("p (a d) -> p a d", d=SW_DH),
                           ACT.Copy).then_inc(sw_raw, 1)
            wait(act, e_mm, i - 2)
            act.activation(vp_hi[:, v_cols(t)], ps[:, SA, SW_GQ + SW_DH:SW_COLS],
                           ACT.Copy).then_inc(sw_vhi, 1)

        def prob_act(act, g, t):
            i = TT * g + t
            act.wait_ge(sw_den, 2 * (i + 1))
            for hh in (2, 3):
                last = act.activation(prob[:, hh, :, :], prob[:, hh, :, :], ACT.Copy, scale=rden[:, hh:hh + 1])
            last.then_inc(sw_prob, 1)

        def qkT_act(act, g, t):
            i = TT * g + t
            act.wait_ge(b_mm, i + 1)
            wait(act, c_mm, 2 * i)
            tr = ps[:, SB, :].rearrange("p (j n) -> p j n", n=P)
            act.activation(qT_hi[:], tr[:, 0:2, :], ACT.Copy).then_inc(sw_qhi, 1)
            act.activation(kT_hi[:, :, t % 2, :], tr[:, 2:4, :], ACT.Copy).then_inc(sw_qhi, 1)

        def pT_act(act, g, t):
            i = TT * g + t
            for s in range(2):
                act.wait_ge(d_mm, 2 * i + s + 1)
                wait(act, e_mm, i)
                act.activation(pT_hi[:, s, :, :], ps[:, SP_ + s, :].rearrange("p (j n) -> p j n", n=P),
                               ACT.Copy).then_inc(sw_phi, 1)

        def exp_act(act, g, t):
            i = TT * g + t
            act.wait_ge(sw_max, 5 * (i + 1))
            wait(act, sw_den, 2 * i)
            for hh in range(4):
                act.activation(prob[:, hh, :, :], prob[:, hh, :, :], ACT.Exp, bias=nmax[:, hh:hh + 1],
                               accum_out=ssum[:, hh:hh + 1]).then_inc(sw_exp, 1)
            act.activation(esink[:], sdif[:], ACT.Exp).then_inc(sw_exp, 1)

        def oT_act(act, g, t):
            i = TT * g + t
            act.wait_ge(e_mm, i + 1)
            wait(act, down_mm, 16 * (DG_SW + g - 1) + 2 * t + 2)
            act.activation(aT_hi[0][:, :, t * P:(t + 1) * P], ps[:, SO, 0:2 * P].rearrange("p (j n) -> p j n", n=P),
                           ACT.Copy).then_inc(sw_ohi, 1)

        def qkT_dve(dve, g, t):
            i = TT * g + t
            tr = ps[:, SB, :].rearrange("p (j n) -> p j n", n=P)
            dve.wait_ge(sw_qhi, 2 * i + 2)
            dve.tensor_tensor(qT_lo[:], tr[:, 0:2, :], qT_hi[:].bitcast(F32), ALU.subtract).then_inc(sw_qlo, 1)
            dve.tensor_tensor(kT_lo[:, :, t % 2, :], tr[:, 2:4, :], kT_hi[:, :, t % 2, :].bitcast(F32),
                              ALU.subtract).then_inc(sw_qlo, 1)

        def pT_dve(dve, g, t, s):
            i = TT * g + t
            dve.wait_ge(sw_phi, 2 * i + s + 1)
            dve.tensor_tensor(pT_lo[:, s, :, :], ps[:, SP_ + s, :].rearrange("p (j n) -> p j n", n=P),
                              pT_hi[:, s, :, :].bitcast(F32), ALU.subtract).then_inc(sw_plo, 1)

        def mask_half(dve, g, t, j):
            i = TT * g + t
            b = 2 if t == 0 else (1 if t % 2 else 0)
            dve.wait_ge(c_mm, 2 * i + j + 1)
            wait(dve, d_mm, 2 * i)
            mask = swmask[:, b:b + 2, :].rearrange("p s n -> p (s n)").unsqueeze(1).to_broadcast([P, 2, 2 * P])
            dve.scalar_tensor_tensor(prob[:, 2 * j:2 * j + 2, :, :].rearrange("p h s n -> p h (s n)"),
                                     ps[:, SS + j, :].rearrange("p (h n) -> p h n", h=2),
                                     SW_DH ** -0.5, mask, ALU.mult, ALU.add).then_inc(sw_masked, 1)

        def max_dve(dve, g, t, j):
            i = TT * g + t
            dve.wait_ge(sw_masked, 2 * i + j + 1)
            wait(dve, sw_exp, 5 * i)
            dve.tensor_reduce(smax[:, 2 * j:2 * j + 2], prob[:, 2 * j:2 * j + 2, :, :].rearrange("p h s n -> p h (s n)"),
                              axis=AX.X, op=ALU.max).then_inc(sw_max, 1)

        def sink_dve(dve, g, t, step):
            i = TT * g + t
            if step == 0:
                dve.wait_ge(sw_max, 5 * i + 2)
                dve.tensor_tensor(smax[:], smax[:], sink_b[:, bass.ds(4 * g, 4)], ALU.max).then_inc(sw_max, 1)
            else:
                dve.wait_ge(sw_max, 5 * i + 3)
                dve.tensor_scalar(nmax[:], smax[:], -1.0, None, ALU.mult).then_inc(sw_max, 1)
                dve.tensor_tensor(sdif[:], sink_b[:, bass.ds(4 * g, 4)], smax[:], ALU.subtract).then_inc(sw_max, 1)

        def den_dve(dve, g, t):
            i = TT * g + t
            dve.wait_ge(sw_exp, 5 * (i + 1))
            wait(dve, sw_prob, 2 * i)
            dve.tensor_tensor(den[:], ssum[:], esink[:], ALU.add).then_inc(sw_den, 1)
            dve.wait_ge(sw_den, 2 * i + 1)
            dve.reciprocal(rden[:], den[:]).then_inc(sw_den, 1)

        def var_dve(dve, g, t):
            i = TT * g + t
            dve.wait_ge(sw_vhi, i + 1)
            dve.tensor_tensor(vp_lo[:, v_cols(t)], ps[:, SA, SW_GQ + SW_DH:SW_COLS],
                              vp_hi[:, v_cols(t)].bitcast(F32), ALU.subtract).then_inc(sw_vlo, 1)
            dve.wait_ge(sw_sq, i + 1)
            dve.tensor_reduce(hss[:], qkn, axis=AX.X, op=ALU.add).then_inc(sw_var, 1)
            dve.wait_ge(sw_var, 2 * i + 1)
            dve.tensor_scalar(hvar[:], hss[:], 1.0 / SW_DH, EPS, ALU.mult, ALU.add).then_inc(sw_var, 1)

        def scale_dve(dve, g, t, meanwhile):
            i = TT * g + t
            dve.wait_ge(sw_var, 2 * i + 2)
            rsqrt(dve, sw_rsq, RSQ * i, hvar[:], hrs[:], htmp[:], meanwhile)
            dve.wait_ge(sw_gain, i + 1)
            dve.tensor_tensor(qkn, qk_raw[:],
                              hrs[:].unsqueeze(2).to_broadcast([P, SW_NH, SW_DH]), ALU.mult).then_inc(sw_norm, 1)
            dve.wait_ge(sw_norm, i + 1)
            wait(dve, sw_radd, i)
            dve.tensor_tensor(rope_s.rearrange("p a (e d) -> p a e d", e=2), qkn.rearrange("p a (e d) -> p a e d", e=2),
                              sins[:, t, :].unsqueeze(1).unsqueeze(1).to_broadcast([P, SW_NH, 2, SW_DH // 2]),
                              ALU.mult).then_inc(sw_rsin, 1)

        def rope_sw_pool(pool, g, t):
            i = TT * g + t
            h = SW_DH // 2
            nq = SW_NH - 1
            pool.wait_ge(sw_raw, i + 1)
            pool.tensor_tensor(qk_raw[:], qk_raw[:], qkgain[:], ALU.mult).then_inc(sw_gain, 1)
            pool.wait_ge(sw_norm, i + 1)
            wait(pool, b_mm, i)
            x4 = qkn.rearrange("p a (e d) -> p a e d", e=2)
            q4 = qr.rearrange("p (a e d) -> p a e d", e=2, d=h)
            k3 = kr[:, 1, :].rearrange("p (e d) -> p e d", e=2)
            pool.tensor_tensor(q4, x4[:, 0:nq], coss[:, t, :].unsqueeze(1).unsqueeze(1).to_broadcast([P, nq, 2, h]),
                               ALU.mult)
            pool.tensor_tensor(k3, x4[:, nq], coss[:, t, :].unsqueeze(1).to_broadcast([P, 2, h]),
                               ALU.mult).then_inc(sw_rcos, 1)
            pool.wait_ge(sw_rcos, i + 1)
            pool.wait_ge(sw_rsin, i + 1)
            s4 = rope_s.rearrange("p a (e d) -> p a e d", e=2)
            pool.tensor_tensor(q4[:, :, 0, :], q4[:, :, 0, :], s4[:, 0:nq, 1, :], ALU.subtract)
            pool.tensor_tensor(q4[:, :, 1, :], q4[:, :, 1, :], s4[:, 0:nq, 0, :], ALU.add)
            pool.tensor_tensor(k3[:, 0, :], k3[:, 0, :], s4[:, nq, 1, :], ALU.subtract)
            pool.tensor_tensor(k3[:, 1, :], k3[:, 1, :], s4[:, nq, 0, :], ALU.add).then_inc(sw_radd, 1)

        def prob_dve(dve, g, t):
            i = TT * g + t
            dve.wait_ge(sw_den, 2 * (i + 1))
            half = prob[:, 0:2, :, :].rearrange("p h s n -> p h (s n)")
            dve.tensor_tensor(half, half, rden[:, 0:2].unsqueeze(2).to_broadcast([P, 2, 2 * P]),
                               ALU.mult).then_inc(sw_prob, 1)

        def oT_dve(dve, g, t):
            i = TT * g + t
            dve.wait_ge(sw_ohi, i + 1)
            dve.tensor_tensor(aT_lo[0][:, :, t * P:(t + 1) * P], ps[:, SO, 0:2 * P].rearrange("p (j n) -> p j n", n=P),
                              aT_hi[0][:, :, t * P:(t + 1) * P].bitcast(F32), ALU.subtract).then_inc(sw_olo, 1)

        def sw_steps(which, eng):
            def item(g, s, lag):
                if s - lag >= 0:
                    return (g, s - lag)
                if isinstance(g, int) and g == 0:
                    return None
                return (g - 1, s - lag + TT)

            def run(f, g, s, lag):
                it = item(g, s, lag)
                if it and (s - lag < TT):
                    f(eng, *it)

            def step(g, s, last_group):
                if which == "pe":
                    if isinstance(g, int) and g == 0 and s == 1:
                        norm_pe(eng, 2, TT - 2)
                        norm_pe(eng, 2, TT - 1)
                    run(a_pe, g, s, 0)
                    run(b_pe, g, s, 1)
                    run(d_pe, g, s, 2)
                    run(lambda *a: f_pe(*a, 0), g, s, 3)
                    run(c_pe, g, s, 1)
                    run(lambda *a: f_pe(*a, 1), g, s, 3)
                    run(e_pe, g, s, 2)
                if which == "act":
                    run(sq_act, g, s, 0)
                    run(qkT_act, g, s, 1)
                    run(copy_act, g, s, 0)
                    run(pT_act, g, s, 2)
                    if s == 2:
                        eng.wait_ge(down_mm, 16 * (DG_SW + g))
                        for j in range(4, 8):
                            sw_split_hi(eng, g, j)
                    if s == TT - 1 and not last_group:
                        eng.wait_ge(a_mm, TT * (g + 1))
                        for j in range(4):
                            sw_split_hi(eng, g + 1, j)
                    run(exp_act, g, s, 1)
                    run(oT_act, g, s, 2)
                    run(prob_act, g, s, 1)
                if which == "dve":
                    run(qkT_dve, g, s, 1)
                    run(var_dve, g, s, 0)
                    behind = item(g, s, 2)
                    lows = [lambda j=j: pT_dve(eng, *behind, j) for j in range(2)] if behind and s - 2 < TT else []
                    softmax = item(g, s, 1)
                    masks = ([lambda j=j: mask_half(eng, *softmax, j) for j in range(2)] +
                             [lambda j=j: max_dve(eng, *softmax, j) for j in range(2)] +
                             [lambda j=j: sink_dve(eng, *softmax, j) for j in range(2)]
                             if softmax and s - 1 < TT else [])
                    if s == TT - 1 and not last_group:
                        splits = [lambda j=j: sw_split_lo(eng, g + 1, j) for j in range(4)]
                        work = lows + splits[:1] + masks[:4] + splits[1:3] + masks[4:] + splits[3:]
                    else:
                        work = lows + masks
                    if s < TT:
                        scale_dve(eng, g, s, work)
                    else:
                        for w in work:
                            w()
                    if s == 2:
                        for j in range(4, 8):
                            sw_split_lo(eng, g, j)
                    down = item(g, s, 3)
                    if down and s - 3 < TT:
                        add_tile(eng, DG_SW + down[0], down[1], BDS)
                    run(oT_dve, g, s, 2)
                    run(den_dve, g, s, 1)
                    run(prob_dve, g, s, 1)
                if which == "pool":
                    run(rope_sw_pool, g, s, 0)
            def group(g, last_group):
                for s in range(TT):
                    step(g, s, last_group)
            group(0, False)
            with eng.Fori(1, SW_KV - 1) as g:
                group(g, False)
            group(SW_KV - 1, True)
            units = ((0, 4), (4, 7), (7, NU))
            for n, s in enumerate(range(TT, TT + 3)):
                step(SW_KV - 1, s, True)
                for u in range(*units[n]):
                    if which == "pe" and 3 <= u < NU - 2:
                        norm_pe(eng, 3, u - 3)
                    if which == "act":
                        if u == NU - 2:
                            eng.wait_ge(down_mm, 16 * DG_M1)
                            mlp_up_hi(eng, 0, PC_M1)
                        norm_act(eng, 3, u, x_final(eng, DG_M1 - 1))
                    if which == "dve":
                        if u == NU - 2:
                            mlp_up_lo(eng, 0, PC_M1)
                        norm_dve(eng, 3, u)
                    if which == "pool" and u < TT:
                        norm_pool(eng, 3, u, x_final(eng, DG_M1 - 1))

        SW_FIRST_SPLITS = {2: (0, 1), 4: (2, 3)}
        SW_TABLES = {4: (0, 3), 6: (3, 8), 7: (8, 11), 8: (11, 17)}

        def table(dve, base, angle, turn, work, quarter):
            steps = (
                lambda: dve.tensor_scalar(work, angle, 1.0 / TWO_PI, quarter, ALU.mult, ALU.add),
                lambda: dve.tensor_scalar(work, work, ROUND, ROUND, ALU.add, ALU.subtract),
                lambda: dve.scalar_tensor_tensor(turn, work, -C1, angle, ALU.mult, ALU.add),
                lambda: dve.scalar_tensor_tensor(turn, work, -C2, turn, ALU.mult, ALU.add),
                lambda: dve.scalar_tensor_tensor(turn, work, -C3, turn, ALU.mult, ALU.add),
                lambda: dve.tensor_scalar(turn, turn, quarter * TWO_PI, PI_IN, ALU.add, ALU.min),
                lambda: dve.tensor_scalar(turn, turn, -PI_IN, None, ALU.max),
            )
            def one(n, step):
                dve.wait_ge(tab, base + n)
                step().then_inc(tab, 1)
            return [lambda n=n, step=step: one(n, step) for n, step in enumerate(steps)]

        @block.sync
        def _(sp):
            load_x(sp, 0)
            sp.dma_start(pos_i, positions[0].partition_broadcast(P)).then_inc(pos_in, 16)
            for dst, src in ((ident[:], c_ident), (causal[:], c_causal), (headc[:], c_head), (freq[:], c_freq)):
                sp.dma_start(dst, src).then_inc(const_in, 16)
            load_gain(sp, 0, norm_mix[0])
            for t in range(1, 4):
                load_x(sp, t)
            qk_sp(sp, 0)
            for t in range(4, TT):
                load_x(sp, t)
            load_gain(sp, 1, norm_mlp[0])
            head_sp(sp, 0, False)
            with sp.Fori(1, HEADS - 1) as h:
                yT_sp(sp, h - 1, NCH - 1)
                head_sp(sp, h, False)
            yT_sp(sp, HEADS - 2, NCH - 1)
            head_sp(sp, HEADS - 1, True)
            sp.wait_ge(v_mm, NCH * HEADS)
            for t in range(TT):
                load_x(sp, t)
            yT_sp(sp, HEADS - 1, NCH - 1)
            with sp.Fori(1, RET_GROUPS - 2) as g:
                out_sp(sp, g)
            sp.wait_ge(yT_out, 16 * NCH * HEADS)
            for g in (RET_GROUPS - 2, RET_GROUPS - 1):
                out_sp(sp, g)
            mlp_sp_all(sp, 0, PC_M0)
            load_gain(sp, 2, norm_mix[1])
            sw_sp_in(sp, 0)
            sp.wait_ge(a_lo_s, 4 * MLP_GROUPS)
            for a in range(SW_NH - 1):
                sp.dma_start(qkgain[:, a, :], q_gain[0].partition_broadcast(P)).then_inc(sw_const, 16)
            sp.dma_start(qkgain[:, SW_NH - 1, :], k_gain[0].partition_broadcast(P)).then_inc(sw_const, 16)
            sp.dma_start(sink_b[:], sinks[0].partition_broadcast(P)).then_inc(sw_const, 16)
            sp.dma_start(pos_si[:], positions[0].rearrange("(t p) -> p t", p=P),
                         allow_slow_non_contiguous=True).then_inc(sw_const, 16)
            sp.dma_start(freq_row[:], c_freq_row).then_inc(sw_const, 16)
            sp.dma_start(swmask[:], c_mask).then_inc(sw_const, 16)
            with sp.Fori(0, SW_KV - 1) as g:
                sw_sp_out(sp, g)
                sw_sp_in(sp, g + 1)
            sw_sp_out(sp, SW_KV - 1)
            load_gain(sp, 3, norm_mlp[1])
            mlp_sp_all(sp, 1, PC_M1)
            for t in range(TT):
                sp.wait_ge(x_add, 16 * (DG_M1 + MLP_LAST) + 2 * t + 2)
                sp.dma_start(out[0, t * P:(t + 1) * P, :], x[:, t, :]).then_inc(stored, 16)
            sp.wait_ge(stored, 16 * TT)

        @block.scalar
        def _(act):
            for u in range(7):
                norm_act(act, 0, u, lambda t: act.wait_ge(x_in_s[t], 16))
            qk_hi_act(act, 0)
            for u in range(7, NU):
                norm_act(act, 0, u, lambda t: act.wait_ge(x_in_s[t], 16))
            act.wait_ge(tab, 9)
            act.activation(sinr[:], turns, ACT.Sin).then_inc(tab_act, 1)
            act.wait_ge(tab, 16)
            act.activation(cosr[:], turns, ACT.Sin).then_inc(tab_act, 1)
            head_act(act, 0, True, False)
            with act.Fori(1, HEADS - 1) as h:
                head_act(act, h, False, False)
            head_act(act, HEADS - 1, False, True)
            yT_act(act, HEADS - 1, NCH - 1)
            out_act(act, 1, 1)
            with act.Fori(1, RET_GROUPS // 2) as gg:
                for b in range(2):
                    out_act(act, 2 * gg + b, b)
            mlp_up_hi(act, 0, PC_M0)
            for u in range(NU):
                norm_act(act, 1, u, x_final(act, RET_GROUPS - 1))
            mlp_act_all(act, 0, DG_M0, PC_M0)
            for u in range(NU):
                norm_act(act, 2, u, x_final(act, DG_SW - 1))
                if u == 2:
                    act.wait_ge(a_lo_s, 4 * MLP_GROUPS)
                for j in SW_FIRST_SPLITS.get(u, ()):
                    sw_split_hi(act, 0, j)
            act.wait_ge(tab, 26)
            act.activation(sins[:], sins[:], ACT.Sin).then_inc(tab_act, 1)
            act.wait_ge(tab, 33)
            act.activation(coss[:], coss[:], ACT.Sin).then_inc(tab_act, 1)
            act.wait_ge(tab_act, 4)
            act.wait_ge(sw_zero, 5)
            sw_steps("act", act)
            mlp_act_all(act, MLP_GROUPS, DG_M1, PC_M1)

        @block.vector
        def _(dve):
            dve.wait_ge(pos_in, 16)
            dve.wait_ge(const_in, 64)
            dve.tensor_copy(posf, pos_i).then_inc(tab, 1)
            dve.wait_ge(tab, 1)
            dve.tensor_scalar(ang, posf, freq[:], None, ALU.mult).then_inc(tab, 1)
            for u in range(7):
                norm_dve(dve, 0, u)
            qk_lo_dve(dve, 0)
            for step in table(dve, 2, ang, turns, posf, 0.0):
                step()
            for u in range(7, NU):
                norm_dve(dve, 0, u)
            dve.wait_ge(tab_act, 1)
            for step in table(dve, 9, ang, turns, posf, 0.25):
                step()
            dve.wait_ge(tab_act, 2)
            head_dve(dve, 0, False)
            with dve.Fori(1, HEADS - 1) as h:
                head_dve(dve, h, False)
            head_dve(dve, HEADS - 1, True)
            for t in range(TT):
                dve.wait_ge(x_in_s[t], 32)
            out_dve(dve, 0, 0)
            with dve.Fori(0, RET_GROUPS // 2 - 1) as gg:
                out_dve(dve, 2 * gg + 1, 1)
                out_dve(dve, 2 * gg + 2, 0)
            last_group_dve(dve, RET_GROUPS - 1, 1, lambda u: mlp_up_lo(dve, 0, PC_M0) if u == 1 else None)

            def angles(step):
                if step == 0:
                    dve.wait_ge(sw_const, 16 * (SW_NH + 4))
                    dve.tensor_copy(pos_sf[:], pos_si[:]).then_inc(tab, 1)
                else:
                    dve.wait_ge(tab, 17)
                    dve.tensor_tensor((sins, coss)[step - 1][:], pos_sf[:].unsqueeze(2).to_broadcast([P, TT, 32]),
                                      freq_row[:].unsqueeze(1).to_broadcast([P, TT, 32]), ALU.mult).then_inc(tab, 1)

            table_steps = ([lambda i=i: angles(i) for i in range(3)] + table(dve, 19, sins[:], sins[:], work_s, 0.0) +
                           table(dve, 26, coss[:], coss[:], work_s, 0.25))

            def attention_ahead(u):
                for j in SW_FIRST_SPLITS.get(u, ()):
                    sw_split_lo(dve, 0, j)
                for step in table_steps[slice(*SW_TABLES.get(u, (0, 0)))]:
                    step()

            mlp_dve_all(dve, 0, DG_M0, PC_M0, lambda: last_group_dve(dve, DG_SW - 1, 2, attention_ahead))
            dve.wait_ge(tab_act, 4)
            dve.wait_ge(sw_zero, 5)
            sw_steps("dve", dve)
            mlp_dve_all(dve, MLP_GROUPS, DG_M1, PC_M1,
                        lambda: [add_tile(dve, DG_M1 + MLP_LAST, t) for t in range(TT)])

        @block.gpsimd
        def _(pool):
            for t in range(TT):
                norm_pool(pool, 0, t, lambda t: pool.wait_ge(x_in_s[t], 16))
            head_pool(pool, 0)
            with pool.Fori(1, HEADS) as h:
                head_pool(pool, h)
            for t in range(TT):
                norm_pool(pool, 1, t, x_final(pool, RET_GROUPS - 1))
            mlp_pool_all(pool, 0)
            pool.wait_ge(a_lo_s, 4 * MLP_GROUPS)
            for z in (kr, kT_hi, kT_lo, vp_hi, vp_lo):
                flat = z[:].rearrange({2: "p a -> p a", 3: "p a b -> p (a b)", 4: "p a b c -> p (a b c)"}[len(z.shape)])
                pool.memset(flat if z is kr else flat.bitcast(F32), 0.0).then_inc(sw_zero, 1)
            for t in range(TT):
                norm_pool(pool, 2, t, x_final(pool, DG_SW - 1))
            sw_steps("pool", pool)
            mlp_pool_all(pool, MLP_GROUPS)

        @block.tensor
        def _(pe):
            pe.wait_ge(const_in, 64)
            head_pe(pe, 0, True)
            with pe.Fori(1, HEADS) as h:
                head_pe(pe, h, False)
            pe.wait_ge(k_lo_s, NCH * HEADS)
            out_pe(pe, 0, 0, lambda t: y_transpose(pe, HEADS - 1, NCH - 1) if t == 1 else None)
            with pe.Fori(0, RET_GROUPS // 2 - 1) as gg:
                out_pe(pe, 2 * gg + 1, 1)
                out_pe(pe, 2 * gg + 2, 0)
            out_pe(pe, RET_GROUPS - 1, 1, norm_behind(pe, 1))
            mlp_pe_all(pe, 0, DG_M0, PC_M0, 1, 2)
            sw_steps("pe", pe)
            mlp_pe_all(pe, MLP_GROUPS, DG_M1, PC_M1, 3, None)


_INS = ["x", "positions", "norm_mix", "norm_mlp", "w_up", "w_down", "ret_w_in", "ret_w_out", "swa_w_in",
        "swa_q_gain", "swa_k_gain", "swa_sinks", "swa_w_out"]


def _constants():
    import numpy as np
    i = np.arange(P)
    causal = (i[:, None] <= i[None, :]).astype(np.float32)
    cur = np.where(i[None, :] <= i[:, None], 0.0, NEG)
    prev = np.where(i[None, :] > i[:, None], 0.0, NEG)
    mask = np.stack([cur, prev, cur, np.full((P, P), NEG)], axis=1).astype(np.float32)
    head = np.zeros((P, HEADS, 4), np.float32)
    for h in range(HEADS):
        log_gamma = math.log1p(-(2.0 ** (-5.0 - h)))
        head[:, h, 0] = np.exp(-log_gamma * (i + 1)) * DK ** -0.5
        head[:, h, 1] = np.exp(log_gamma * (i + 1))
        head[:, h, 2] = np.exp(2 * log_gamma * (i + 1))
        head[:, h, 3] = np.exp(log_gamma * CH)
    freq = lambda d: np.float32(THETA) ** (-np.arange(0, d, 2, dtype=np.float32) / np.float32(d))
    return {"c_ident": np.eye(P, dtype=np.float32), "c_causal": causal, "c_mask": mask, "c_head": head,
            "c_freq": freq(DK).astype(np.float32).reshape(P, 1),
            "c_freq_row": np.ascontiguousarray(np.broadcast_to(freq(SW_DH).astype(np.float32), (P, 32)))}


def kernel(**inputs):
    import numpy as np
    from concourse import bacc
    from concourse.bass_utils import run_bass_kernel_spmd

    nc = bacc.Bacc("TRN2", target_bir_lowering=False, num_devices=1)
    arrays, args = {}, []
    for name in _INS:
        arrays[f"in_{name}"] = np.ascontiguousarray(inputs[name])
    arrays.update(_constants())
    for name, a in arrays.items():
        args.append(nc.dram_tensor(name, a.shape, mybir.dt.from_np(a.dtype), kind="ExternalInput").ap())
    out = nc.dram_tensor("out", (1, S, D), F32, kind="ExternalOutput").ap()
    y_dram = nc.dram_tensor("y_dram", (HEADS * DV, S), F32, kind="Internal").ap()
    trunk(nc, *args, out, y_dram)
    r = run_bass_kernel_spmd(nc, [arrays], core_ids=[0])
    return r.results[0]["out"]
```

```python
import math
from contextlib import ExitStack

import concourse.bass as bass
from concourse import mybir

F32 = mybir.dt.float32
F32R = mybir.dt.float32r
I32 = mybir.dt.int32
ALU = mybir.AluOpType
ACT = mybir.ActivationFunctionType
AX = mybir.AxisListType

P = 128
D = 1024
S = 1024
KT = D // P
TT = S // P
HALF = 512
EPS = 1e-6
D_FF = 4 * D
PIECE = 1024
RING = 4

HEADS = 4
DK = D // HEADS
DV = 2 * DK
CH = P
NCH = S // CH

SW_HEADS = 16
SW_KV = 4
SW_DH = 64
SW_GQ = (SW_HEADS // SW_KV) * SW_DH
SW_COLS = SW_GQ + 2 * SW_DH
SW_NH = SW_GQ // SW_DH + 1
THETA = 10000.0

RET_GROUPS = HEADS * DV // 256
MLP_GROUPS = D_FF // 256
RET_PIECES = 12
SW_PIECES = 8
PC_OUT = RET_PIECES * HEADS
PC_M0 = PC_OUT + 4 * RET_GROUPS
PC_SW = PC_M0 + 4 * MLP_GROUPS
PC_M1 = PC_SW + SW_PIECES * SW_KV
DG_M0 = RET_GROUPS
DG_SW = DG_M0 + MLP_GROUPS
DG_M1 = DG_SW + SW_KV
RSQ = 9

TWO_PI = 2.0 * math.pi
C1 = 6.28125
C2 = 1.93500518798828125e-3
C3 = TWO_PI - C1 - C2
PI_IN = 3.1415925
NEG = -1e30
NU = TT + 3
ROUND = 12582912.0


def wait(eng, sem, value):
    if isinstance(value, int) and value <= 0:
        return
    eng.wait_ge(sem, value)


def trunk(nc, x_in, positions, norm_mix, norm_mlp, w_up, w_down, ret_in, ret_out, sw_in, q_gain,
          k_gain, sinks, sw_out, c_ident, c_causal, c_mask, c_head, c_freq, c_freq_row, out, y_dram):
    ctx = ExitStack()
    with ctx:
        def sb(name, shape, dt=F32, stack=ctx):
            return stack.enter_context(nc.sbuf_tensor(name, shape, dt))

        def sem(name):
            return ctx.enter_context(nc.semaphore(name))

        ident = sb("ident", [P, P])
        causal = sb("causal", [P, P])
        headc = sb("headc", [P, HEADS, 4])
        hc = sb("hc", [P, 4])
        freq = sb("freq", [P, 1])
        gain_b = sb("gain_b", [P, D])
        raw = sb("raw", [P, RING, PIECE])
        xn = sb("xn", [P, 2, D])
        ss = sb("ss", [P, TT])
        var = sb("var", [P, TT])
        rstd = sb("rstd", [P, TT])
        rtmp = sb("rtmp", [P, TT])
        hT_hi = sb("hT_hi", [P, KT, S], F32R)
        hT_lo = sb("hT_lo", [P, KT, S], F32R)

        with ExitStack() as place:
            x = sb("x", [P, TT, D], F32, place)
        with ExitStack() as ret:
            wv_hi = sb("wv_hi", [P, 4, PIECE], F32R, ret)
            wv_lo = sb("wv_lo", [P, 4, PIECE], F32R, ret)
            wqg_hi = sb("wqg_hi", [P, 4, PIECE], F32R, ret)
            wqg_lo = sb("wqg_lo", [P, 4, PIECE], F32R, ret)
            kq = sb("kq", [P, 4, S], F32, ret)
            cosr = sb("cosr", [P, S], F32, ret)
            sinr = sb("sinr", [P, S], F32, ret)
            rope_t = sb("rope_t", [P, HALF], F32, ret)
            q_hi = sb("q_hi", [P, 2, CH], F32R, ret)
            q_lo = sb("q_lo", [P, 2, CH], F32R, ret)
            k_hi = sb("k_hi", [P, DK], F32R, ret)
            k_lo = sb("k_lo", [P, DK], F32R, ret)
            v_hi = sb("v_hi", [P, DV], F32R, ret)
            v_lo = sb("v_lo", [P, DV], F32R, ret)
            sc = sb("sc", [P, CH], F32, ret)
            sc_hi = sb("sc_hi", [P, CH], F32R, ret)
            sc_lo = sb("sc_lo", [P, CH], F32R, ret)
            state = sb("state", [P, 2, DV], F32, ret)
            st_hi = sb("st_hi", [P, 2, DV], F32R, ret)
            st_lo = sb("st_lo", [P, 2, DV], F32R, ret)
            sgate = sb("sgate", [P, DV], F32, ret)
            bn = sb("bn", [P, 6], F32, ret)
            mv = sb("mv", [P, 2], F32, ret)
            gvar = sb("gvar", [P, 1], F32, ret)
            grs = sb("grs", [P, 1], F32, ret)
            gtmp = sb("gtmp", [P, 1], F32, ret)
            gscale = sb("gscale", [P, 1], F32, ret)
            gbias = sb("gbias", [P, 1], F32, ret)
        yn, y, yT, rope_u = xn[:, 0, 0:DV], xn[:, 0, DV:D], xn[:, 1, 0:DV], xn[:, 1, DV:D]
        posf = kq[:, 0, :]
        turns = kq[:, 1, :]
        pos_i = kq[:, 2, :].bitcast(I32)
        ang = kq[:, 3, :]

        with ExitStack() as later:
            sb("x_place", [P, TT, D], F32, later)
            aT_hi = [sb("aT_hi0", [P, 2, S], F32R, later)]
            aT_lo = [sb("aT_lo0", [P, 2, S], F32R, later)]
            wd_hi = [sb("wd_hi0", [P, 2, D], F32R, later)]
            wd_lo = [sb("wd_lo0", [P, 2, D], F32R, later)]
            with ExitStack() as o:
                aT_hi.append(sb("aT_hi1", [P, 2, S], F32R, o))
                aT_lo.append(sb("aT_lo1", [P, 2, S], F32R, o))
                wd_hi.append(sb("wd_hi1", [P, 2, D], F32R, o))
                wd_lo.append(sb("wd_lo1", [P, 2, D], F32R, o))
                wu_hi = sb("wu_hi", [P, KT, 256], F32R, o)
                wu_lo = sb("wu_lo", [P, KT, 256], F32R, o)
            with ExitStack() as m:
                relu_t = sb("relu_t", [P, 2, HALF], F32, m)
                sqr_t = sb("sqr_t", [P, 2, HALF], F32, m)
                squares = sb("squares", [P, D], F32, m)
            with ExitStack() as s:
                ws_hi = sb("ws_hi", [P, KT, SW_COLS], F32R, s)
                ws_lo = sb("ws_lo", [P, KT, SW_COLS], F32R, s)
                kr = sb("kr", [P, 3, SW_DH], F32, s)
                qT_hi = sb("qT_hi", [P, 2, P], F32R, s)
                qT_lo = sb("qT_lo", [P, 2, P], F32R, s)
                kT_hi = sb("kT_hi", [P, 2, 2, P], F32R, s)
                kT_lo = sb("kT_lo", [P, 2, 2, P], F32R, s)
                vp_hi = sb("vp_hi", [P, 9 * SW_DH], F32R, s)
                vp_lo = sb("vp_lo", [P, 9 * SW_DH], F32R, s)
                pT_hi = sb("pT_hi", [P, 2, 4, P], F32R, s)
                pT_lo = sb("pT_lo", [P, 2, 4, P], F32R, s)
                coss = sb("coss", [P, TT, 32], F32, s)
                sins = sb("sins", [P, TT, 32], F32, s)
                qkgain = sb("qkgain", [P, SW_NH, SW_DH], F32, s)
                sink_b = sb("sink_b", [P, SW_HEADS], F32, s)
                swmask = sb("swmask", [P, 4, P], F32, s)
                pos_si = sb("pos_si", [P, TT], I32, s)
                pos_sf = sb("pos_sf", [P, TT], F32, s)
                freq_row = sb("freq_row", [P, 32], F32, s)
                hss = sb("hss", [P, SW_NH], F32, s)
                hvar = sb("hvar", [P, SW_NH], F32, s)
                hrs = sb("hrs", [P, SW_NH], F32, s)
                htmp = sb("htmp", [P, SW_NH], F32, s)
                smax = sb("smax", [P, 4], F32, s)
                nmax = sb("nmax", [P, 4], F32, s)
                sdif = sb("sdif", [P, 4], F32, s)
                ssum = sb("ssum", [P, 4], F32, s)
                esink = sb("esink", [P, 4], F32, s)
                den = sb("den", [P, 4], F32, s)
                rden = sb("rden", [P, 4], F32, s)
                qk_raw = sb("qk_raw", [P, SW_NH, SW_DH], F32, s)
        prob = xn[:, 0, :].rearrange("p (h s n) -> p h s n", s=2, n=P)
        nqk = SW_NH * SW_DH
        qkn = gain_b[:, 0:nqk].rearrange("p (a d) -> p a d", d=SW_DH)
        rope_s = gain_b[:, nqk:2 * nqk].rearrange("p (a d) -> p a d", d=SW_DH)
        qr = gain_b[:, 2 * nqk:2 * nqk + SW_GQ]
        gains = (gain_b[:], gain_b[:], gain_b[:], xn[:, 1, :])
        work_s = swmask[:, 0:2, :].rearrange("p b n -> p (b n)").rearrange("p (t f) -> p t f", f=32)

        ps = ctx.enter_context(nc.psum_tensor("ps", [P, 8, HALF], F32))
        BT = ((6, 7), (6, 7), (6, 7), (2, 3))
        BU = (4, 5)
        BD = (0, 1, 2, 3)
        BV, BG, BK, BSC, BO, BST, BY = 0, 1, 2, 3, 4, 5, 7
        SA, SB, SS, SP_, SO = 0, 1, 2, 4, 6
        BDS = (7, 1)

        raw_in = [sem(f"raw_in{i}") for i in range(RING)]
        const_in = sem("const_in")
        passed = {"SP": sem("sp_passed"), "DVE": sem("dve_passed")}
        gain_in = sem("gain_in")
        pos_in = sem("pos_in")
        x_in_s = [sem(f"x_in{t}") for t in range(TT)]
        w_hi = sem("w_hi")
        w_lo = sem("w_lo")
        n_sq = sem("n_sq")
        n_var = sem("n_var")
        n_rsq = sem("n_rsq")
        n_gained = sem("n_gained")
        n0_gained = sem("n0_gained")
        n0_even = sem("n0_even")
        n0_odd = sem("n0_odd")
        n_scaled = sem("n_scaled")
        n_tr = sem("n_tr")
        n_hi = sem("n_hi")
        n_lo = sem("n_lo")
        tab = sem("tab")
        tab_act = sem("tab_act")
        hc_set = sem("hc_set")
        qk_mm = sem("qk_mm")
        rope_mul = sem("rope_mul")
        rope_add = sem("rope_add")
        v_mm = sem("v_mm")
        g_mm = sem("g_mm")
        kt_mm = sem("kt_mm")
        sc_mm = sem("sc_mm")
        o_mm = sem("o_mm")
        upd_mm = sem("upd_mm")
        yt_mm = sem("yt_mm")
        v_hi_s = sem("v_hi_s")
        v_lo_s = sem("v_lo_s")
        silu_s = sem("silu_s")
        q_hi_s = sem("q_hi_s")
        q_lo_s = sem("q_lo_s")
        k_hi_s = sem("k_hi_s")
        k_lo_s = sem("k_lo_s")
        sc_masked = sem("sc_masked")
        sc_hi_s = sem("sc_hi_s")
        sc_lo_s = sem("sc_lo_s")
        stats = sem("stats")
        g_rsq = sem("g_rsq")
        g_scale = sem("g_scale")
        st_upd = sem("st_upd")
        st_hi_s = sem("st_hi_s")
        st_lo_s = sem("st_lo_s")
        yn_s = sem("yn_s")
        y_s = sem("y_s")
        yT_s = sem("yT_s")
        yT_out = sem("yT_out")
        down_mm = sem("down_mm")
        x_add = sem("x_add")
        up_mm = sem("up_mm")
        relu_s = sem("relu_s")
        sqr_s = sem("sqr_s")
        a_hi_s = sem("a_hi_s")
        a_lo_s = sem("a_lo_s")
        sw_const = sem("sw_const")
        sw_zero = sem("sw_zero")
        sw_mask = sem("sw_mask")
        a_mm = sem("a_mm")
        sw_sq = sem("sw_sq")
        sw_raw = sem("sw_raw")
        sw_vhi = sem("sw_vhi")
        sw_vlo = sem("sw_vlo")
        sw_var = sem("sw_var")
        sw_rsq = sem("sw_rsq")
        sw_norm = sem("sw_norm")
        sw_gain = sem("sw_gain")
        sw_rcos = sem("sw_rcos")
        sw_rsin = sem("sw_rsin")
        sw_radd = sem("sw_radd")
        b_mm = sem("b_mm")
        sw_qhi = sem("sw_qhi")
        sw_qlo = sem("sw_qlo")
        c_mm = sem("c_mm")
        sw_masked = sem("sw_masked")
        sw_max = sem("sw_max")
        sw_exp = sem("sw_exp")
        sw_den = sem("sw_den")
        sw_prob = sem("sw_prob")
        d_mm = sem("d_mm")
        sw_phi = sem("sw_phi")
        sw_plo = sem("sw_plo")
        e_mm = sem("e_mm")
        sw_ohi = sem("sw_ohi")
        sw_olo = sem("sw_olo")
        stored = sem("stored")

        block = ctx.enter_context(nc.Block())

        def apart(eng):
            eng.sem_inc(passed[eng.engine.name], 1)

        def arrived(eng, m0, i, per, j, dmas=1):
            eng.wait_ge(raw_in[j % RING], 16 * (m0 // RING + j // RING + 1) + 16 * (per // RING) * i)

        def load_piece(sp, m0, i, per, j, src, fold):
            wait(sp, w_lo, m0 + per * i + j - RING + 1)
            apart(sp)
            dst = raw[:, j % RING, :]
            sp.dma_start(dst.rearrange("p (k n) -> p k n", n=fold), src).then_inc(raw_in[j % RING], 16)

        def split_hi(act, m0, i, per, j, dst, shape=None):
            arrived(act, m0, i, per, j)
            src = raw[:, j % RING, :]
            if shape:
                src = src.rearrange("p (k n) -> p k n", n=shape)
            act.activation(dst, src, ACT.Copy).then_inc(w_hi, 1)

        def split_lo(dve, m0, i, per, j, dst, hi, shape=None):
            dve.wait_ge(w_hi, m0 + per * i + j + 1)
            src = raw[:, j % RING, :]
            if shape:
                src = src.rearrange("p (k n) -> p k n", n=shape)
            dve.tensor_tensor(dst, src, hi.bitcast(F32), ALU.subtract).then_inc(w_lo, 1)

        def rsqrt(dve, count, base, a, r, t, meanwhile=()):
            todo = list(meanwhile)
            each = -(-len(todo) // (RSQ - 1)) if todo else 0

            def step(k, ins):
                ins.then_inc(count, 1)
                for work in todo[each * k:each * (k + 1)]:
                    work()
                dve.wait_ge(count, base + k + 1)

            step(0, dve.tensor_scalar(r.bitcast(I32), a.bitcast(I32), 1, None, ALU.logical_shift_right))
            step(1, dve.tensor_scalar(r.bitcast(I32), r.bitcast(I32), -1.0, float(0x5F3759DF), ALU.mult, ALU.add))
            step(2, dve.scalar_tensor_tensor(t, r, -0.5, r, ALU.mult, ALU.mult))
            step(3, dve.tensor_tensor(t, t, a, ALU.mult))
            step(4, dve.scalar_tensor_tensor(r, t, 1.5, r, ALU.add, ALU.mult))
            c = math.sqrt(3 / 8)
            step(5, dve.scalar_tensor_tensor(t, r, c, r, ALU.mult, ALU.mult))
            step(6, dve.tensor_tensor(t, t, a, ALU.mult))
            step(7, dve.scalar_tensor_tensor(t, t, -10 / 8 / c, t, ALU.add, ALU.mult))
            step(8, dve.scalar_tensor_tensor(r, t, 15 / 8, r, ALU.add, ALU.mult))

        def product(pe, bank, pairs, halfway=None):
            last = None
            for i, (ah, al, bh, bl) in enumerate(pairs):
                if halfway and 2 * i == len(pairs):
                    halfway()
                pe.matmul(bank, ah, bh, start=(i == 0), stop=False)
                pe.matmul(bank, ah, bl, start=False, stop=False)
                last = pe.matmul(bank, al, bh, start=False, stop=(i == len(pairs) - 1))
            return last

        def xslot(n, t):
            if n == 0:
                return (xn[:, 0, :], xn[:, 1, :], state[:].rearrange("p a b -> p (a b)"), cosr[:])[t % 4]
            if n < 3:
                return xn[:, t % 2, :]
            return (relu_t, sqr_t)[t % 2][:].rearrange("p a b -> p (a b)")

        def tr_bank(n, t, q):
            return ((6, 7), (2, 3))[t % 2][q] if n == 0 else BT[n][q]

        def norm_sq(act, n, t, x_ready):
            k = TT * n + t
            x_ready(t)
            wait(act, n_sq, k)
            to = ps[:, 4:6, :] if n < 3 else squares[:].rearrange("p (a b) -> p a b", b=HALF)
            act.activation(to, x[:, t, :].rearrange("p (a b) -> p a b", b=HALF), ACT.Square,
                           accum_out=ss[:, t:t + 1]).then_inc(n_sq, 1)

        def norm_hi(act, n, t):
            for q in range(2):
                act.wait_ge(n_tr, 2 * (TT * n + t) + q + 1)
                act.activation(hT_hi[:, 4 * q:4 * q + 4, t * P:(t + 1) * P],
                               ps[:, tr_bank(n, t, q), :].rearrange("p (k n) -> p k n", n=P), ACT.Copy).then_inc(n_hi, 1)

        def norm_scale(act, n, t):
            act.wait_ge(n_rsq, RSQ * ((TT * n + t) // 2 + 1))
            if n == 0:
                act.wait_ge(n0_gained, t // 2 + 1)
            else:
                act.wait_ge(n_gained, TT * (n - 1) + t + 1)
            act.activation(xslot(n, t), xslot(n, t), ACT.Copy,
                           scale=rstd[:, t:t + 1]).then_inc(n0_even if n == 0 else n_scaled, 1)

        def norm_act(act, n, u, x_ready):
            if u < TT:
                norm_sq(act, n, u, x_ready)
            if u >= 3:
                norm_hi(act, n, u - 3)
            if 1 <= u <= TT:
                norm_scale(act, n, u - 1)

        def norm_dve_lo(dve, n, t, q):
            dve.wait_ge(n_hi, 2 * (TT * n + t) + q + 1)
            dve.tensor_tensor(hT_lo[:, 4 * q:4 * q + 4, t * P:(t + 1) * P],
                              ps[:, tr_bank(n, t, q), :].rearrange("p (k n) -> p k n", n=P),
                              hT_hi[:, 4 * q:4 * q + 4, t * P:(t + 1) * P].bitcast(F32),
                              ALU.subtract).then_inc(n_lo, 1)

        def norm_lows(dve, n, t):
            return [lambda q=q: norm_dve_lo(dve, n, t, q) for q in range(2)]

        def norm_rstd(dve, n, t, lows=()):
            k = TT * n + t
            pair = slice(t - 1, t + 1)
            dve.wait_ge(n_sq, k + 1)
            dve.tensor_scalar(var[:, pair], ss[:, pair], 1.0 / D, EPS, ALU.mult, ALU.add).then_inc(n_var, 1)
            dve.wait_ge(n_var, k // 2 + 1)
            work = [lambda: None] * (RSQ - 1)
            work[2:2 + 2 * len(lows):2] = lows
            rsqrt(dve, n_rsq, RSQ * (k // 2), var[:, pair], rstd[:, pair], rtmp[:, pair], work)

        def norm_dve(dve, n, u, behind=()):
            lows = norm_lows(dve, n, u - 3) if u >= 3 else []
            if u < TT and u % 2:
                norm_rstd(dve, n, u, lows)
                lows = []
            for work in lows + list(behind):
                work()

        def norm_pool(pool, n, t, x_ready):
            if t == 0:
                pool.wait_ge(gain_in, 16 * (n + 1))
            x_ready(t)
            wait(pool, n_tr, 2 * (t - 3) if n == 0 else 2 * (TT * n + t - 1))
            pool.tensor_tensor(xslot(n, t), x[:, t, :], gains[n], ALU.mult).then_inc(n0_gained if n == 0 else n_gained, 1)

        def norm_odd_dve(dve, t):
            if t == 1:
                dve.wait_ge(gain_in, 16)
            dve.wait_ge(n_rsq, RSQ * (t // 2 + 1))
            wait(dve, n_tr, 2 * (t - 3))
            dve.scalar_tensor_tensor(xslot(0, t), x[:, t, :], rstd[:, t:t + 1], gain_b[:], ALU.mult,
                                     ALU.mult).then_inc(n0_odd, 1)

        def norm_pe(pe, n, t):
            k = TT * n + t
            if n == 0:
                pe.wait_ge((n0_even, n0_odd)[t % 2], t // 2 + 1)
            else:
                pe.wait_ge(n_scaled, k - TT + 1)
            if n == 3 and t == 0:
                pe.wait_ge(sw_masked, 2 * TT * SW_KV)
            for q in range(2):
                wait(pe, n_lo, 2 * (t - 2) + q + 1 if n == 0 else 2 * (k - 1) + q + 1)
                for j in range(4):
                    c = (4 * q + j) * P
                    last = pe.transpose(ps[:, tr_bank(n, t, q), j * P:(j + 1) * P], xslot(n, t)[:, c:c + P], ident[:])
                last.then_inc(n_tr, 1)

        def norm_behind(pe, n):
            def done(t):
                if t >= 3:
                    norm_pe(pe, n, t - 3)
                if t == TT - 1:
                    if n == 2:
                        a_pe(pe, 0, 0)
                    norm_pe(pe, n, TT - 3)
            return done

        def hT_ready(eng, n, t):
            eng.wait_ge(n_lo, 2 * (TT * n + t + 1))

        def load_x(sp, t):
            sp.dma_start(x[:, t, :], x_in[0, t * P:(t + 1) * P, :]).then_inc(x_in_s[t], 16)

        def load_gain(sp, n, row):
            if n == 1:
                sp.wait_ge(n0_gained, TT // 2)
                sp.wait_ge(n0_odd, TT // 2)
            elif n == 2:
                sp.wait_ge(n_gained, TT)
            elif n == 3:
                sp.wait_ge(n_tr, 2 * TT * 3)
            sp.dma_start(gains[n], row.partition_broadcast(P)).then_inc(gain_in, 16)

        def down_half(pe, g, t, c, b=0, banks=BD):
            nb = len(banks)
            wait(pe, x_add, 16 * g + 2 * t + c + 1 - nb)
            product(pe, ps[:, banks[(2 * t + c) % nb], :],
                    [(aT_hi[b][:, k, t * P:(t + 1) * P], aT_lo[b][:, k, t * P:(t + 1) * P],
                      wd_hi[b][:, k, c * HALF:(c + 1) * HALF], wd_lo[b][:, k, c * HALF:(c + 1) * HALF])
                     for k in range(2)]).then_inc(down_mm, 1)

        def down_tile(pe, g, t, b=0, banks=BD):
            for c in range(2):
                down_half(pe, g, t, c, b, banks)

        def add_half(dve, g, t, c, banks=BD):
            dve.wait_ge(down_mm, 16 * g + 2 * t + c + 1)
            xs = x[:, t, c * HALF:(c + 1) * HALF]
            dve.tensor_tensor(xs, ps[:, banks[(2 * t + c) % len(banks)], :], xs, ALU.add).then_inc(x_add, 1)

        def add_tile(dve, g, t, banks=BD):
            for c in range(2):
                add_half(dve, g, t, c, banks)

        def last_group_dve(dve, g, n, lo, units=NU):
            add_tile(dve, g, 0)
            for u in range(units):
                more = [lambda c=c: add_half(dve, g, u + 1, c) for c in range(2)] if u + 1 < TT else []
                norm_dve(dve, n, u, more)
                lo(u)

        def x_final(eng, g):
            return lambda t: eng.wait_ge(x_add, 16 * g + 2 * t + 2)

        def mlp_up(pe, u, i, halfway=None):
            half, f = i // 2, i % 2
            wait(pe, relu_s, 4 * u + i - 1)
            product(pe, ps[:, BU[i % 2], :],
                    [(wu_hi[:, k, f * P:(f + 1) * P], wu_lo[:, k, f * P:(f + 1) * P],
                      hT_hi[:, k, half * HALF:(half + 1) * HALF], hT_lo[:, k, half * HALF:(half + 1) * HALF])
                     for k in range(KT)], halfway).then_inc(up_mm, 1)

        LAST_TR = {1: {(1, 0): TT - 2, (1, 1): TT - 1}, 3: {(0, 1): TT - 3, (1, 0): TT - 2, (1, 1): TT - 1}}

        def mlp_pe(pe, g, u0, dg0, pc0, n, tile_done):
            pe.wait_ge(w_lo, pc0 + 4 * g + 2)
            for i in range(4):
                if isinstance(g, int) and g == 0:
                    if i == 0:
                        pe.wait_ge(n_sq, TT * (n + 1))
                    if (i, 0) in LAST_TR[n]:
                        norm_pe(pe, n, LAST_TR[n][i, 0])
                    hT_ready(pe, n, 3 if i < 2 else TT - 1)
                    if (i, 1) in LAST_TR[n]:
                        mlp_up(pe, u0 + g, i, lambda: norm_pe(pe, n, LAST_TR[n][i, 1]))
                        continue
                mlp_up(pe, u0 + g, i)
            pe.wait_ge(w_lo, pc0 + 4 * g + 4)
            for t in range(TT):
                if t % 4 == 0:
                    pe.wait_ge(a_lo_s, 4 * (u0 + g) + 2 * (t // 4) + 2)
                down_tile(pe, dg0 + g, t)
                if tile_done:
                    tile_done(t)

        def mlp_sp(sp, layer, g, pc0, up):
            wu = w_up[layer].rearrange("(k p) n -> p k n", p=P)
            wd = w_down[layer].rearrange("(k p) n -> p k n", p=P)
            for j in range(2):
                if up:
                    load_piece(sp, pc0, g, 4, j, wu[:, 4 * j:4 * j + 4, bass.ds(256 * g, 256)], 256)
            for j in range(2):
                if not up:
                    load_piece(sp, pc0, g, 4, 2 + j, wd[:, bass.ds(2 * g + j, 1), :], D)

        def mlp_up_hi(act, g, pc0, js=(0, 1)):
            for j in js:
                split_hi(act, pc0, g, 4, j, wu_hi[:, 4 * j:4 * j + 4, :], 256)

        def mlp_up_lo(dve, g, pc0, js=(0, 1)):
            for j in js:
                split_lo(dve, pc0, g, 4, j, wu_lo[:, 4 * j:4 * j + 4, :], wu_hi[:, 4 * j:4 * j + 4, :], 256)

        def mlp_act(act, g, u0, dg0, pc0):
            act.wait_ge(down_mm, 16 * (dg0 + g))
            for j in range(2):
                split_hi(act, pc0, g, 4, 2 + j, wd_hi[0][:, j, :])
            for i in range(4):
                half, f = i // 2, i % 2
                k = 4 * (u0 + g) + i
                act.wait_ge(up_mm, k + 1)
                wait(act, sqr_s, k - 1)
                wait(act, a_hi_s, k - 1)
                act.activation(relu_t[:, i % 2, :], ps[:, BU[i % 2], :], ACT.Relu).then_inc(relu_s, 1)
                act.wait_ge(relu_s, k + 1)
                act.activation(aT_hi[0][:, f, half * HALF:(half + 1) * HALF], relu_t[:, i % 2, :],
                               ACT.Square).then_inc(a_hi_s, 1)

        def mlp_pool(pool, g, u0):
            for i in range(4):
                k = 4 * (u0 + g) + i
                pool.wait_ge(relu_s, k + 1)
                wait(pool, a_lo_s, k - 1)
                pool.tensor_tensor(sqr_t[:, i % 2, :], relu_t[:, i % 2, :], relu_t[:, i % 2, :], ALU.mult).then_inc(sqr_s, 1)

        def mlp_dve(dve, g, u0, dg0, pc0, adds):
            for i in range(4):
                half, f = i // 2, i % 2
                k = 4 * (u0 + g) + i
                if i < 2:
                    split_lo(dve, pc0, g, 4, 2 + i, wd_lo[0][:, i, :], wd_hi[0][:, i, :])
                dve.wait_ge(sqr_s, k + 1)
                dve.wait_ge(a_hi_s, k + 1)
                dve.tensor_tensor(aT_lo[0][:, f, half * HALF:(half + 1) * HALF], sqr_t[:, i % 2, :],
                                  aT_hi[0][:, f, half * HALF:(half + 1) * HALF].bitcast(F32),
                                  ALU.subtract).then_inc(a_lo_s, 1)
            adds()

        MLP_LAST = MLP_GROUPS - 1

        def mlp_pe_all(pe, u0, dg0, pc0, n, n_next):
            mlp_pe(pe, 0, u0, dg0, pc0, n, None)
            with pe.Fori(1, MLP_LAST) as g:
                mlp_pe(pe, g, u0, dg0, pc0, n, None)
            mlp_pe(pe, MLP_LAST, u0, dg0, pc0, n, None if n_next is None else norm_behind(pe, n_next))

        def mlp_act_all(act, u0, dg0, pc0):
            def body(g):
                mlp_act(act, g, u0, dg0, pc0)
                act.wait_ge(up_mm, 4 * (u0 + g + 1))
                mlp_up_hi(act, g + 1, pc0)
            body(0)
            with act.Fori(1, MLP_LAST) as g:
                body(g)
            mlp_act(act, MLP_LAST, u0, dg0, pc0)

        def mlp_dve_all(dve, u0, dg0, pc0, last_adds):
            def adds(g):
                for t in range(TT):
                    add_tile(dve, dg0 + g, t)
                    if t == 1:
                        mlp_up_lo(dve, g + 1, pc0)
            mlp_dve(dve, 0, u0, dg0, pc0, lambda: adds(0))
            with dve.Fori(1, MLP_LAST) as g:
                mlp_dve(dve, g, u0, dg0, pc0, lambda: adds(g))
            mlp_dve(dve, MLP_LAST, u0, dg0, pc0, last_adds)

        def mlp_pool_all(pool, u0):
            mlp_pool(pool, 0, u0)
            with pool.Fori(1, MLP_GROUPS) as g:
                mlp_pool(pool, g, u0)

        def mlp_sp_all(sp, layer, pc0):
            mlp_sp(sp, layer, 0, pc0, True)
            with sp.Fori(0, MLP_LAST) as g:
                mlp_sp(sp, layer, g, pc0, False)
                mlp_sp(sp, layer, g + 1, pc0, True)
            mlp_sp(sp, layer, MLP_LAST, pc0, False)

        def qk_pair(pe, h, i, between=None):
            pe.wait_ge(w_lo, RET_PIECES * h + 2 * (i // 2) + 2)
            if i == 0:
                wait(pe, v_lo_s, NCH * h)
                wait(pe, silu_s, NCH * h)
            if i == 1:
                wait(pe, k_lo_s, NCH * h)
                wait(pe, sc_masked, NCH * h)
            if i >= 2:
                pe.wait_ge(rope_mul, 16 * h + 4 * (i - 1))
            half = i % 2
            for a in range(2):
                j = 2 * (i // 2) + a
                wh = wqg_hi[:, j, :].rearrange("p (k n) -> p k n", n=P)
                wl = wqg_lo[:, j, :].rearrange("p (k n) -> p k n", n=P)
                last = product(pe, ps[:, 2 * (i % 2) + a, :],
                               [(wh[:, k, :], wl[:, k, :], hT_hi[:, k, half * HALF:(half + 1) * HALF],
                                 hT_lo[:, k, half * HALF:(half + 1) * HALF]) for k in range(KT)],
                               between and between[2 * a])
                if a == 1:
                    last.then_inc(qk_mm, 1)
                if between:
                    between[2 * a + 1]()

        def vg_product(pe, n, bank, w_h, w_l):
            return product(pe, ps[:, bank, :],
                           [(hT_hi[:, k, n * P:(n + 1) * P], hT_lo[:, k, n * P:(n + 1) * P],
                             w_h[:, k // 2, (k % 2) * HALF:(k % 2 + 1) * HALF],
                             w_l[:, k // 2, (k % 2) * HALF:(k % 2 + 1) * HALF]) for k in range(KT)])

        def v_proj(pe, h, n):
            if n == 0:
                pe.wait_ge(w_lo, RET_PIECES * h + 8)
                pe.wait_ge(rope_mul, 16 * h + 12)
            else:
                pe.wait_ge(v_lo_s, NCH * h + n)
            vg_product(pe, n, BV, wv_hi, wv_lo).then_inc(v_mm, 1)

        def g_proj(pe, h, n):
            if n == 0:
                pe.wait_ge(w_lo, RET_PIECES * h + 12)
            else:
                pe.wait_ge(silu_s, NCH * h + n)
            vg_product(pe, n, BG, wqg_hi, wqg_lo).then_inc(g_mm, 1)

        def y_transpose(pe, h, n):
            pe.wait_ge(y_s, NCH * h + n + 1)
            wait(pe, yT_s, NCH * h + n)
            for j in range(4):
                last = pe.transpose(ps[:, BY, j * P:(j + 1) * P], y[:, j * P:(j + 1) * P], ident[:])
            last.then_inc(yt_mm, 1)

        def chunk_pe(pe, h, n):
            k = NCH * h + n
            cols = slice(n * CH, (n + 1) * CH)
            if n == 0:
                pe.wait_ge(rope_add, 8 * h + 8)
                pe.wait_ge(rope_mul, 16 * h + 16)
            else:
                pe.wait_ge(k_lo_s, k)
                pe.wait_ge(sc_masked, k)
            for j in range(2):
                last = pe.transpose(ps[:, BK, j * P:(j + 1) * P], kq[:, j, cols], ident[:])
            last.then_inc(kt_mm, 1)
            for j in range(2):
                last = pe.matmul(ps[:, BSC, 0:CH], kq[:, j, cols], kq[:, 2 + j, cols], start=(j == 0), stop=(j == 1))
            last.then_inc(sc_mm, 1)
            if n < NCH - 1:
                v_proj(pe, h, n + 1)
            wait(pe, yn_s, k)
            pe.wait_ge(q_lo_s, k + 1)
            pairs = []
            if n:
                pe.wait_ge(st_lo_s, (NCH - 1) * h + n)
                pairs = [(q_hi[:, j, :], q_lo[:, j, :], st_hi[:, j, :], st_lo[:, j, :]) for j in range(2)]
            pe.wait_ge(sc_lo_s, k + 1)
            pe.wait_ge(v_lo_s, k + 1)
            last = product(pe, ps[:, BO, :], pairs + [(sc_hi[:], sc_lo[:], v_hi[:], v_lo[:])])
            last.then_inc(o_mm, 1)
            if n < NCH - 1:
                pe.wait_ge(k_lo_s, k + 1)
                wait(pe, st_upd, (NCH - 1) * h + n)
                for j in range(2):
                    last = product(pe, ps[:, BST + j, :],
                                   [(k_hi[:, j * P:(j + 1) * P], k_lo[:, j * P:(j + 1) * P], v_hi[:], v_lo[:])])
                last.then_inc(upd_mm, 1)
                g_proj(pe, h, n + 1)
                y_transpose(pe, h, n)

        def head_pe(pe, h, first):
            if first:
                for t in range(4):
                    norm_pe(pe, 0, t)
                hT_ready(pe, 0, 3)
                qk_pair(pe, h, 0, [lambda t=t: norm_pe(pe, 0, t) for t in range(4, TT)])
                hT_ready(pe, 0, TT - 1)
            else:
                qk_pair(pe, h, 0)
                y_transpose(pe, h - 1, NCH - 1)
            for i in range(1, 4):
                qk_pair(pe, h, i)
            v_proj(pe, h, 0)
            g_proj(pe, h, 0)
            for n in range(NCH):
                chunk_pe(pe, h, n)

        def chunk_used(eng, h, n):
            if n:
                eng.wait_ge(upd_mm, (NCH - 1) * h + n)
            else:
                wait(eng, o_mm, NCH * h)

        def v_hi_act(act, h, n):
            k = NCH * h + n
            if n == 0:
                act.wait_ge(hc_set, h + 1)
            act.wait_ge(v_mm, k + 1)
            chunk_used(act, h, n)
            act.activation(v_hi[:], ps[:, BV, :], ACT.Copy, scale=hc[:, 0:1]).then_inc(v_hi_s, 1)

        def silu_act(act, h, n):
            k = NCH * h + n
            act.wait_ge(g_mm, k + 1)
            wait(act, y_s, k)
            act.activation(sgate[:], ps[:, BG, :], ACT.Silu).then_inc(silu_s, 1)

        def yT_act(act, h, n):
            k = NCH * h + n
            act.wait_ge(yt_mm, k + 1)
            wait(act, yT_out, 16 * k)
            act.activation(yT, ps[:, BY, :], ACT.Copy).then_inc(yT_s, 1)

        def qk_hi_act(act, h):
            wait(act, g_mm, NCH * h)
            for j in range(4):
                split_hi(act, 0, h, RET_PIECES, j, wqg_hi[:, j, :])

        def chunk_act(act, h, n, before_end):
            k = NCH * h + n
            cols = slice(n * CH, (n + 1) * CH)
            if n == 0:
                act.wait_ge(rope_add, 8 * h + 8)
            chunk_used(act, h, n)
            act.activation(q_hi[:], kq[:, 2:4, cols], ACT.Copy).then_inc(q_hi_s, 1)
            act.wait_ge(kt_mm, k + 1)
            act.activation(k_hi[:], ps[:, BK, 0:DK], ACT.Copy).then_inc(k_hi_s, 1)
            act.wait_ge(sc_masked, k + 1)
            act.activation(sc_hi[:], sc[:], ACT.Copy).then_inc(sc_hi_s, 1)
            if n < NCH - 1:
                v_hi_act(act, h, n + 1)
            else:
                before_end()
            act.wait_ge(g_scale, 2 * k + 2)
            wait(act, y_s, k)
            act.activation(yn, ps[:, BO, :], ACT.Identity, bias=gbias[:], scale=gscale[:]).then_inc(yn_s, 1)
            if n < NCH - 1:
                act.wait_ge(st_upd, (NCH - 1) * h + n + 1)
                act.activation(st_hi[:], state[:], ACT.Copy, scale=hc[:, 3:4]).then_inc(st_hi_s, 1)
                silu_act(act, h, n + 1)
                yT_act(act, h, n)

        def head_act(act, h, first, last):
            if not first:
                yT_act(act, h - 1, NCH - 1)
            for j in range(4):
                if j == 0:
                    if first:
                        act.wait_ge(n0_even, TT // 2)
                        act.wait_ge(n0_odd, TT // 2)
                        act.wait_ge(n_sq, TT)
                    else:
                        act.wait_ge(v_mm, NCH * h)
                split_hi(act, 0, h, RET_PIECES, 4 + j, wv_hi[:, j, :])
            for j in range(4):
                act.wait_ge(qk_mm, 4 * h + 2 * (j // 2) + 2)
                split_hi(act, 0, h, RET_PIECES, 8 + j, wqg_hi[:, j, :])
            v_hi_act(act, h, 0)
            silu_act(act, h, 0)
            for n in range(NCH):
                chunk_act(act, h, n, (lambda: out_act(act, 0, 0)) if last else (lambda: qk_hi_act(act, h + 1)))

        def rope_dve(dve, h, i):
            half = i % 2
            cols = slice(half * HALF, (half + 1) * HALF)
            a, b = ps[:, 2 * (i % 2), :], ps[:, 2 * (i % 2) + 1, :]
            j = 2 * (i // 2)
            dve.wait_ge(qk_mm, 4 * h + i + 1)
            dve.tensor_tensor(kq[:, j, cols], a, cosr[:, cols], ALU.mult).then_inc(rope_mul, 1)
            dve.tensor_tensor(kq[:, j + 1, cols], b, cosr[:, cols], ALU.mult).then_inc(rope_mul, 1)
            wait(dve, rope_add, 8 * h + 2 * i - 1)
            dve.tensor_tensor(rope_t[:], b, sinr[:, cols], ALU.mult).then_inc(rope_mul, 1)
            wait(dve, rope_add, 8 * h + 2 * i)
            dve.tensor_tensor(rope_u, a, sinr[:, cols], ALU.mult).then_inc(rope_mul, 1)

        def rope_pool(pool, h, i):
            cols = slice((i % 2) * HALF, (i % 2 + 1) * HALF)
            j = 2 * (i // 2)
            pool.wait_ge(rope_mul, 16 * h + 4 * i + 3)
            pool.tensor_tensor(kq[:, j, cols], kq[:, j, cols], rope_t[:], ALU.subtract).then_inc(rope_add, 1)
            pool.wait_ge(rope_mul, 16 * h + 4 * i + 4)
            pool.tensor_tensor(kq[:, j + 1, cols], kq[:, j + 1, cols], rope_u, ALU.add).then_inc(rope_add, 1)

        def y_pool(pool, h, n):
            k = NCH * h + n
            pool.wait_ge(yn_s, k + 1)
            pool.wait_ge(silu_s, k + 1)
            wait(pool, yt_mm, k)
            pool.tensor_tensor(y, yn, sgate[:], ALU.mult).then_inc(y_s, 1)

        def v_lo_dve(dve, h, n):
            dve.wait_ge(v_hi_s, NCH * h + n + 1)
            dve.scalar_tensor_tensor(v_lo[:], ps[:, BV, :], hc[:, 0:1], v_hi[:].bitcast(F32),
                                     ALU.mult, ALU.subtract).then_inc(v_lo_s, 1)

        def qk_lo_dve(dve, h):
            for j in range(4):
                split_lo(dve, 0, h, RET_PIECES, j, wqg_lo[:, j, :], wqg_hi[:, j, :])

        def chunk_dve(dve, h, n, before_end):
            k = NCH * h + n
            cols = slice(n * CH, (n + 1) * CH)
            dve.wait_ge(q_hi_s, k + 1)
            dve.tensor_tensor(q_lo[:], kq[:, 2:4, cols], q_hi[:].bitcast(F32), ALU.subtract).then_inc(q_lo_s, 1)
            dve.wait_ge(sc_mm, k + 1)
            wait(dve, sc_lo_s, k)
            wait(dve, sc_hi_s, k)
            dve.tensor_tensor(sc[:], ps[:, BSC, 0:CH], causal[:], ALU.mult).then_inc(sc_masked, 1)
            dve.wait_ge(k_hi_s, k + 1)
            dve.tensor_tensor(k_lo[:], ps[:, BK, 0:DK], k_hi[:].bitcast(F32), ALU.subtract).then_inc(k_lo_s, 1)
            dve.wait_ge(sc_hi_s, k + 1)
            dve.wait_ge(sc_masked, k + 1)
            dve.tensor_tensor(sc_lo[:], sc[:], sc_hi[:].bitcast(F32), ALU.subtract).then_inc(sc_lo_s, 1)
            if n == NCH - 1:
                before_end()
            dve.wait_ge(o_mm, k + 1)
            dve.bn_stats(bn[:], ps[:, BO, :]).then_inc(stats, 1)
            dve.wait_ge(stats, 3 * k + 1)
            apart(dve)
            dve.bn_aggr(mv[:], bn[:]).then_inc(stats, 1)
            dve.wait_ge(stats, 3 * k + 2)
            dve.tensor_scalar(gvar[:], mv[:, 1:2], hc[:, 2:3], EPS, ALU.mult, ALU.add).then_inc(stats, 1)
            dve.wait_ge(stats, 3 * k + 3)
            more = n < NCH - 1

            def update():
                upd = ps[:, BST:BST + 2, :]
                dve.wait_ge(upd_mm, (NCH - 1) * h + n + 1)
                if n == 0:
                    dve.tensor_copy(state[:], upd).then_inc(st_upd, 1)
                else:
                    dve.scalar_tensor_tensor(state[:], state[:], hc[:, 3:4], upd, ALU.mult, ALU.add).then_inc(st_upd, 1)

            rsqrt(dve, g_rsq, RSQ * k, gvar[:], grs[:], gtmp[:],
                  [lambda: None] * 4 + [lambda: v_lo_dve(dve, h, n + 1)] if more else ())
            wait(dve, yn_s, k)
            dve.tensor_tensor(gscale[:], grs[:], hc[:, 1:2], ALU.mult).then_inc(g_scale, 1)
            dve.wait_ge(g_scale, 2 * k + 1)
            dve.scalar_tensor_tensor(gbias[:], mv[:, 0:1], -1.0, gscale[:], ALU.mult, ALU.mult).then_inc(g_scale, 1)
            if more:
                update()
                s = (NCH - 1) * h + n
                dve.wait_ge(st_hi_s, s + 1)
                dve.wait_ge(st_upd, s + 1)
                dve.scalar_tensor_tensor(st_lo[:], state[:], hc[:, 3:4], st_hi[:].bitcast(F32),
                                         ALU.mult, ALU.subtract).then_inc(st_lo_s, 1)

        def head_dve(dve, h, last):
            wait(dve, yn_s, NCH * h)
            dve.tensor_copy(hc[:], headc[:, bass.ds(h, 1), :]).then_inc(hc_set, 1)
            dve.wait_ge(hc_set, h + 1)
            for i in range(4):
                rope_dve(dve, h, i)
                for j in range(2):
                    m = 4 + 2 * i + j
                    if isinstance(h, int) and h == 0 and m == 4:
                        dve.wait_ge(w_lo, 4)
                    hi, lo, jj = (wv_hi, wv_lo, m - 4) if m < 8 else (wqg_hi, wqg_lo, m - 8)
                    split_lo(dve, 0, h, RET_PIECES, m, lo[:, jj, :], hi[:, jj, :])
            v_lo_dve(dve, h, 0)
            for n in range(NCH):
                chunk_dve(dve, h, n, (lambda: [out_lo(dve, 0, 0, j) for j in range(4)]) if last
                          else (lambda: qk_lo_dve(dve, h + 1)))

        def head_pool(pool, h):
            for i in range(4):
                rope_pool(pool, h, i)
            for n in range(NCH):
                y_pool(pool, h, n)

        ret_w = ret_in[0].rearrange("(k p) n -> p k n", p=P)

        def qk_sp(sp, h, js=range(4)):
            for j in js:
                c = (D if j < 2 else 0) + (j % 2) * P
                load_piece(sp, 0, h, RET_PIECES, j, ret_w[:, :, bass.ds(c + DK * h, P)], P)

        def yT_sp(sp, h, n):
            k = NCH * h + n
            sp.wait_ge(yT_s, k + 1)
            apart(sp)
            dst = y_dram[bass.ds(DV * h, DV), n * P:(n + 1) * P].rearrange("(j p) n -> p j n", p=P)
            sp.dma_start(dst, yT.rearrange("p (j n) -> p j n", n=P)).then_inc(yT_out, 16)

        def head_sp(sp, h, last):
            for j in range(8):
                c = 2 * D + (j // 4) * HEADS * DV
                load_piece(sp, 0, h, RET_PIECES, 4 + j,
                           ret_w[:, 2 * (j % 4):2 * (j % 4) + 2, bass.ds(c + DV * h, DV)], DV)
            for n in range(NCH):
                if n == 4 and not last:
                    qk_sp(sp, h + 1)
                if n == 4 and last:
                    sp.wait_ge(yT_out, 16 * NCH * (HEADS - 1))
                    out_sp(sp, 0)
                if n < NCH - 1:
                    yT_sp(sp, h, n)

        ret_o = ret_out[0].rearrange("(k p) n -> p k n", p=P)
        y_k = y_dram.rearrange("(k p) n -> p k n", p=P)

        def out_sp(sp, g):
            for j in range(2):
                load_piece(sp, PC_OUT, g, 4, j, y_k[:, bass.ds(2 * g + j, 1), :], D)
            for j in range(2):
                load_piece(sp, PC_OUT, g, 4, 2 + j, ret_o[:, bass.ds(2 * g + j, 1), :], D)

        def out_act(act, g, b):
            if isinstance(g, int) and g == 0:
                act.wait_ge(g_mm, NCH * HEADS)
            elif isinstance(g, int) and g == 1:
                act.wait_ge(yt_mm, NCH * HEADS)
            else:
                act.wait_ge(down_mm, 16 * (g - 1))
            for j in range(2):
                split_hi(act, PC_OUT, g, 4, j, aT_hi[b][:, j, :])
            for j in range(2):
                split_hi(act, PC_OUT, g, 4, 2 + j, wd_hi[b][:, j, :])

        def out_lo(dve, g, b, j):
            if j < 2:
                split_lo(dve, PC_OUT, g, 4, j, aT_lo[b][:, j, :], aT_hi[b][:, j, :])
            else:
                split_lo(dve, PC_OUT, g, 4, j, wd_lo[b][:, j - 2, :], wd_hi[b][:, j - 2, :])

        def out_dve(dve, g, b):
            for t in range(TT):
                add_tile(dve, g, t)
                if t % 2 == 0:
                    out_lo(dve, g + 1, 1 - b, t // 2)

        def out_pe(pe, g, b, tile_done=None):
            pe.wait_ge(w_lo, PC_OUT + 4 * g + 4)
            for t in range(TT):
                down_tile(pe, g, t, b)
                if tile_done:
                    tile_done(t)

        sw_w = sw_in[0].rearrange("(k p) n -> p k n", p=P)
        sw_o = sw_out[0].rearrange("(k p) n -> p k n", p=P)
        KC = SW_HEADS * SW_DH
        VC = KC + SW_KV * SW_DH

        def sw_sp_in(sp, g):
            for j in range(2):
                load_piece(sp, PC_SW, g, SW_PIECES, j, sw_w[:, :, bass.ds(SW_GQ * g + j * P, P)], P)
            for j in range(2):
                m = PC_SW + SW_PIECES * g + 2 + j
                wait(sp, w_lo, m - RING + 1)
                apart(sp)
                c = KC if j == 0 else VC
                dst = raw[:, 2 + j, 0:KT * SW_DH].rearrange("p (k n) -> p k n", n=SW_DH)
                sp.dma_start(dst, sw_w[:, :, bass.ds(c + SW_DH * g, SW_DH)]).then_inc(raw_in[2 + j], 16)

        def sw_sp_out(sp, g):
            for j in range(4):
                m = PC_SW + SW_PIECES * g + 4 + j
                wait(sp, w_lo, m - RING + 1)
                apart(sp)
                src = sw_o[:, bass.ds(2 * g + j // 2, 1), (j % 2) * HALF:(j % 2 + 1) * HALF]
                dst = raw[:, j, 0:HALF].rearrange("p (k n) -> p k n", n=HALF)
                sp.dma_start(dst, src).then_inc(raw_in[j], 16)

        def sw_piece(j):
            if j < 2:
                return (raw[:, j, :].rearrange("p (k n) -> p k n", n=P),
                        ws_hi[:, :, j * P:(j + 1) * P], ws_lo[:, :, j * P:(j + 1) * P])
            if j < 4:
                c = SW_GQ + (j - 2) * SW_DH
                return (raw[:, j, 0:KT * SW_DH].rearrange("p (k n) -> p k n", n=SW_DH),
                        ws_hi[:, :, c:c + SW_DH], ws_lo[:, :, c:c + SW_DH])
            k, c = (j - 4) // 2, (j % 2) * HALF
            return raw[:, j - 4, 0:HALF], wd_hi[0][:, k, c:c + HALF], wd_lo[0][:, k, c:c + HALF]

        def sw_split_hi(act, g, j):
            arrived(act, PC_SW, g, SW_PIECES, j)
            src, hi, _ = sw_piece(j)
            act.activation(hi, src, ACT.Copy).then_inc(w_hi, 1)

        def sw_split_lo(dve, g, j):
            dve.wait_ge(w_hi, PC_SW + SW_PIECES * g + j + 1)
            src, hi, lo = sw_piece(j)
            dve.tensor_tensor(lo, src, hi.bitcast(F32), ALU.subtract).then_inc(w_lo, 1)

        def a_pe(pe, g, t):
            i = TT * g + t
            if t == 0:
                pe.wait_ge(w_lo, PC_SW + SW_PIECES * g + 4)
                if isinstance(g, int) and g == 0:
                    pe.wait_ge(x_add, 16 * DG_SW)
            if isinstance(g, int) and g == 0:
                hT_ready(pe, 2, min(t, TT - 1))
            wait(pe, sw_vlo, i)
            product(pe, ps[:, SA, 0:SW_COLS],
                    [(hT_hi[:, k, t * P:(t + 1) * P], hT_lo[:, k, t * P:(t + 1) * P], ws_hi[:, k, :], ws_lo[:, k, :])
                     for k in range(KT)]).then_inc(a_mm, 1)

        def b_pe(pe, g, t):
            i = TT * g + t
            pe.wait_ge(sw_radd, i + 1)
            wait(pe, sw_qlo, 2 * i)
            wait(pe, x_add, 16 * DG_SW + 2 * (i - 2))
            krf = kr[:, :, :].rearrange("p a d -> p (a d)")
            for j in range(2):
                pe.transpose(ps[:, SB, j * P:(j + 1) * P], qr[:, j * P:(j + 1) * P], ident[:])
            pe.transpose(ps[:, SB, 2 * P:3 * P], krf[:, SW_DH:3 * SW_DH], ident[:])
            pe.transpose(ps[:, SB, 3 * P:4 * P], krf[:, 0:2 * SW_DH], ident[:]).then_inc(b_mm, 1)

        def c_pe(pe, g, t):
            i = TT * g + t
            pe.wait_ge(sw_qlo, 2 * (i + 1))
            for j in range(2):
                wait(pe, sw_masked, 2 * (i - 1) + j + 1)
                product(pe, ps[:, SS + j, :],
                        [(qT_hi[:, j, :], qT_lo[:, j, :], kT_hi[:].rearrange("p e s n -> p (e s n)"),
                          kT_lo[:].rearrange("p e s n -> p (e s n)"))]).then_inc(c_mm, 1)

        def d_pe(pe, g, t):
            i = TT * g + t
            pe.wait_ge(sw_prob, 2 * (i + 1))
            for s in range(2):
                wait(pe, sw_plo, 2 * (i - 1) + s + 1)
                for hh in range(4):
                    last = pe.transpose(ps[:, SP_ + s, hh * P:(hh + 1) * P], prob[:, hh, s, :], ident[:])
                last.then_inc(d_mm, 1)

        def e_pe(pe, g, t):
            i = TT * g + t
            pe.wait_ge(sw_plo, 2 * (i + 1))
            wait(pe, sw_olo, i)
            if isinstance(g, int) and i == 0:
                hT_ready(pe, 2, TT - 1)
            pairs = []
            for s in range(2):
                vs = t % 4 if t % 2 == s else (t - 1) % 4
                for odd in range(2):
                    c = slice(2 * SW_DH * vs + SW_DH * (1 - odd), 2 * SW_DH * vs + SW_DH * (3 - odd))
                    pairs.append((vp_hi[:, c], vp_lo[:, c], pT_hi[:, s, odd::2, :], pT_lo[:, s, odd::2, :]))
            product(pe, ps[:, SO, 0:2 * P].rearrange("p (j n) -> p j n", n=P), pairs).then_inc(e_mm, 1)

        def f_pe(pe, g, t, c):
            i = TT * g + t
            if c == 0:
                pe.wait_ge(sw_olo, i + 1)
                if t == 0:
                    pe.wait_ge(w_lo, PC_SW + SW_PIECES * g + 8)
            down_half(pe, DG_SW + g, t, c, 0, BDS)

        def v_cols(t):
            c = SW_DH * (2 * (t % 4) + 1)
            return slice(c, c + SW_DH)

        def sq_act(act, g, t):
            i = TT * g + t
            act.wait_ge(a_mm, i + 1)
            wait(act, sw_rcos, i)
            wait(act, sw_rsin, i)
            if isinstance(g, int) and i == 0:
                act.wait_ge(n_gained, TT * 2)
            act.activation(qkn, ps[:, SA, 0:SW_NH * SW_DH].rearrange("p (a d) -> p a d", d=SW_DH),
                           ACT.Square).then_inc(sw_sq, 1)

        def copy_act(act, g, t):
            i = TT * g + t
            act.wait_ge(a_mm, i + 1)
            wait(act, sw_norm, i)
            act.activation(qk_raw[:], ps[:, SA, 0:SW_NH * SW_DH].rearrange("p (a d) -> p a d", d=SW_DH),
                           ACT.Copy).then_inc(sw_raw, 1)
            wait(act, e_mm, i - 2)
            act.activation(vp_hi[:, v_cols(t)], ps[:, SA, SW_GQ + SW_DH:SW_COLS],
                           ACT.Copy).then_inc(sw_vhi, 1)

        def prob_act(act, g, t):
            i = TT * g + t
            act.wait_ge(sw_den, 2 * (i + 1))
            for hh in (2, 3):
                last = act.activation(prob[:, hh, :, :], prob[:, hh, :, :], ACT.Copy, scale=rden[:, hh:hh + 1])
            last.then_inc(sw_prob, 1)

        def qkT_act(act, g, t):
            i = TT * g + t
            act.wait_ge(b_mm, i + 1)
            wait(act, c_mm, 2 * i)
            tr = ps[:, SB, :].rearrange("p (j n) -> p j n", n=P)
            act.activation(qT_hi[:], tr[:, 0:2, :], ACT.Copy).then_inc(sw_qhi, 1)
            act.activation(kT_hi[:, :, t % 2, :], tr[:, 2:4, :], ACT.Copy).then_inc(sw_qhi, 1)

        def pT_act(act, g, t):
            i = TT * g + t
            for s in range(2):
                act.wait_ge(d_mm, 2 * i + s + 1)
                wait(act, e_mm, i)
                act.activation(pT_hi[:, s, :, :], ps[:, SP_ + s, :].rearrange("p (j n) -> p j n", n=P),
                               ACT.Copy).then_inc(sw_phi, 1)

        def exp_act(act, g, t):
            i = TT * g + t
            act.wait_ge(sw_max, 5 * (i + 1))
            wait(act, sw_den, 2 * i)
            for hh in range(4):
                act.activation(prob[:, hh, :, :], prob[:, hh, :, :], ACT.Exp, bias=nmax[:, hh:hh + 1],
                               accum_out=ssum[:, hh:hh + 1]).then_inc(sw_exp, 1)
            act.activation(esink[:], sdif[:], ACT.Exp).then_inc(sw_exp, 1)

        def oT_act(act, g, t):
            i = TT * g + t
            act.wait_ge(e_mm, i + 1)
            wait(act, down_mm, 16 * (DG_SW + g - 1) + 2 * t + 2)
            act.activation(aT_hi[0][:, :, t * P:(t + 1) * P], ps[:, SO, 0:2 * P].rearrange("p (j n) -> p j n", n=P),
                           ACT.Copy).then_inc(sw_ohi, 1)

        def qkT_dve(dve, g, t):
            i = TT * g + t
            tr = ps[:, SB, :].rearrange("p (j n) -> p j n", n=P)
            dve.wait_ge(sw_qhi, 2 * i + 2)
            dve.tensor_tensor(qT_lo[:], tr[:, 0:2, :], qT_hi[:].bitcast(F32), ALU.subtract).then_inc(sw_qlo, 1)
            dve.tensor_tensor(kT_lo[:, :, t % 2, :], tr[:, 2:4, :], kT_hi[:, :, t % 2, :].bitcast(F32),
                              ALU.subtract).then_inc(sw_qlo, 1)

        def pT_dve(dve, g, t, s):
            i = TT * g + t
            dve.wait_ge(sw_phi, 2 * i + s + 1)
            dve.tensor_tensor(pT_lo[:, s, :, :], ps[:, SP_ + s, :].rearrange("p (j n) -> p j n", n=P),
                              pT_hi[:, s, :, :].bitcast(F32), ALU.subtract).then_inc(sw_plo, 1)

        def mask_half(dve, g, t, j):
            i = TT * g + t
            b = 2 if t == 0 else (1 if t % 2 else 0)
            if isinstance(g, int) and i == 0 and j == 0:
                dve.wait_ge(sw_mask, 16)
            dve.wait_ge(c_mm, 2 * i + j + 1)
            wait(dve, d_mm, 2 * i)
            mask = swmask[:, b:b + 2, :].rearrange("p s n -> p (s n)").unsqueeze(1).to_broadcast([P, 2, 2 * P])
            dve.scalar_tensor_tensor(prob[:, 2 * j:2 * j + 2, :, :].rearrange("p h s n -> p h (s n)"),
                                     ps[:, SS + j, :].rearrange("p (h n) -> p h n", h=2),
                                     SW_DH ** -0.5, mask, ALU.mult, ALU.add).then_inc(sw_masked, 1)

        def max_dve(dve, g, t, j):
            i = TT * g + t
            dve.wait_ge(sw_masked, 2 * i + j + 1)
            wait(dve, sw_exp, 5 * i)
            dve.tensor_reduce(smax[:, 2 * j:2 * j + 2], prob[:, 2 * j:2 * j + 2, :, :].rearrange("p h s n -> p h (s n)"),
                              axis=AX.X, op=ALU.max).then_inc(sw_max, 1)

        def sink_dve(dve, g, t, step):
            i = TT * g + t
            if step == 0:
                dve.wait_ge(sw_max, 5 * i + 2)
                dve.tensor_tensor(smax[:], smax[:], sink_b[:, bass.ds(4 * g, 4)], ALU.max).then_inc(sw_max, 1)
            else:
                dve.wait_ge(sw_max, 5 * i + 3)
                dve.tensor_scalar(nmax[:], smax[:], -1.0, None, ALU.mult).then_inc(sw_max, 1)
                dve.tensor_tensor(sdif[:], sink_b[:, bass.ds(4 * g, 4)], smax[:], ALU.subtract).then_inc(sw_max, 1)

        def den_dve(dve, g, t):
            i = TT * g + t
            dve.wait_ge(sw_exp, 5 * (i + 1))
            wait(dve, sw_prob, 2 * i)
            dve.tensor_tensor(den[:], ssum[:], esink[:], ALU.add).then_inc(sw_den, 1)
            dve.wait_ge(sw_den, 2 * i + 1)
            dve.reciprocal(rden[:], den[:]).then_inc(sw_den, 1)

        def vlo_dve(dve, g, t):
            i = TT * g + t
            dve.wait_ge(sw_sq, i + 1)
            dve.wait_ge(sw_vhi, i + 1)
            dve.tensor_tensor(vp_lo[:, v_cols(t)], ps[:, SA, SW_GQ + SW_DH:SW_COLS],
                              vp_hi[:, v_cols(t)].bitcast(F32), ALU.subtract).then_inc(sw_vlo, 1)

        def var_dve(dve, g, t):
            i = TT * g + t
            dve.wait_ge(sw_sq, i + 1)
            dve.tensor_reduce(hss[:], qkn, axis=AX.X, op=ALU.add).then_inc(sw_var, 1)
            dve.wait_ge(sw_var, 2 * i + 1)
            dve.tensor_scalar(hvar[:], hss[:], 1.0 / SW_DH, EPS, ALU.mult, ALU.add).then_inc(sw_var, 1)

        def scale_dve(dve, g, t, meanwhile):
            i = TT * g + t
            dve.wait_ge(sw_var, 2 * i + 2)
            rsqrt(dve, sw_rsq, RSQ * i, hvar[:], hrs[:], htmp[:], meanwhile)
            dve.wait_ge(sw_gain, i + 1)
            dve.tensor_tensor(qkn, qk_raw[:],
                              hrs[:].unsqueeze(2).to_broadcast([P, SW_NH, SW_DH]), ALU.mult).then_inc(sw_norm, 1)
            dve.wait_ge(sw_norm, i + 1)
            wait(dve, sw_radd, i)
            if isinstance(g, int) and i == 0:
                dve.wait_ge(tab_act, 3)
            dve.tensor_tensor(rope_s.rearrange("p a (e d) -> p a e d", e=2), qkn.rearrange("p a (e d) -> p a e d", e=2),
                              sins[:, t, :].unsqueeze(1).unsqueeze(1).to_broadcast([P, SW_NH, 2, SW_DH // 2]),
                              ALU.mult).then_inc(sw_rsin, 1)

        def rope_sw_pool(pool, g, t):
            i = TT * g + t
            h = SW_DH // 2
            nq = SW_NH - 1
            pool.wait_ge(sw_raw, i + 1)
            pool.tensor_tensor(qk_raw[:], qk_raw[:], qkgain[:], ALU.mult).then_inc(sw_gain, 1)
            pool.wait_ge(sw_norm, i + 1)
            wait(pool, b_mm, i)
            if isinstance(g, int) and i == 0:
                pool.wait_ge(tab_act, 4)
            x4 = qkn.rearrange("p a (e d) -> p a e d", e=2)
            q4 = qr.rearrange("p (a e d) -> p a e d", e=2, d=h)
            k3 = kr[:, 1, :].rearrange("p (e d) -> p e d", e=2)
            pool.tensor_tensor(q4, x4[:, 0:nq], coss[:, t, :].unsqueeze(1).unsqueeze(1).to_broadcast([P, nq, 2, h]),
                               ALU.mult)
            pool.tensor_tensor(k3, x4[:, nq], coss[:, t, :].unsqueeze(1).to_broadcast([P, 2, h]),
                               ALU.mult).then_inc(sw_rcos, 1)
            pool.wait_ge(sw_rcos, i + 1)
            pool.wait_ge(sw_rsin, i + 1)
            s4 = rope_s.rearrange("p a (e d) -> p a e d", e=2)
            pool.tensor_tensor(q4[:, :, 0, :], q4[:, :, 0, :], s4[:, 0:nq, 1, :], ALU.subtract)
            pool.tensor_tensor(q4[:, :, 1, :], q4[:, :, 1, :], s4[:, 0:nq, 0, :], ALU.add)
            pool.tensor_tensor(k3[:, 0, :], k3[:, 0, :], s4[:, nq, 1, :], ALU.subtract)
            pool.tensor_tensor(k3[:, 1, :], k3[:, 1, :], s4[:, nq, 0, :], ALU.add).then_inc(sw_radd, 1)

        def prob_dve(dve, g, t):
            i = TT * g + t
            dve.wait_ge(sw_den, 2 * (i + 1))
            half = prob[:, 0:2, :, :].rearrange("p h s n -> p h (s n)")
            dve.tensor_tensor(half, half, rden[:, 0:2].unsqueeze(2).to_broadcast([P, 2, 2 * P]),
                               ALU.mult).then_inc(sw_prob, 1)

        def oT_dve(dve, g, t):
            i = TT * g + t
            dve.wait_ge(sw_ohi, i + 1)
            dve.tensor_tensor(aT_lo[0][:, :, t * P:(t + 1) * P], ps[:, SO, 0:2 * P].rearrange("p (j n) -> p j n", n=P),
                              aT_hi[0][:, :, t * P:(t + 1) * P].bitcast(F32), ALU.subtract).then_inc(sw_olo, 1)

        def drain_pe(pe, s, at):
            if (s, at) == (TT, "end"):
                norm_pe(pe, 3, 0)
            if (s, at) == (TT + 1, "D"):
                norm_pe(pe, 3, 1)
            if (s, at) == (TT + 1, "end"):
                norm_pe(pe, 3, 2)
            if (s, at) == (TT + 2, "end"):
                norm_pe(pe, 3, 3)
                norm_pe(pe, 3, 4)

        def drain_act(act, s, at):
            ready = x_final(act, DG_M1 - 1)
            if (s, at) == (TT - 1, "pT"):
                act.wait_ge(a_mm, TT * SW_KV)
                for t in range(4):
                    norm_sq(act, 3, t, ready)
            if (s, at) == (TT, "pT"):
                norm_scale(act, 3, 0)
                norm_scale(act, 3, 1)
            if (s, at) == (TT, "oT"):
                norm_hi(act, 3, 0)
            if (s, at) == (TT + 1, "pT"):
                norm_hi(act, 3, 1)
                norm_scale(act, 3, 2)
                norm_sq(act, 3, 4, ready)
            if (s, at) == (TT + 1, "oT"):
                norm_hi(act, 3, 2)
                norm_scale(act, 3, 3)
                norm_sq(act, 3, 5, ready)
                act.wait_ge(e_mm, TT * SW_KV)
                mlp_up_hi(act, 0, PC_M1, (0,))
                norm_hi(act, 3, 3)
                mlp_up_hi(act, 0, PC_M1, (1,))
                norm_scale(act, 3, 4)
                norm_sq(act, 3, 6, ready)
                norm_sq(act, 3, 7, ready)
                norm_hi(act, 3, 4)
                norm_scale(act, 3, 5)
                norm_scale(act, 3, 6)
                norm_hi(act, 3, 5)
                norm_scale(act, 3, 7)
                norm_hi(act, 3, 6)
                norm_hi(act, 3, 7)

        def drain_dve(dve, s, at):
            def lows(*tiles):
                for t in tiles:
                    for low in norm_lows(dve, 3, t):
                        low()
            if (s, at) == (TT - 1, "end"):
                norm_rstd(dve, 3, 1)
            if (s, at) == (TT, "pT"):
                norm_rstd(dve, 3, 3)
            if (s, at) == (TT, "end"):
                lows(0)
            if (s, at) == (TT + 1, "down"):
                lows(1)
            if (s, at) == (TT + 1, "end"):
                lows(2)
                norm_rstd(dve, 3, 5)
                mlp_up_lo(dve, 0, PC_M1, (0,))
                lows(3)
                mlp_up_lo(dve, 0, PC_M1, (1,))
            if (s, at) == (TT + 2, "end"):
                norm_rstd(dve, 3, 7)
                lows(4, 5, 6, 7)

        def sw_steps(which, eng):
            def item(g, s, lag):
                if s - lag >= 0:
                    return (g, s - lag)
                if isinstance(g, int) and g == 0:
                    return None
                return (g - 1, s - lag + TT)

            def run(f, g, s, lag):
                it = item(g, s, lag)
                if it and (s - lag < TT):
                    f(eng, *it)

            def step(g, s, last_group):
                if which == "pe":
                    begins = isinstance(g, int) and g == 0
                    if begins and s == 1:
                        norm_pe(eng, 2, TT - 2)
                    if not (begins and s == 0):
                        run(a_pe, g, s, 0)
                    if begins and s == 1:
                        norm_pe(eng, 2, TT - 1)
                    run(b_pe, g, s, 1)
                    run(d_pe, g, s, 2)
                    if last_group:
                        drain_pe(eng, s, "D")
                    run(lambda *a: f_pe(*a, 0), g, s, 3)
                    run(c_pe, g, s, 1)
                    run(lambda *a: f_pe(*a, 1), g, s, 3)
                    run(e_pe, g, s, 2)
                    if last_group:
                        drain_pe(eng, s, "end")
                if which == "act":
                    ahead = isinstance(g, int) and g == 0 and s == 0
                    if not ahead:
                        run(sq_act, g, s, 0)
                    run(qkT_act, g, s, 1)
                    if not ahead:
                        run(copy_act, g, s, 0)
                    run(pT_act, g, s, 2)
                    if s == 2:
                        eng.wait_ge(down_mm, 16 * (DG_SW + g))
                        for j in range(4, 8):
                            sw_split_hi(eng, g, j)
                    if s == TT - 1 and not last_group:
                        eng.wait_ge(a_mm, TT * (g + 1))
                        for j in range(4):
                            sw_split_hi(eng, g + 1, j)
                    if last_group:
                        drain_act(eng, s, "pT")
                    run(exp_act, g, s, 1)
                    run(oT_act, g, s, 2)
                    if last_group:
                        drain_act(eng, s, "oT")
                    run(prob_act, g, s, 1)
                if which == "dve":
                    run(qkT_dve, g, s, 1)
                    ahead = isinstance(g, int) and g == 0 and s == 0
                    if not ahead:
                        run(vlo_dve, g, s, 0)
                        run(var_dve, g, s, 0)
                    behind = item(g, s, 2)
                    lows = [lambda j=j: pT_dve(eng, *behind, j) for j in range(2)] if behind and s - 2 < TT else []
                    softmax = item(g, s, 1)
                    masks = ([lambda j=j: mask_half(eng, *softmax, j) for j in range(2)] +
                             [lambda j=j: max_dve(eng, *softmax, j) for j in range(2)] +
                             [lambda j=j: sink_dve(eng, *softmax, j) for j in range(2)]
                             if softmax and s - 1 < TT else [])
                    if s == TT - 1 and not last_group:
                        splits = [lambda j=j: sw_split_lo(eng, g + 1, j) for j in range(4)]
                        work = lows + splits[:2] + masks[:2] + splits[2:] + masks[2:]
                    else:
                        work = lows + masks
                        if last_group and s == TT:
                            work = lows + [lambda: drain_dve(eng, s, "pT")] + masks
                    if s < TT:
                        if not ahead:
                            scale_dve(eng, g, s, work)
                    else:
                        for w in work:
                            w()
                    if s == 2:
                        for j in range(4, 8):
                            sw_split_lo(eng, g, j)
                    down = item(g, s, 3)
                    if down and s - 3 < TT:
                        add_tile(eng, DG_SW + down[0], down[1], BDS)
                    if last_group:
                        drain_dve(eng, s, "down")
                    run(oT_dve, g, s, 2)
                    run(den_dve, g, s, 1)
                    run(prob_dve, g, s, 1)
                    if last_group:
                        drain_dve(eng, s, "end")
                if which == "pool":
                    run(rope_sw_pool, g, s, 0)
                    if last_group and s == TT - 1:
                        for t in range(TT):
                            norm_pool(eng, 3, t, x_final(eng, DG_M1 - 1))
            def group(g, last_group):
                for s in range(TT):
                    step(g, s, last_group)
            group(0, False)
            with eng.Fori(1, SW_KV - 1) as g:
                group(g, False)
            group(SW_KV - 1, True)
            for s in range(TT, TT + 3):
                step(SW_KV - 1, s, True)

        SW_FIRST_HI = {3: (0, 1), 5: (2, 3)}
        SW_FIRST_LO = {3: (0,), 4: (1,), 5: (2, 3)}

        def table(dve, base, angle, turn, work, quarter):
            steps = (
                lambda: dve.tensor_scalar(work, angle, 1.0 / TWO_PI, quarter, ALU.mult, ALU.add),
                lambda: dve.tensor_scalar(work, work, ROUND, ROUND, ALU.add, ALU.subtract),
                lambda: dve.scalar_tensor_tensor(turn, work, -C1, angle, ALU.mult, ALU.add),
                lambda: dve.scalar_tensor_tensor(turn, work, -C2, turn, ALU.mult, ALU.add),
                lambda: dve.scalar_tensor_tensor(turn, work, -C3, turn, ALU.mult, ALU.add),
                lambda: dve.tensor_scalar(turn, turn, quarter * TWO_PI, PI_IN, ALU.add, ALU.min),
                lambda: dve.tensor_scalar(turn, turn, -PI_IN, None, ALU.max),
            )
            def one(n, step):
                dve.wait_ge(tab, base + n)
                step().then_inc(tab, 1)
            return [lambda n=n, step=step: one(n, step) for n, step in enumerate(steps)]

        @block.sync
        def _(sp):
            load_x(sp, 0)
            load_x(sp, 1)
            load_gain(sp, 0, norm_mix[0])
            sp.dma_start(pos_i, positions[0].partition_broadcast(P)).then_inc(pos_in, 16)
            for dst, src in ((ident[:], c_ident), (causal[:], c_causal), (headc[:], c_head), (freq[:], c_freq)):
                sp.dma_start(dst, src).then_inc(const_in, 16)
            load_x(sp, 2)
            load_x(sp, 3)
            qk_sp(sp, 0, (0, 1))
            for t in range(4, TT):
                load_x(sp, t)
            qk_sp(sp, 0, (2, 3))
            load_gain(sp, 1, norm_mlp[0])
            head_sp(sp, 0, False)
            with sp.Fori(1, HEADS - 1) as h:
                yT_sp(sp, h - 1, NCH - 1)
                head_sp(sp, h, False)
            yT_sp(sp, HEADS - 2, NCH - 1)
            head_sp(sp, HEADS - 1, True)
            sp.wait_ge(v_mm, NCH * HEADS)
            for t in range(TT):
                load_x(sp, t)
            out_sp(sp, 1)
            yT_sp(sp, HEADS - 1, NCH - 1)
            with sp.Fori(2, RET_GROUPS - 2) as g:
                out_sp(sp, g)
            sp.wait_ge(yT_out, 16 * NCH * HEADS)
            for g in (RET_GROUPS - 2, RET_GROUPS - 1):
                out_sp(sp, g)
            mlp_sp_all(sp, 0, PC_M0)
            load_gain(sp, 2, norm_mix[1])
            sw_sp_in(sp, 0)
            sp.wait_ge(a_lo_s, 4 * MLP_GROUPS)
            for a in range(SW_NH - 1):
                sp.dma_start(qkgain[:, a, :], q_gain[0].partition_broadcast(P)).then_inc(sw_const, 16)
            sp.dma_start(qkgain[:, SW_NH - 1, :], k_gain[0].partition_broadcast(P)).then_inc(sw_const, 16)
            sp.dma_start(sink_b[:], sinks[0].partition_broadcast(P)).then_inc(sw_const, 16)
            sp.dma_start(pos_si[:], positions[0].rearrange("(t p) -> p t", p=P),
                         allow_slow_non_contiguous=True).then_inc(sw_const, 16)
            sp.dma_start(freq_row[:], c_freq_row).then_inc(sw_const, 16)
            sp.wait_ge(tab, 33)
            sp.dma_start(swmask[:], c_mask).then_inc(sw_mask, 16)
            with sp.Fori(0, SW_KV - 1) as g:
                sw_sp_out(sp, g)
                sw_sp_in(sp, g + 1)
            sw_sp_out(sp, SW_KV - 1)
            load_gain(sp, 3, norm_mlp[1])
            mlp_sp_all(sp, 1, PC_M1)
            for t in range(TT):
                sp.wait_ge(x_add, 16 * (DG_M1 + MLP_LAST) + 2 * t + 2)
                sp.dma_start(out[0, t * P:(t + 1) * P, :], x[:, t, :]).then_inc(stored, 16)
            sp.wait_ge(stored, 16 * TT)

        @block.scalar
        def _(act):
            ready = lambda t: act.wait_ge(x_in_s[t], 16)
            weights = lambda j: split_hi(act, 0, 0, RET_PIECES, j, wqg_hi[:, j, :])
            norm_sq(act, 0, 0, ready)
            norm_sq(act, 0, 1, ready)
            norm_sq(act, 0, 2, ready)
            norm_scale(act, 0, 0)
            norm_sq(act, 0, 3, ready)
            norm_hi(act, 0, 0)
            weights(0)
            norm_scale(act, 0, 2)
            norm_hi(act, 0, 1)
            weights(1)
            norm_hi(act, 0, 2)
            norm_hi(act, 0, 3)
            norm_sq(act, 0, 4, ready)
            norm_sq(act, 0, 5, ready)
            norm_sq(act, 0, 6, ready)
            norm_scale(act, 0, 4)
            norm_sq(act, 0, 7, ready)
            norm_hi(act, 0, 4)
            norm_scale(act, 0, 6)
            weights(2)
            norm_hi(act, 0, 5)
            weights(3)
            norm_hi(act, 0, 6)
            norm_hi(act, 0, 7)
            act.wait_ge(tab, 9)
            act.activation(sinr[:], turns, ACT.Sin).then_inc(tab_act, 1)
            act.wait_ge(tab, 16)
            act.activation(cosr[:], turns, ACT.Sin).then_inc(tab_act, 1)
            head_act(act, 0, True, False)
            with act.Fori(1, HEADS - 1) as h:
                head_act(act, h, False, False)
            head_act(act, HEADS - 1, False, True)
            yT_act(act, HEADS - 1, NCH - 1)
            out_act(act, 1, 1)
            with act.Fori(1, RET_GROUPS // 2) as gg:
                for b in range(2):
                    out_act(act, 2 * gg + b, b)
            mlp_up_hi(act, 0, PC_M0)
            for u in range(NU):
                norm_act(act, 1, u, x_final(act, RET_GROUPS - 1))
            mlp_act_all(act, 0, DG_M0, PC_M0)
            ready = x_final(act, DG_SW - 1)
            for u in range(TT - 1):
                if u == 3:
                    act.wait_ge(a_lo_s, 4 * MLP_GROUPS)
                norm_sq(act, 2, u, ready)
                if u >= 3:
                    norm_hi(act, 2, u - 3)
                for j in SW_FIRST_HI.get(u, ()):
                    sw_split_hi(act, 0, j)
                if u:
                    norm_scale(act, 2, u - 1)
            norm_sq(act, 2, TT - 1, ready)
            norm_hi(act, 2, 4)
            norm_scale(act, 2, 6)
            act.wait_ge(sw_zero, 5)
            copy_act(act, 0, 0)
            norm_hi(act, 2, 5)
            norm_scale(act, 2, 7)
            sq_act(act, 0, 0)
            norm_hi(act, 2, 6)
            act.wait_ge(tab, 26)
            act.activation(sins[:], sins[:], ACT.Sin).then_inc(tab_act, 1)
            act.wait_ge(tab, 33)
            act.activation(coss[:], coss[:], ACT.Sin).then_inc(tab_act, 1)
            norm_hi(act, 2, 7)
            sw_steps("act", act)
            mlp_act_all(act, MLP_GROUPS, DG_M1, PC_M1)

        @block.vector
        def _(dve):
            sine = table(dve, 2, ang, turns, posf, 0.0)
            lows = lambda *tiles: [low for t in tiles for low in norm_lows(dve, 0, t)]
            norm_rstd(dve, 0, 1)
            norm_odd_dve(dve, 1)
            norm_rstd(dve, 0, 3, lows(0))
            norm_odd_dve(dve, 3)
            for low in lows(1, 2, 3):
                low()
            dve.wait_ge(pos_in, 16)
            dve.wait_ge(const_in, 64)
            dve.tensor_copy(posf, pos_i).then_inc(tab, 1)
            dve.wait_ge(tab, 1)
            dve.tensor_scalar(ang, posf, freq[:], None, ALU.mult).then_inc(tab, 1)
            norm_rstd(dve, 0, 5)
            norm_odd_dve(dve, 5)
            for step in sine[:2]:
                step()
            norm_rstd(dve, 0, 7, lows(4))
            norm_odd_dve(dve, 7)
            for step in sine[2:3] + lows(5) + sine[3:4] + lows(6, 7) + sine[4:]:
                step()
            dve.wait_ge(tab_act, 1)
            for step in table(dve, 9, ang, turns, posf, 0.25):
                step()
            dve.wait_ge(tab_act, 2)
            head_dve(dve, 0, False)
            with dve.Fori(1, HEADS - 1) as h:
                head_dve(dve, h, False)
            head_dve(dve, HEADS - 1, True)
            for t in range(TT):
                dve.wait_ge(x_in_s[t], 32)
                add_tile(dve, 0, t)
                if 3 <= t < 7:
                    out_lo(dve, 1, 1, t - 3)
            with dve.Fori(0, RET_GROUPS // 2 - 1) as gg:
                out_dve(dve, 2 * gg + 1, 1)
                out_dve(dve, 2 * gg + 2, 0)
            last_group_dve(dve, RET_GROUPS - 1, 1, lambda u: mlp_up_lo(dve, 0, PC_M0) if u == 1 else None)

            def angles(step):
                if step == 0:
                    dve.wait_ge(sw_const, 16 * (SW_NH + 3))
                    dve.tensor_copy(pos_sf[:], pos_si[:]).then_inc(tab, 1)
                else:
                    dve.wait_ge(tab, 17)
                    dve.tensor_tensor((sins, coss)[step - 1][:], pos_sf[:].unsqueeze(2).to_broadcast([P, TT, 32]),
                                      freq_row[:].unsqueeze(1).to_broadcast([P, TT, 32]), ALU.mult).then_inc(tab, 1)

            table_steps = ([lambda i=i: angles(i) for i in range(3)] + table(dve, 19, sins[:], sins[:], work_s, 0.0) +
                           table(dve, 26, coss[:], coss[:], work_s, 0.25))

            def attention_ahead(u):
                for j in SW_FIRST_LO.get(u, ()):
                    sw_split_lo(dve, 0, j)
                if u in (4, 6):
                    tables(3)

            def tables(count):
                for step in table_steps[:count]:
                    step()
                del table_steps[:count]

            def last_adds():
                last_group_dve(dve, DG_SW - 1, 2, attention_ahead, TT - 1)
                lows = lambda *tiles: [low for t in tiles for low in norm_lows(dve, 2, t)]
                norm_rstd(dve, 2, 7, lows(4))
                tables(3)
                for low in lows(5):
                    low()
                tables(4)
                vlo_dve(dve, 0, 0)
                var_dve(dve, 0, 0)
                scale_dve(dve, 0, 0, table_steps + lows(6))
                for low in lows(7):
                    low()

            mlp_dve_all(dve, 0, DG_M0, PC_M0, last_adds)
            sw_steps("dve", dve)
            mlp_dve_all(dve, MLP_GROUPS, DG_M1, PC_M1,
                        lambda: [add_tile(dve, DG_M1 + MLP_LAST, t) for t in range(TT)])

        @block.gpsimd
        def _(pool):
            ready = lambda t: pool.wait_ge(x_in_s[t], 16)
            weights = lambda j: split_lo(pool, 0, 0, RET_PIECES, j, wqg_lo[:, j, :], wqg_hi[:, j, :])
            norm_pool(pool, 0, 0, ready)
            norm_pool(pool, 0, 2, ready)
            weights(0)
            weights(1)
            norm_pool(pool, 0, 4, ready)
            norm_pool(pool, 0, 6, ready)
            weights(2)
            weights(3)
            head_pool(pool, 0)
            with pool.Fori(1, HEADS) as h:
                head_pool(pool, h)
            for t in range(TT):
                norm_pool(pool, 1, t, x_final(pool, RET_GROUPS - 1))
            mlp_pool_all(pool, 0)
            pool.wait_ge(a_lo_s, 4 * MLP_GROUPS)
            for z in (kr, kT_hi, kT_lo, vp_hi, vp_lo):
                flat = z[:].rearrange({2: "p a -> p a", 3: "p a b -> p (a b)", 4: "p a b c -> p (a b c)"}[len(z.shape)])
                pool.memset(flat if z is kr else flat.bitcast(F32), 0.0).then_inc(sw_zero, 1)
            for t in range(TT):
                norm_pool(pool, 2, t, x_final(pool, DG_SW - 1))
            sw_steps("pool", pool)
            mlp_pool_all(pool, MLP_GROUPS)

        @block.tensor
        def _(pe):
            pe.wait_ge(const_in, 64)
            head_pe(pe, 0, True)
            with pe.Fori(1, HEADS) as h:
                head_pe(pe, h, False)
            pe.wait_ge(k_lo_s, NCH * HEADS)
            out_pe(pe, 0, 0, lambda t: y_transpose(pe, HEADS - 1, NCH - 1) if t == 1 else None)
            with pe.Fori(0, RET_GROUPS // 2 - 1) as gg:
                out_pe(pe, 2 * gg + 1, 1)
                out_pe(pe, 2 * gg + 2, 0)
            out_pe(pe, RET_GROUPS - 1, 1, norm_behind(pe, 1))
            mlp_pe_all(pe, 0, DG_M0, PC_M0, 1, 2)
            sw_steps("pe", pe)
            mlp_pe_all(pe, MLP_GROUPS, DG_M1, PC_M1, 3, None)


_INS = ["x", "positions", "norm_mix", "norm_mlp", "w_up", "w_down", "ret_w_in", "ret_w_out", "swa_w_in",
        "swa_q_gain", "swa_k_gain", "swa_sinks", "swa_w_out"]


def _constants():
    import numpy as np
    i = np.arange(P)
    causal = (i[:, None] <= i[None, :]).astype(np.float32)
    cur = np.where(i[None, :] <= i[:, None], 0.0, NEG)
    prev = np.where(i[None, :] > i[:, None], 0.0, NEG)
    mask = np.stack([cur, prev, cur, np.full((P, P), NEG)], axis=1).astype(np.float32)
    head = np.zeros((P, HEADS, 4), np.float32)
    for h in range(HEADS):
        log_gamma = math.log1p(-(2.0 ** (-5.0 - h)))
        head[:, h, 0] = np.exp(-log_gamma * (i + 1)) * DK ** -0.5
        head[:, h, 1] = np.exp(log_gamma * (i + 1))
        head[:, h, 2] = np.exp(2 * log_gamma * (i + 1))
        head[:, h, 3] = np.exp(log_gamma * CH)
    freq = lambda d: np.float32(THETA) ** (-np.arange(0, d, 2, dtype=np.float32) / np.float32(d))
    return {"c_ident": np.eye(P, dtype=np.float32), "c_causal": causal, "c_mask": mask, "c_head": head,
            "c_freq": freq(DK).astype(np.float32).reshape(P, 1),
            "c_freq_row": np.ascontiguousarray(np.broadcast_to(freq(SW_DH).astype(np.float32), (P, 32)))}


def kernel(**inputs):
    import numpy as np
    from concourse import bacc
    from concourse.bass_utils import run_bass_kernel_spmd

    nc = bacc.Bacc("TRN2", target_bir_lowering=False, num_devices=1)
    arrays, args = {}, []
    for name in _INS:
        arrays[f"in_{name}"] = np.ascontiguousarray(inputs[name])
    arrays.update(_constants())
    for name, a in arrays.items():
        args.append(nc.dram_tensor(name, a.shape, mybir.dt.from_np(a.dtype), kind="ExternalInput").ap())
    out = nc.dram_tensor("out", (1, S, D), F32, kind="ExternalOutput").ap()
    y_dram = nc.dram_tensor("y_dram", (HEADS * DV, S), F32, kind="Internal").ap()
    trunk(nc, *args, out, y_dram)
    r = run_bass_kernel_spmd(nc, [arrays], core_ids=[0])
    return r.results[0]["out"]
```
